# Optimizing a Trainium2 kernel written in Bass

```python
import math
import jax, jax.numpy as jnp
from jax import lax
import numpy as np

D_MODEL = 1024
BATCH = 1
SEQ = 2048
DEPTH = 1
DEC_BATCH = 8
DEC_SEQ = 4
PAST_LEN = 2048
PAGE_SIZE = 128

GLA_HEADS = 4
GLA_DK = 64
GLA_DV = 128
GLA_RANK = 16
GLA_TAU = 16.0
GLA_CHUNK = 64
SWA_HEADS = 8
SWA_KV_HEADS = 2
SWA_GROUP = SWA_HEADS // SWA_KV_HEADS
SWA_HD = 64
WINDOW = 128
D_FF = 2816
CONV_W = 3
EPS = 1e-6

GLA_K = GLA_HEADS * GLA_DK
GLA_V = GLA_HEADS * GLA_DV
SWA_Q = SWA_HEADS * SWA_HD
SWA_KV = SWA_KV_HEADS * SWA_HD
IN_SPLITS = (GLA_K, GLA_K, GLA_V, GLA_RANK, GLA_V, SWA_Q, SWA_KV, SWA_KV, D_MODEL, D_MODEL)
IN_COLS = sum(IN_SPLITS)

kernel_name = "gla_swa_sink_alibi_convffn_step"

def _split(z, sizes):
    out = []
    o = 0
    for s in sizes:
        out.append(z[..., o:o + s])
        o += s
    return out

def rmsnorm(x, w):
    xf = x.astype(jnp.float32)
    y = xf * lax.rsqrt(jnp.mean(xf * xf, axis=-1, keepdims=True) + EPS) * w.astype(jnp.float32)
    return y.astype(x.dtype)

def alibi_slopes():
    return jnp.exp2(-(8.0 / SWA_HEADS) * jnp.arange(1, SWA_HEADS + 1, dtype=jnp.float32))

def gla_recurrence(q, k, v, log_a, S0):
    B, T, H, _ = q.shape
    C = math.gcd(T, GLA_CHUNK)
    n = T // C

    def to_chunks(a):
        return a.astype(jnp.float32).reshape(B, n, C, H, a.shape[-1]).transpose(1, 0, 3, 2, 4)

    tri = jnp.tril(jnp.ones((C, C), dtype=bool))

    def step(S, inp):
        qc, kc, vc, lc = inp
        b = jnp.cumsum(lc, axis=2)
        inter = jnp.einsum('bhcd,bhdv->bhcv', qc * jnp.exp(b), S)
        diff = b[:, :, :, None, :] - b[:, :, None, :, :]
        decay = jnp.exp(jnp.where(tri[:, :, None], diff, -jnp.inf))
        att = jnp.einsum('bhid,bhjd,bhijd->bhij', qc, kc, decay)
        out = inter + jnp.einsum('bhij,bhjv->bhiv', att, vc)
        bl = b[:, :, -1:, :]
        S_new = jnp.exp(bl[:, :, 0, :])[..., None] * S + jnp.einsum('bhjd,bhjv->bhdv', kc * jnp.exp(bl - b), vc)
        return S_new, out

    S, o = lax.scan(step, S0.astype(jnp.float32), (to_chunks(q), to_chunks(k), to_chunks(v), to_chunks(log_a)))
    o = o.transpose(1, 0, 3, 2, 4).reshape(B, T, H, GLA_DV)
    return o, S

def sink_attention(q, k, v, rel, valid, sinks):
    s = jnp.einsum('...qkgd,...skd->...kgqs', q, k).astype(jnp.float32) * (SWA_HD ** -0.5)
    slopes = alibi_slopes().reshape(SWA_KV_HEADS, SWA_GROUP)[:, :, None, None]
    bias = -slopes * rel.astype(jnp.float32)
    mask = ((rel >= 0) & (rel < WINDOW)) & valid[..., None, None, None, :]
    s = jnp.where(mask, s + bias, -jnp.inf)
    sink = sinks.astype(jnp.float32).reshape(SWA_KV_HEADS, SWA_GROUP)[:, :, None, None]
    m = jnp.maximum(jnp.max(s, axis=-1, keepdims=True), sink)
    p = jnp.exp(s - m)
    denom = jnp.sum(p, axis=-1, keepdims=True) + jnp.exp(sink - m)
    return jnp.einsum('...kgqs,...skd->...qkgd', (p / denom).astype(v.dtype), v)

def token_mixers(h, S0, kbuf, vbuf, w_in, w_gate_up, b_gate, gla_norm, sinks, w_branch_a, w_branch_b, w_out):
    B, L, _ = h.shape
    z = h @ w_in
    q_a, k_a, v_a, r_a, g_a, q_b, k_b, v_b, gate_a, gate_b = _split(z, IN_SPLITS)

    log_a = jax.nn.log_sigmoid((r_a @ w_gate_up + b_gate).astype(jnp.float32)) / GLA_TAU
    q_a = q_a.reshape(B, L, GLA_HEADS, GLA_DK) * (GLA_DK ** -0.5)
    k_a = k_a.reshape(B, L, GLA_HEADS, GLA_DK)
    v_a = v_a.reshape(B, L, GLA_HEADS, GLA_DV)
    log_a = log_a.reshape(B, L, GLA_HEADS, GLA_DK)
    o_a, S_new = gla_recurrence(q_a, k_a, v_a, log_a, S0)
    o_a = rmsnorm(o_a, gla_norm).astype(h.dtype).reshape(B, L, GLA_V) * jax.nn.silu(g_a)

    q_b = q_b.reshape(B, L, SWA_KV_HEADS, SWA_GROUP, SWA_HD)
    k_b = k_b.reshape(B, L, SWA_KV_HEADS, SWA_HD)
    v_b = v_b.reshape(B, L, SWA_KV_HEADS, SWA_HD)
    if kbuf is None:
        nb = L // WINDOW
        qb = q_b.reshape(B, nb, WINDOW, SWA_KV_HEADS, SWA_GROUP, SWA_HD)

        def band(a):
            a = a.reshape(B, nb, WINDOW, SWA_KV_HEADS, SWA_HD)
            prev = jnp.concatenate([jnp.zeros_like(a[:, :1]), a[:, :-1]], axis=1)
            return jnp.concatenate([prev, a], axis=2)

        rel = jnp.arange(WINDOW)[:, None] + WINDOW - jnp.arange(2 * WINDOW)[None, :]
        valid = (jnp.arange(nb)[:, None] * WINDOW - WINDOW + jnp.arange(2 * WINDOW)[None, :]) >= 0
        o_b = sink_attention(qb, band(k_b), band(v_b), rel, valid, sinks).reshape(B, L, SWA_Q)
        keep = min(WINDOW, L)
        k_new, v_new = k_b[:, L - keep:], v_b[:, L - keep:]
    else:
        buf = kbuf.shape[1]
        k_all = jnp.concatenate([kbuf.astype(k_b.dtype), k_b], axis=1)
        v_all = jnp.concatenate([vbuf.astype(v_b.dtype), v_b], axis=1)
        rel = jnp.arange(L)[:, None] + buf - jnp.arange(buf + L)[None, :]
        valid = jnp.ones((buf + L,), dtype=bool)
        o_b = sink_attention(q_b, k_all, v_all, rel, valid, sinks).reshape(B, L, SWA_Q)
        k_new, v_new = k_all[:, L:], v_all[:, L:]

    merged = jax.nn.sigmoid(gate_a) * (o_a @ w_branch_a) + jax.nn.sigmoid(gate_b) * (o_b @ w_branch_b)
    return merged @ w_out, S_new, k_new, v_new

def conv_ffn(h, conv_buf, w_ffn_in, conv_w, conv_b, w_ffn_out):
    L = h.shape[1]
    u, g = _split(h @ w_ffn_in, (D_FF, D_FF))
    up = jnp.concatenate([conv_buf.astype(u.dtype), u], axis=1)
    c = conv_b
    for j in range(CONV_W):
        c = c + conv_w[j] * up[:, j:j + L]
    y = (jax.nn.gelu(c, approximate=True) * g) @ w_ffn_out
    return y, up[:, L:]

def layer(x, S0, kbuf, vbuf, cbuf, norm_mix_pre, norm_mix_post, w_in, w_gate_up, b_gate, gla_norm, sinks,
          w_branch_a, w_branch_b, w_out, norm_ffn_pre, norm_ffn_post, w_ffn_in, conv_w, conv_b, w_ffn_out):
    m, S, k_new, v_new = token_mixers(rmsnorm(x, norm_mix_pre), S0, kbuf, vbuf, w_in, w_gate_up, b_gate,
                                      gla_norm, sinks, w_branch_a, w_branch_b, w_out)
    x = x + rmsnorm(m, norm_mix_post)
    f, c_new = conv_ffn(rmsnorm(x, norm_ffn_pre), cbuf, w_ffn_in, conv_w, conv_b, w_ffn_out)
    x = x + rmsnorm(f, norm_ffn_post)
    return x, S, k_new, v_new, c_new

def setup_inputs(seed: int = 0) -> dict:
    key = jax.random.key(seed)
    ks = jax.random.split(key, 24)
    f32 = jnp.float32
    buf = min(WINDOW, PAST_LEN)

    def nrm(k, shape, scale):
        return jax.random.normal(k, shape, f32) * scale

    return {
        "x_prompt": nrm(ks[0], (BATCH, SEQ, D_MODEL), 1.0),
        "x_sample": nrm(ks[1], (DEC_BATCH, DEC_SEQ, D_MODEL), 1.0),
        "state_gla": nrm(ks[2], (DEPTH, DEC_BATCH, GLA_HEADS, GLA_DK, GLA_DV), 0.5),
        "cache_swa_k": nrm(ks[3], (DEPTH, DEC_BATCH, buf, SWA_KV_HEADS, SWA_HD), 1.0),
        "cache_swa_v": nrm(ks[4], (DEPTH, DEC_BATCH, buf, SWA_KV_HEADS, SWA_HD), 1.0),
        "state_ffn_conv": nrm(ks[5], (DEPTH, DEC_BATCH, CONV_W - 1, D_FF), 1.0),
        "norm_mix_pre": 1.0 + nrm(ks[6], (DEPTH, D_MODEL), 0.02),
        "norm_mix_post": 1.0 + nrm(ks[7], (DEPTH, D_MODEL), 0.02),
        "w_in": nrm(ks[8], (DEPTH, D_MODEL, IN_COLS), D_MODEL ** -0.5),
        "w_gate_up": nrm(ks[9], (DEPTH, GLA_RANK, GLA_K), GLA_RANK ** -0.5),
        "b_gate": nrm(ks[10], (DEPTH, GLA_K), 0.1),
        "gla_norm": 1.0 + nrm(ks[11], (DEPTH, GLA_DV), 0.02),
        "sinks": nrm(ks[12], (DEPTH, SWA_HEADS), 0.5),
        "w_branch_a": nrm(ks[13], (DEPTH, GLA_V, D_MODEL), GLA_V ** -0.5),
        "w_branch_b": nrm(ks[14], (DEPTH, SWA_Q, D_MODEL), SWA_Q ** -0.5),
        "w_out": nrm(ks[15], (DEPTH, D_MODEL, D_MODEL), D_MODEL ** -0.5),
        "norm_ffn_pre": 1.0 + nrm(ks[16], (DEPTH, D_MODEL), 0.02),
        "norm_ffn_post": 1.0 + nrm(ks[17], (DEPTH, D_MODEL), 0.02),
        "w_ffn_in": nrm(ks[18], (DEPTH, D_MODEL, 2 * D_FF), D_MODEL ** -0.5),
        "conv_w": nrm(ks[19], (DEPTH, CONV_W, D_FF), CONV_W ** -0.5),
        "conv_b": nrm(ks[20], (DEPTH, D_FF), 0.02),
        "w_ffn_out": nrm(ks[21], (DEPTH, D_FF, D_MODEL), D_FF ** -0.5),
    }

def reference(x_prompt, x_sample, state_gla, cache_swa_k, cache_swa_v, state_ffn_conv,
              norm_mix_pre, norm_mix_post, w_in, w_gate_up, b_gate, gla_norm, sinks,
              w_branch_a, w_branch_b, w_out, norm_ffn_pre, norm_ffn_post, w_ffn_in, conv_w, conv_b, w_ffn_out):
    yp, ys = x_prompt, x_sample
    gp, gs, kp, vp, ksm, vsm, cp, cs = [], [], [], [], [], [], [], []
    for l in range(DEPTH):
        params = (norm_mix_pre[l], norm_mix_post[l], w_in[l], w_gate_up[l], b_gate[l], gla_norm[l], sinks[l],
                  w_branch_a[l], w_branch_b[l], w_out[l], norm_ffn_pre[l], norm_ffn_post[l],
                  w_ffn_in[l], conv_w[l], conv_b[l], w_ffn_out[l])
        S0p = jnp.zeros((BATCH, GLA_HEADS, GLA_DK, GLA_DV), jnp.float32)
        c0p = jnp.zeros((BATCH, CONV_W - 1, D_FF), x_prompt.dtype)
        yp, S_p, k_p, v_p, c_p = layer(yp, S0p, None, None, c0p, *params)
        ys, S_s, k_s, v_s, c_s = layer(ys, state_gla[l], cache_swa_k[l], cache_swa_v[l], state_ffn_conv[l], *params)
        gp.append(S_p.astype(x_prompt.dtype)); gs.append(S_s.astype(state_gla.dtype))
        kp.append(k_p); vp.append(v_p)
        ksm.append(k_s.astype(cache_swa_k.dtype)); vsm.append(v_s.astype(cache_swa_v.dtype))
        cp.append(c_p); cs.append(c_s.astype(state_ffn_conv.dtype))
    gla_state_prompt = jnp.stack(gp)
    gla_state_sample = jnp.stack(gs)
    swa_k_prompt = jnp.stack(kp)
    swa_v_prompt = jnp.stack(vp)
    swa_k_sample = jnp.stack(ksm)
    swa_v_sample = jnp.stack(vsm)
    conv_prompt = jnp.stack(cp)
    conv_sample = jnp.stack(cs)
    return (yp, ys, gla_state_prompt, gla_state_sample, swa_k_prompt, swa_v_prompt,
            swa_k_sample, swa_v_sample, conv_prompt, conv_sample)


_drawn_inputs = setup_inputs


def setup_inputs(seed=0):
    import zlib

    import numpy as np

    out = dict(_drawn_inputs(seed))
    spreads = {}
    factors = {'norm_mix_post': 3.485,
     'gla_norm': 3.576,
     'sinks': 5.828,
     'norm_ffn_pre': 2.83,
     'norm_ffn_post': 4.977,
     'conv_b': 4.88}
    for name, (base, spread) in spreads.items():
        noise = np.random.default_rng([zlib.crc32(name.encode()), seed]).standard_normal(out[name].shape)
        drawn = base * np.exp(spread * noise) if base else spread * noise
        out[name] = __import__('jax').numpy.asarray(drawn.astype(out[name].dtype))
    for name, factor in factors.items():
        out[name] = (out[name] * factor).astype(out[name].dtype)
    return out
```

```python
import math
from contextlib import ExitStack

import numpy as np

import concourse.bass as bass
from concourse import mybir

ALU = mybir.AluOpType
ACT = mybir.ActivationFunctionType
AX = mybir.AxisListType
F32 = mybir.dt.float32
F32R = mybir.dt.float32r
I32 = mybir.dt.int32

P = 128
D = 1024
SEQ = 2048
NSEQ, SLEN = 8, 4
NS = NSEQ * SLEN
T = SEQ + NS
NB = 5
TB = T // NB
KD = D // P
FF = 2816
KF = FF // P
H, DK, DV, RANK = 4, 64, 128, 16
CH = 64
WIN = 128
NWIN = SEQ // WIN
QH, KVH, HD = 8, 2, 64
EPS = 1e-6
TAU = 16.0
NEG = -1.0e30

Z_QA, Z_KA, Z_VA, Z_GA, Z_R, Z_QB, Z_KB, Z_VB, Z_GATE_A, Z_GATE_B = 0, 2, 4, 8, 12, 13, 17, 18, 19, 27
N_MIX = 19
N_Z = 35

STEP_SIGNALS = """
    abs_exp abs_ready att_full att_ready b_ready centred ei_ready ek_ready eo_ready eq_ready gate_den gate_exp kd_ready
    kd_ready_turned kd_turned kt_ready lm_ready log_a_ready log_ms logits_full o_full o_normed o_squared ow0_full pt0_full
    pt0_read_a pt0_read_b qez_ready qz_ready rstd_ready shifted sigmoid_ready silu_ready softplus_ready sums_full tail_ready
    u_full v_ready v_turned m0_ready exp0_ready sink0_ready sinkexp0_ready s0_ready max0_ready den0_ready inv0_ready p0_ready
    scores0_full
""".split()


class Signal:

    def __init__(self, nc, ctx, name):
        self.sem = ctx.enter_context(nc.semaphore(name))
        self.base = 0

    def count(self, n):
        return None if isinstance(n, int) and n <= 0 else n + self.base

    def passed(self, n):
        self.base += n


def each_pair(engine, n, body):
    for i in range(min(n, 2)):
        body(i, 0, i)
    if n // 2 > 1:
        with engine.Fori(1, n // 2) as t:
            body(t * 2, t, 0)
            body(t * 2 + 1, t, 1)
    if n % 2 and n > 2:
        body(n - 1, n // 2, 0)


def each(engine, n, body):
    body(0)
    if n > 1:
        with engine.Fori(1, n) as i:
            body(i)


def one(i):
    return slice(i, i + 1) if isinstance(i, int) else bass.ds(i, 1)


def span(i, size):
    return slice(i * size, i * size + size) if isinstance(i, int) else bass.ds(i * size, size)


class Program:
    def __init__(self, nc, ctx, dram):
        self.nc, self.ctx, self.dram = nc, ctx, dram
        self.signals = {}
        self.bank = [ctx.enter_context(nc.psum_tensor(f"bank{i}", [P, 512], F32)) for i in range(8)]

    def __getitem__(self, name):
        if name not in self.signals:
            self.signals[name] = Signal(self.nc, self.ctx, name)
        return self.signals[name]

    def split_matmul(self, out, w_hi, w_lo, x_hi, x_lo, first, last):
        pe = self.nc.tensor
        pe.matmul(out, w_hi, x_hi, start=first, stop=False)
        pe.matmul(out, w_lo, x_hi, start=False, stop=False)
        return pe.matmul(out, w_hi, x_lo, start=False, stop=last)


def norm_blocks(pg, sb, block, src, norm_w, h_hi, h_lo, tag):
    nc = pg.nc
    x = [sb(f"x{i}_{tag}", [P, KD, TB], F32) for i in range(2)]
    h = sb(f"h_{tag}", [P, KD, TB], F32)
    rstd = sb(f"rstd_{tag}", [P, TB], F32)
    w = sb(f"normw_{tag}", [P, KD], F32)
    ones = sb(f"ones_{tag}", [P, P], F32)
    eps = sb(f"eps_{tag}", [P, 1], F32)
    sums = pg.bank[7]
    x_in = [pg["x_in_even"], pg["x_in_odd"]]
    const_in, const_set = pg["const_in"], pg["const_set"]
    squared, summed, rooted, inverted = pg["squared"], pg["summed"], pg["rooted"], pg["inverted"]
    h_full, h_hi_ready, h_lo_ready = pg["h_full"], pg["h_hi_ready"], pg["h_lo_ready"]
    xT = src.rearrange("(k p) t -> p k t", p=P)

    def sync_consts(sp):
        sp.dma_start(w[:], norm_w).then_inc(const_in.sem, 16)

    def sync(sp, b):
        if (due := h_full.count(b - 1)) is not None:
            sp.wait_ge(h_full.sem, due)
        sp.dma_start(x[b % 2][:], xT[:, :, b * TB:(b + 1) * TB]).then_inc(x_in[b % 2].sem, 16)

    def scalar(act, b):
        act.wait_ge(x_in[b % 2].sem, x_in[b % 2].count(16 * (b // 2 + 1)))
        if (due := h_lo_ready.count(b)) is not None:
            act.wait_ge(h_lo_ready.sem, due)
        nc.scalar.activation(h[:], x[b % 2][:], ACT.Square).then_inc(squared.sem, 1)
        act.wait_ge(summed.sem, summed.count(b + 1))
        if (due := inverted.count(b)) is not None:
            act.wait_ge(inverted.sem, due)
        if (due := h_full.count(b)) is not None:
            act.wait_ge(h_full.sem, due)
        act.wait_ge(const_set.sem, const_set.count(2))
        nc.scalar.activation(rstd[:], sums[:, :TB], ACT.Sqrt, bias=eps[:], scale=1.0 / D).then_inc(rooted.sem, 1)
        act.wait_ge(h_full.sem, h_full.count(b + 1))
        nc.scalar.activation(h_hi[:, :, b * TB:(b + 1) * TB], h[:], ACT.Copy).then_inc(h_hi_ready.sem, 1)

    def vector(dve):
        nc.vector.memset(ones[:], 1.0).then_inc(const_set.sem, 1)
        nc.vector.memset(eps[:], EPS).then_inc(const_set.sem, 1)
        dve.wait_ge(const_in.sem, const_in.count(16))
        for b in range(NB):
            dve.wait_ge(rooted.sem, rooted.count(b + 1))
            nc.vector.reciprocal(rstd[:], rstd[:]).then_inc(inverted.sem, 1)
            dve.wait_ge(inverted.sem, inverted.count(b + 1))
            dve.wait_ge(x_in[b % 2].sem, x_in[b % 2].count(16 * (b // 2 + 1)))
            for k in range(KD):
                last = nc.vector.scalar_tensor_tensor(h[:, k], x[b % 2][:, k], w[:, k:k + 1], rstd[:], ALU.mult, ALU.mult)
            last.then_inc(h_full.sem, 1)
            dve.wait_ge(h_hi_ready.sem, h_hi_ready.count(b + 1))
            dve.wait_ge(h_full.sem, h_full.count(b + 1))
            nc.vector.tensor_tensor(h_lo[:, :, b * TB:(b + 1) * TB], h[:], h_hi[:, :, b * TB:(b + 1) * TB].bitcast(F32),
                                    ALU.subtract).then_inc(h_lo_ready.sem, 1)

    def tensor(pe):
        for b in range(NB):
            pe.wait_ge(squared.sem, squared.count(b + 1))
            pe.wait_ge(const_set.sem, const_set.count(1))
            if (due := rooted.count(b)) is not None:
                pe.wait_ge(rooted.sem, due)
            for k in range(KD):
                last = nc.tensor.matmul(sums[:, :TB], ones[:], h[:, k], start=(k == 0), stop=(k == KD - 1))
            last.then_inc(summed.sem, 1)

    def done():
        x_in[0].passed(16 * 3)
        x_in[1].passed(16 * 2)
        const_in.passed(16)
        const_set.passed(2)
        for s in (squared, summed, rooted, inverted, h_full, h_hi_ready, h_lo_ready):
            s.passed(NB)

    return sync_consts, sync, scalar, vector, tensor, done, x


class WeightStream:

    def __init__(self, pg, sb, src, nk, tag):
        self.pg, self.nc, self.src, self.nk = pg, pg.nc, src, nk
        self.raw = [sb(f"w_raw{i}_{tag}", [P, nk, P], F32) for i in range(2)]
        self.hi = [sb(f"w_hi{i}_{tag}", [P, nk, P], F32R) for i in range(2)]
        self.lo = [sb(f"w_lo{i}_{tag}", [P, nk, P], F32R) for i in range(2)]
        self.w_in = [pg["w_in_even"], pg["w_in_odd"]]
        self.hi_ready, self.lo_ready, self.psum_full = pg["w_hi_ready"], pg["w_lo_ready"], pg["psum_full"]

    def load(self, sp, n, pair, slot, at=None):
        if (due := self.lo_ready.count(n - 1)) is not None:
            sp.wait_ge(self.lo_ready.sem, due)
        sp.dma_start(self.raw[slot][:], self.src[one(n if at is None else at)].rearrange("o p k c -> p (o k) c")
                     ).then_inc(self.w_in[slot].sem, 16)

    def split_hi(self, act, n, pair, slot, fulls=NB):
        act.wait_ge(self.w_in[slot].sem, self.w_in[slot].count((pair + 1) * 16))
        if (due := self.psum_full.count((n - 1) * fulls)) is not None:
            act.wait_ge(self.psum_full.sem, due)
        self.nc.scalar.activation(self.hi[slot][:], self.raw[slot][:], ACT.Copy).then_inc(self.hi_ready.sem, 1)

    def split_lo(self, dve, n, pair, slot):
        dve.wait_ge(self.hi_ready.sem, self.hi_ready.count(n + 1))
        self.nc.vector.tensor_tensor(self.lo[slot][:], self.raw[slot][:], self.hi[slot][:].bitcast(F32),
                                     ALU.subtract).then_inc(self.lo_ready.sem, 1)

    def passed(self, n):
        self.w_in[0].passed((n + 1) // 2 * 16)
        self.w_in[1].passed(n // 2 * 16)
        self.hi_ready.passed(n)
        self.lo_ready.passed(n)


def project_block(pg, ws, h_hi, h_lo, bank, n, slot, b):
    for k in range(KD):
        last = pg.split_matmul(bank[:, :TB], ws.hi[slot][:, k], ws.lo[slot][:, k],
                               h_hi[:, k, b * TB:(b + 1) * TB], h_lo[:, k, b * TB:(b + 1) * TB],
                               k == 0, k == KD - 1)
    last.then_inc(ws.psum_full.sem, 1)


def mixer_phases(pg):
    nc, dram = pg.nc, pg.dram
    with ExitStack() as keep:
        def sb_keep(name, shape, dt):
            return keep.enter_context(nc.sbuf_tensor(f"{name}_sb", shape, dt))
        h_hi = sb_keep("h_hi", [P, KD, T], F32R)
        h_lo = sb_keep("h_lo", [P, KD, T], F32R)
        stage = [sb_keep(f"z_stage{i}", [P, TB], F32) for i in range(2)]
        ws = WeightStream(pg, sb_keep, dram["w_in"], KD, "in")
        z = dram["z"]
        psum_full, psum_read = pg["psum_full"], pg["psum_read"]
        stored = [pg["z_stored_even"], pg["z_stored_odd"]]

        def store_index(pair, slot, b):
            return pair * 5 + (slot * NB + b) // 2

        def evacuate(act, n, pair, slot, b, bank, tile0):
            s = (slot + b) % 2
            act.wait_ge(psum_full.sem, psum_full.count(n * NB + (b + 1)))
            if (due := stored[s].count(store_index(pair, slot, b) * 16)) is not None:
                act.wait_ge(stored[s].sem, due)
            nc.scalar.activation(stage[s][:], bank[:, :TB], ACT.Copy).then_inc(psum_read.sem, 1)

        def store(sp, n, pair, slot, b, tile0):
            s = (slot + b) % 2
            sp.wait_ge(psum_read.sem, psum_read.count(n * NB + (b + 1)))
            sp.dma_start(z[one(n + tile0), :, b * TB:(b + 1) * TB].rearrange("o p t -> (o p) t"), stage[s][:]
                         ).then_inc(stored[s].sem, 16)

        def stores_passed(n):
            stored[0].passed((n * NB + 1) // 2 * 16)
            stored[1].passed(n * NB // 2 * 16)
            psum_full.passed(n * NB)
            psum_read.passed(n * NB)
            ws.passed(n)

        with ExitStack() as own, nc.Block() as block:
            def sb(name, shape, dt):
                return own.enter_context(nc.sbuf_tensor(f"{name}_sb", shape, dt))
            consts, norm_sync, norm_scalar, norm_vector, norm_tensor, norm_done, _ = norm_blocks(
                pg, sb, block, dram["xT"], dram["norm_mix_pre"], h_hi, h_lo, "pre")

            @block.sync
            def _(sp):
                consts(sp)
                norm_sync(sp, 0)
                norm_sync(sp, 1)
                ws.load(sp, 0, 0, 0)
                ws.load(sp, 1, 0, 1)
                for b in range(2, NB):
                    norm_sync(sp, b)

                def body(n, pair, slot):
                    for b in range(NB):
                        store(sp, n, pair, slot, b, 0)
                    if not isinstance(n, int) or n + 2 < N_MIX:
                        ws.load(sp, n + 2, pair + 1, slot)
                each_pair_ahead(sp, N_MIX, body)

            @block.scalar
            def _(act):
                norm_scalar(act, 0)
                ws.split_hi(act, 0, 0, 0)
                ws.split_hi(act, 1, 0, 1)
                for b in range(1, NB):
                    norm_scalar(act, b)

                def body(n, pair, slot):
                    for b in range(NB):
                        evacuate(act, n, pair, slot, b, pg.bank[b], 0)
                    if not isinstance(n, int) or n + 2 < N_MIX:
                        ws.split_hi(act, n + 2, pair + 1, slot)
                each_pair_ahead(act, N_MIX, body)

            @block.vector
            def _(dve):
                norm_vector(dve)
                each_pair(dve, N_MIX, lambda n, pair, slot: ws.split_lo(dve, n, pair, slot))

            @block.tensor
            def _(pe):
                norm_tensor(pe)

                def body(n, pair, slot):
                    pe.wait_ge(ws.hi_ready.sem, ws.hi_ready.count(n + 1))
                    pe.wait_ge(ws.lo_ready.sem, ws.lo_ready.count(n + 1))
                    for b in range(NB):
                        if isinstance(n, int) and n == 0:
                            pe.wait_ge(pg["h_lo_ready"].sem, pg["h_lo_ready"].count(b + 1))
                            pe.wait_ge(pg["h_hi_ready"].sem, pg["h_hi_ready"].count(b + 1))
                        if (due := psum_read.count((n - 1) * NB + (b + 1))) is not None:
                            pe.wait_ge(psum_read.sem, due)
                        project_block(pg, ws, h_hi, h_lo, pg.bank[b], n, slot, b)
                each_pair(pe, N_MIX, body)

            norm_done()
            stores_passed(N_MIX)
        attention_phase(pg, ws, h_hi, h_lo, evacuate, store, stores_passed)


def each_pair_ahead(engine, n, body):
    for i in range(2):
        body(i, 0, i)
    pairs = (n - 2) // 2
    with engine.Fori(1, pairs) as t:
        body(t * 2, t, 0)
        body(t * 2 + 1, t, 1)
    for i in range(pairs * 2, n):
        body(i, i // 2, i % 2)


def slope(head):
    return 2.0 ** (-8.0 / QH * (head + 1))


def attention_phase(pg, ws, h_hi, h_lo, evacuate, store, stores_passed):
    nc, dram = pg.nc, pg.dram
    z, o_all = dram["z"], dram["o"]
    HALF = DK
    S = pg
    with ExitStack() as own, nc.Block() as block:
        def sb(name, shape, dt=F32):
            return own.enter_context(nc.sbuf_tensor(f"{name}_sb", shape, dt))
        gla = sb("gla_z", [P, 13, P])
        swa = sb("swa_z", [P, 6, P])
        ident, ones = sb("ident", [P, P]), sb("ones_dv", [P, P])
        rel = sb("rel", [P, 2 * WIN])
        w_up, b_up, g_norm = sb("w_up", [P, 2, P]), sb("b_up", [P, 2]), sb("g_norm", [P, 1])
        minus_sink = sb("minus_sink", [P, 4, 2])
        keep, causal = sb("keep", [P, 2 * P]), sb("causal", [P, P])
        eps, key_scale = sb("eps_dv", [P, 1]), sb("key_scale", [P, P])
        a1, a2, a3, a4 = (sb(f"decay{i}", [P, 2 * P]) for i in range(4))
        e1, e2 = sb("exp_centred", [P, 2 * P]), sb("exp_start", [P, 2 * P])
        qz, qez = sb("q_centred", [P, 2, 2, P]), sb("q_start", [P, 2, 2, P])
        kt, kdz = sb("k_centred", [P, 2, P]), sb("k_end_turned", [P, 2, 2, P])
        v_tok, att = sb("v_tokens", [P, 4, P]), sb("att", [P, 4, P])
        state = [sb(f"state{i}", [P, 2, P]) for i in range(2)]
        rstd = sb("rstd_dv", [P, 4, P])
        kz, v_win = sb("k_window", [P, 2, 2 * WIN]), sb("v_window", [P, 2, P])
        p = sb("probs", [P, 4, 2 * WIN])
        p_t = sb("probs_turned", [P, 2, 4, P])
        o_win = sb("o_window", [P, 4, P])
        m, row, den, sink_e = (sb(x, [P, 2, 4]) for x in ("minus_max", "row_sum", "denominator", "sink_exp"))
        b_gemm, b_s, b_att, b_o, b_m, b_w = pg.bank[0:2], pg.bank[2:4], pg.bank[4], pg.bank[5], pg.bank[6], pg.bank[7]
        att_v, gate_v = gla[:, 4:8], att

        def chunks(ap):
            return ap.rearrange("p (c t) -> p c t", t=CH)

        loads = [(ident, dram["ident"]), (w_up, dram["w_gate_up"].rearrange("r (t c) -> r t c", t=2)),
                 (b_up, dram["b_gate"]), (g_norm, dram["gla_norm"]),
                 (minus_sink, dram["sinks"]), (keep, dram["scan_keep"]), (causal, dram["causal"]), (rel, dram["rel_first"])]

        @block.sync
        def _(sp):
            for tile, src in loads:
                sp.dma_start(tile[:], src).then_inc(S["att_const_in"].sem, 16)

            def body(i, pair, slot):
                if (due := S["oa_stored"].count(i * 16)) is not None:
                    sp.wait_ge(S["oa_stored"].sem, due)
                if (due := S["gla_out_ready"].count(i)) is not None:
                    sp.wait_ge(S["gla_out_ready"].sem, due)
                sp.dma_start(gla[:], z[0:13, :, span(i, P)].rearrange("t p c -> p t c")).then_inc(S["gla_in"].sem, 16)
                if (due := S["scores1_full"].count(i)) is not None:
                    sp.wait_ge(S["scores1_full"].sem, due)
                if (due := S["vb_turned"].count(i)) is not None:
                    sp.wait_ge(S["vb_turned"].sem, due)
                if (due := S["kz_ready"].count(i)) is not None:
                    sp.wait_ge(S["kz_ready"].sem, due)
                sp.dma_start(swa[:], z[13:19, :, span(i, P)].rearrange("t p c -> p t c")).then_inc(S["swa_in"].sem, 16)
                if isinstance(i, int) and i == 1:
                    sp.wait_ge(S["s1_ready"].sem, S["s1_ready"].count(1))
                    sp.dma_start(rel[:], dram["rel"]).then_inc(S["att_const_in"].sem, 16)
                for b in range(NB):
                    store(sp, i, pair, slot, b, N_MIX)
                if not isinstance(i, int) or i + 2 < NWIN:
                    ws.load(sp, i + 2, pair + 1, slot, i + 2 + N_MIX)
                sp.wait_ge(S["gla_out_ready"].sem, S["gla_out_ready"].count(i + 1))
                sp.dma_start(o_all[0:4, :, span(i, P)].rearrange("t p c -> p t c"), att_v).then_inc(S["oa_stored"].sem, 16)
                sp.wait_ge(S["ow1_read"].sem, S["ow1_read"].count(i + 1))
                sp.dma_start(o_all[4:8, :, span(i, P)].rearrange("t p c -> p t c"), o_win[:]).then_inc(S["ob_stored"].sem, 16)
            ws.load(sp, 0, 0, 0, N_MIX)
            ws.load(sp, 1, 0, 1, N_MIX + 1)
            each_pair_ahead(sp, NWIN, body)
            sp.wait_ge(S["state_end"].sem, S["state_end"].count(NWIN))
            sp.dma_start(dram["gla_state_prompt"].rearrange("(t h) d v -> (h d) t v", t=2), state[0][:]
                         ).then_inc(S["state_stored"].sem, 16)
            sp.wait_ge(S["state_stored"].sem, S["state_stored"].count(16))
            sp.wait_ge(S["oa_stored"].sem, S["oa_stored"].count(NWIN * 16))
            sp.wait_ge(S["ob_stored"].sem, S["ob_stored"].count(NWIN * 16))

        @block.gpsimd
        def _(pool):
            for zeroed in (kz, v_win, qz, qez, kdz, att, state[0]):
                nc.gpsimd.memset(zeroed[:], 0.0).then_inc(S["zeroed"].sem, 1)
            nc.gpsimd.memset(ones[:], 1.0).then_inc(S["zeroed"].sem, 1)
            nc.gpsimd.memset(eps[:], EPS).then_inc(S["zeroed"].sem, 1)
            nc.gpsimd.memset(key_scale[:], HD ** -0.5).then_inc(S["zeroed"].sem, 1)
            pool.wait_ge(S["zeroed"].sem, S["zeroed"].count(10))

            def body(i):
                pool.wait_ge(S["zeroed"].sem, S["zeroed"].count(9))
                if (due := S["scores1_full"].count(i)) is not None:
                    pool.wait_ge(S["scores1_full"].sem, due)
                if (due := S["kz_ready"].count(i)) is not None:
                    pool.wait_ge(S["kz_ready"].sem, due)
                nc.gpsimd.tensor_copy(kz[:, :, 0:WIN], kz[:, :, WIN:2 * WIN]).then_inc(S["kz_shifted"].sem, 1)
                pool.wait_ge(S["zeroed"].sem, S["zeroed"].count(9))
                if (due := S["ow1_full"].count(i)) is not None:
                    pool.wait_ge(S["ow1_full"].sem, due)
                if (due := S["vb_ready"].count(i)) is not None:
                    pool.wait_ge(S["vb_ready"].sem, due)
                nc.gpsimd.tensor_copy(v_win[:, 0], v_win[:, 1]).then_inc(S["vb_shifted"].sem, 1)
                pool.wait_ge(S["kz_shifted"].sem, S["kz_shifted"].count(i + 1))
                pool.wait_ge(S["swa_in"].sem, S["swa_in"].count((i + 1) * 16))
                nc.gpsimd.tensor_tensor(kz[0:HALF, 0, WIN:], swa[0:HALF, 4], key_scale[0:HALF], ALU.mult
                                        ).then_inc(S["kz_low_half"].sem, 1)
                pool.wait_ge(S["vb_shifted"].sem, S["vb_shifted"].count(i + 1))
                pool.wait_ge(S["kz_low_half"].sem, S["kz_low_half"].count(i + 1))
                nc.gpsimd.tensor_tensor(kz[HALF:, 1, WIN:], swa[HALF:, 4], key_scale[HALF:], ALU.mult
                                        ).then_inc(S["kz_ready"].sem, 1)
                pool.wait_ge(S["ek_ready"].sem, S["ek_ready"].count(i + 1))
                pool.wait_ge(S["gla_in"].sem, S["gla_in"].count((i + 1) * 16))
                if (due := S["o_full"].count(i)) is not None:
                    pool.wait_ge(S["o_full"].sem, due)
                pool.wait_ge(S["kz_ready"].sem, S["kz_ready"].count(i + 1))
                nc.gpsimd.tensor_tensor(kt[:], gla[:, 2:4], a4[:].rearrange("p (t c) -> p t c", t=2), ALU.mult
                                        ).then_inc(S["kt_ready"].sem, 1)
                pool.wait_ge(S["eo_ready"].sem, S["eo_ready"].count(i + 1))
                pool.wait_ge(S["kt_ready"].sem, S["kt_ready"].count(i + 1))
                nc.gpsimd.tensor_tensor(gla[:, 2:4], gla[:, 2:4], a1[:].rearrange("p (t c) -> p t c", t=2), ALU.mult
                                        ).then_inc(S["kd_ready"].sem, 1)
                pool.wait_ge(S["sigmoid_ready"].sem, S["sigmoid_ready"].count(i + 1))
                nc.gpsimd.tensor_tensor(gate_v[:], gla[:, 8:12], gate_v[:], ALU.mult).then_inc(S["silu_ready"].sem, 1)
            each(pool, NWIN, body)

        @block.scalar
        def _(act):
            copy = lambda out, in_, **kw: nc.scalar.activation(out, in_, ACT.Copy, **kw)

            def softmax(half, i):
                act.wait_ge(S[f"m{half}_ready"].sem, S[f"m{half}_ready"].count(i + 1))
                for j in range(4):
                    last = nc.scalar.activation(p[:, j], p[:, j], ACT.Exp, bias=m[:, half, j:j + 1],
                                                accum_out=row[:, half, j:j + 1])
                last.then_inc(S[f"exp{half}_ready"].sem, 1)
                act.wait_ge(S[f"sink{half}_ready"].sem, S[f"sink{half}_ready"].count(i + 1))
                nc.scalar.activation(sink_e[:, half], sink_e[:, half], ACT.Exp).then_inc(S[f"sinkexp{half}_ready"].sem, 1)

            def body(i, pair, slot):
                act.wait_ge(S["v_turned"].sem, S["v_turned"].count(i + 1))
                if (due := S["o_full"].count(i)) is not None:
                    act.wait_ge(S["o_full"].sem, due)
                copy(v_tok[:].rearrange("p h c -> p (h c)"), b_m[:]).then_inc(S["v_ready"].sem, 1)
                act.wait_ge(S["vb_turned"].sem, S["vb_turned"].count(i + 1))
                act.wait_ge(S["vb_shifted"].sem, S["vb_shifted"].count(i + 1))
                copy(v_win[:, 1], b_w[:, 0:P]).then_inc(S["vb_ready"].sem, 1)
                softmax(0, i)
                evacuate(act, i, pair, slot, 0, b_gemm[slot], N_MIX)
                act.wait_ge(S["logits_full"].sem, S["logits_full"].count(i + 1))
                if (due := S["kd_ready"].count(i)) is not None:
                    act.wait_ge(S["kd_ready"].sem, due)
                for t in range(2):
                    last = nc.scalar.activation(a1[:, t * P:(t + 1) * P], b_m[:, t * P:(t + 1) * P], ACT.Abs, bias=b_up[:, t:t + 1])
                last.then_inc(S["abs_ready"].sem, 1)
                act.wait_ge(S["abs_ready"].sem, S["abs_ready"].count(i + 1))
                nc.scalar.activation(a1[:], a1[:], ACT.Exp, scale=-1.0).then_inc(S["abs_exp"].sem, 1)
                act.wait_ge(S["abs_exp"].sem, S["abs_exp"].count(i + 1))
                nc.scalar.activation(a1[:], a1[:], ACT.Ln, bias=1.0).then_inc(S["softplus_ready"].sem, 1)
                act.wait_ge(S["centred"].sem, S["centred"].count(i + 1))
                if (due := S["qz_ready"].count(i)) is not None:
                    act.wait_ge(S["qz_ready"].sem, due)
                nc.scalar.activation(e1[:], a4[:], ACT.Exp, scale=1.0 / TAU).then_inc(S["eq_ready"].sem, 1)
                act.wait_ge(S["eq_ready"].sem, S["eq_ready"].count(i + 1))
                nc.scalar.activation(a4[:], a4[:], ACT.Exp, scale=-1.0 / TAU).then_inc(S["ek_ready"].sem, 1)
                act.wait_ge(S["tail_ready"].sem, S["tail_ready"].count(i + 1))
                nc.scalar.activation(a1[:], a1[:], ACT.Exp, scale=1.0 / TAU).then_inc(S["eo_ready"].sem, 1)
                if (due := S["state_end"].count(i)) is not None:
                    act.wait_ge(S["state_end"].sem, due)
                nc.scalar.activation(e2[:], a3[:], ACT.Exp, scale=1.0 / TAU).then_inc(S["ei_ready"].sem, 1)
                evacuate(act, i, pair, slot, 1, b_gemm[1 - slot], N_MIX)
                act.wait_ge(S["kd_turned"].sem, S["kd_turned"].count(i + 1))
                if (due := S["u_full"].count(i)) is not None:
                    act.wait_ge(S["u_full"].sem, due)
                for c in range(2):
                    last = copy(kdz[c * HALF:(c + 1) * HALF, c].rearrange("p t c -> p (t c)"), b_m[c * HALF:(c + 1) * HALF, 2 * P:])
                last.then_inc(S["kd_ready_turned"].sem, 1)
                evacuate(act, i, pair, slot, 2, b_gemm[slot], N_MIX)
                act.wait_ge(S["pt0_full"].sem, S["pt0_full"].count(i + 1))
                if (due := S["ow1_full"].count(i)) is not None:
                    act.wait_ge(S["ow1_full"].sem, due)
                copy(p_t[:, 0].rearrange("p h c -> p (h c)"), b_s[0][:]).then_inc(S["pt0_read_a"].sem, 1)
                evacuate(act, i, pair, slot, 3, b_gemm[1 - slot], N_MIX)
                act.wait_ge(S["ow0_full"].sem, S["ow0_full"].count(i + 1))
                if (due := S["ob_stored"].count(i * 16)) is not None:
                    act.wait_ge(S["ob_stored"].sem, due)
                copy(o_win[:, 0:2].rearrange("p h c -> p (h c)"), b_w[:, 2 * P:]).then_inc(S["ow0_read"].sem, 1)
                softmax(1, i)
                act.wait_ge(S["o_full"].sem, S["o_full"].count(i + 1))
                if (due := S["gla_out_ready"].count(i)) is not None:
                    act.wait_ge(S["gla_out_ready"].sem, due)
                nc.scalar.activation(rstd[:].rearrange("p h c -> p (h c)"), b_o[:], ACT.Square).then_inc(S["o_squared"].sem, 1)
                nc.scalar.activation(gate_v[:], gla[:, 8:12], ACT.Exp, scale=-1.0).then_inc(S["gate_exp"].sem, 1)
                evacuate(act, i, pair, slot, 4, b_gemm[slot], N_MIX)
                act.wait_ge(S["sums_full"].sem, S["sums_full"].count(i + 1))
                flat = rstd[:].rearrange("p h c -> p (h c)")
                nc.scalar.activation(flat, b_att[:], ACT.Ln, scale=1.0 / DV, bias=eps[:]).then_inc(S["log_ms"].sem, 1)
                act.wait_ge(S["log_ms"].sem, S["log_ms"].count(i + 1))
                nc.scalar.activation(flat, flat, ACT.Exp, scale=-0.5).then_inc(S["rstd_ready"].sem, 1)
                act.wait_ge(S["pt1_full"].sem, S["pt1_full"].count(i + 1))
                act.wait_ge(S["ow0_full"].sem, S["ow0_full"].count(i + 1))
                copy(p_t[:, 0].rearrange("p h c -> p (h c)"), b_s[0][:]).then_inc(S["pt1_read_a"].sem, 1)
                act.wait_ge(S["ow1_full"].sem, S["ow1_full"].count(i + 1))
                copy(o_win[:, 2:4].rearrange("p h c -> p (h c)"), b_w[:, 2 * P:]).then_inc(S["ow1_read"].sem, 1)
                if not isinstance(i, int) or i + 2 < NWIN:
                    ws.split_hi(act, i + 2, pair + 1, slot)
            act.wait_ge(S["att_const_in"].sem, S["att_const_in"].count(16 * len(loads)))
            act.wait_ge(S["zeroed"].sem, S["zeroed"].count(9))
            ws.split_hi(act, 0, 0, 0)
            ws.split_hi(act, 1, 0, 1)
            each_pair_ahead(act, NWIN, body)

        @block.vector
        def _(dve):
            v = nc.vector

            def logits(half, i):
                dve.wait_ge(S[f"scores{half}_full"].sem, S[f"scores{half}_full"].count(i + 1))
                if (due := S["pt1_full" if half == 0 else "pt0_full"].count(i if half == 0 else i + 1)) is not None:
                    dve.wait_ge(S["pt1_full" if half == 0 else "pt0_full"].sem, due)
                for t in range(2):
                    for kv in range(2):
                        last = v.scalar_tensor_tensor(p[:, 2 * t + kv], rel[:], slope(kv * 4 + 2 * half + t),
                                                      b_s[t][:, kv * 256:(kv + 1) * 256], ALU.mult, ALU.add)
                last.then_inc(S[f"s{half}_ready"].sem, 1)
                dve.wait_ge(S[f"s{half}_ready"].sem, S[f"s{half}_ready"].count(i + 1))
                v.tensor_reduce(m[:, half], p[:], AX.X, ALU.max, negate=True).then_inc(S[f"max{half}_ready"].sem, 1)
                dve.wait_ge(S[f"max{half}_ready"].sem, S[f"max{half}_ready"].count(i + 1))
                sink = minus_sink[:, 2 * half:2 * half + 2].rearrange("p t k -> p (t k)")
                v.tensor_tensor(m[:, half], m[:, half], sink, ALU.min).then_inc(S[f"m{half}_ready"].sem, 1)
                dve.wait_ge(S[f"m{half}_ready"].sem, S[f"m{half}_ready"].count(i + 1))
                v.tensor_tensor(sink_e[:, half], m[:, half], sink, ALU.subtract).then_inc(S[f"sink{half}_ready"].sem, 1)

            def normalise(half, i):
                dve.wait_ge(S[f"exp{half}_ready"].sem, S[f"exp{half}_ready"].count(i + 1))
                dve.wait_ge(S[f"sinkexp{half}_ready"].sem, S[f"sinkexp{half}_ready"].count(i + 1))
                v.tensor_tensor(den[:, half], row[:, half], sink_e[:, half], ALU.add).then_inc(S[f"den{half}_ready"].sem, 1)
                dve.wait_ge(S[f"den{half}_ready"].sem, S[f"den{half}_ready"].count(i + 1))
                v.reciprocal(den[:, half], den[:, half]).then_inc(S[f"inv{half}_ready"].sem, 1)
                dve.wait_ge(S[f"inv{half}_ready"].sem, S[f"inv{half}_ready"].count(i + 1))
                for j in range(4):
                    last = v.tensor_scalar(p[:, j], p[:, j], den[:, half, j:j + 1], None, ALU.mult)
                last.then_inc(S[f"p{half}_ready"].sem, 1)

            def body(i, pair, slot):
                if isinstance(i, int) and i == 1:
                    dve.wait_ge(S["att_const_in"].sem, S["att_const_in"].count(16 * (len(loads) + 1)))
                logits(0, i)
                dve.wait_ge(S["abs_ready"].sem, S["abs_ready"].count(i + 1))
                for t in range(2):
                    last = v.tensor_scalar(a2[:, t * P:(t + 1) * P], b_m[:, t * P:(t + 1) * P], b_up[:, t:t + 1], 0.0, ALU.add, ALU.min)
                last.then_inc(S["lm_ready"].sem, 1)
                dve.wait_ge(S["softplus_ready"].sem, S["softplus_ready"].count(i + 1))
                dve.wait_ge(S["lm_ready"].sem, S["lm_ready"].count(i + 1))
                v.tensor_tensor(a2[:], a2[:], a1[:], ALU.subtract).then_inc(S["log_a_ready"].sem, 1)
                dve.wait_ge(S["log_a_ready"].sem, S["log_a_ready"].count(i + 1))
                if (due := S["ei_ready"].count(i)) is not None:
                    dve.wait_ge(S["ei_ready"].sem, due)
                v.tensor_tensor_scan(a3[:], keep[:], a2[:], 0.0, ALU.mult, ALU.add).then_inc(S["b_ready"].sem, 1)
                dve.wait_ge(S["b_ready"].sem, S["b_ready"].count(i + 1))
                if (due := S["kt_ready"].count(i)) is not None:
                    dve.wait_ge(S["kt_ready"].sem, due)
                b = chunks(a3[:])
                v.tensor_tensor(chunks(a4[:]), b, b[:, :, CH // 2 - 1:CH // 2].to_broadcast([P, 4, CH]), ALU.subtract
                                ).then_inc(S["shifted"].sem, 1)
                v.tensor_tensor(chunks(a1[:]), b[:, :, CH - 1:CH].to_broadcast([P, 4, CH]), b, ALU.subtract
                                ).then_inc(S["tail_ready"].sem, 1)
                dve.wait_ge(S["shifted"].sem, S["shifted"].count(i + 1))
                v.tensor_scalar(a4[:], a4[:], 80.0 * TAU, -80.0 * TAU, ALU.min, ALU.max).then_inc(S["centred"].sem, 1)
                dve.wait_ge(S["eq_ready"].sem, S["eq_ready"].count(i + 1))
                dve.wait_ge(S["gla_in"].sem, S["gla_in"].count((i + 1) * 16))
                if (due := S["att_full"].count(i)) is not None:
                    dve.wait_ge(S["att_full"].sem, due)
                for t, e in ((0, e1),):
                    for hh in range(2):
                        rows = slice(hh * HALF, (hh + 1) * HALF)
                        last = v.scalar_tensor_tensor(qz[rows, :, hh], gla[rows, 0:2], DK ** -0.5,
                                                      e[rows].rearrange("p (t c) -> p t c", t=2), ALU.mult, ALU.mult)
                last.then_inc(S["qz_ready"].sem, 1)
                dve.wait_ge(S["ei_ready"].sem, S["ei_ready"].count(i + 1))
                if (due := S["o_full"].count(i)) is not None:
                    dve.wait_ge(S["o_full"].sem, due)
                for hh in range(2):
                    rows = slice(hh * HALF, (hh + 1) * HALF)
                    last = v.scalar_tensor_tensor(qez[rows, :, hh], gla[rows, 0:2], DK ** -0.5,
                                                  e2[rows].rearrange("p (t c) -> p t c", t=2), ALU.mult, ALU.mult)
                last.then_inc(S["qez_ready"].sem, 1)
                normalise(0, i)
                dve.wait_ge(S["att_const_in"].sem, S["att_const_in"].count(16 * len(loads)))
                dve.wait_ge(S["att_full"].sem, S["att_full"].count(i + 1))
                if (due := S["gla_out_ready"].count(i)) is not None:
                    dve.wait_ge(S["gla_out_ready"].sem, due)
                dve.wait_ge(S["att_cleared"].sem, S["att_cleared"].count(i + 1))
                for hh in range(4):
                    last = v.copy_predicated(att[:, hh], causal[:].bitcast(I32), b_att[:, hh * P:(hh + 1) * P])
                last.then_inc(S["att_ready"].sem, 1)
                dve.wait_ge(S["u_full"].sem, S["u_full"].count(i + 1))
                for c in range(2):
                    if c == 0:
                        if (due := S["o_full"].count(i)) is not None:
                            dve.wait_ge(S["o_full"].sem, due)
                    else:
                        dve.wait_ge(S["inter0_done"].sem, S["inter0_done"].count(i + 1))
                        dve.wait_ge(S["state_mid"].sem, S["state_mid"].count(i + 1))
                    for t in range(2):
                        at = t * P + c * CH + CH - 1
                        last = v.scalar_tensor_tensor(state[1 - c][:, t], state[c][:, t], e2[:, at:at + 1],
                                                      b_m[:, (2 * c + t) * P:(2 * c + t + 1) * P], ALU.mult, ALU.add)
                    last.then_inc(S["state_end" if c else "state_mid"].sem, 1)
                dve.wait_ge(S["pt0_full"].sem, S["pt0_full"].count(i + 1))
                if (due := S["ow1_full"].count(i)) is not None:
                    dve.wait_ge(S["ow1_full"].sem, due)
                v.tensor_copy(p_t[:, 1].rearrange("p h c -> p (h c)"), b_s[1][:]).then_inc(S["pt0_read_b"].sem, 1)
                logits(1, i)
                dve.wait_ge(S["gate_exp"].sem, S["gate_exp"].count(i + 1))
                v.tensor_scalar(gate_v[:], gate_v[:], 1.0, None, ALU.add).then_inc(S["gate_den"].sem, 1)
                dve.wait_ge(S["gate_den"].sem, S["gate_den"].count(i + 1))
                v.reciprocal(gate_v[:], gate_v[:]).then_inc(S["sigmoid_ready"].sem, 1)
                normalise(1, i)
                dve.wait_ge(S["rstd_ready"].sem, S["rstd_ready"].count(i + 1))
                v.scalar_tensor_tensor(att_v.rearrange("p h c -> p (h c)"), b_o[:], g_norm[:, 0:1],
                                       rstd[:].rearrange("p h c -> p (h c)"), ALU.mult, ALU.mult).then_inc(S["o_normed"].sem, 1)
                dve.wait_ge(S["silu_ready"].sem, S["silu_ready"].count(i + 1))
                dve.wait_ge(S["o_normed"].sem, S["o_normed"].count(i + 1))
                v.tensor_tensor(att_v, att_v, gate_v[:], ALU.mult).then_inc(S["gla_out_ready"].sem, 1)
                dve.wait_ge(S["gla_out_ready"].sem, S["gla_out_ready"].count(i + 1))
                v.memset(att[:], 0.0).then_inc(S["att_cleared"].sem, 1)
                dve.wait_ge(S["pt1_full"].sem, S["pt1_full"].count(i + 1))
                dve.wait_ge(S["ow0_full"].sem, S["ow0_full"].count(i + 1))
                v.tensor_copy(p_t[:, 1].rearrange("p h c -> p (h c)"), b_s[1][:]).then_inc(S["pt1_read_b"].sem, 1)
                if not isinstance(i, int) or i + 2 < NWIN:
                    ws.split_lo(dve, i + 2, pair + 1, slot)
            dve.wait_ge(S["att_const_in"].sem, S["att_const_in"].count(16 * len(loads)))
            dve.wait_ge(S["zeroed"].sem, S["zeroed"].count(9))
            v.memset(att[:], 0.0).then_inc(S["att_cleared"].sem, 1)
            v.tensor_scalar(minus_sink[:], minus_sink[:], -1.0, None, ALU.mult).then_inc(S["sink_negated"].sem, 1)
            dve.wait_ge(S["sink_negated"].sem, S["sink_negated"].count(1))
            ws.split_lo(dve, 0, 0, 0)
            ws.split_lo(dve, 1, 0, 1)
            each_pair_ahead(dve, NWIN, body)

        @block.tensor
        def _(pe):
            mm = nc.tensor.matmul

            def gemm(i, pair, slot, b):
                if b == 0:
                    pe.wait_ge(ws.hi_ready.sem, ws.hi_ready.count(i + 1))
                    pe.wait_ge(ws.lo_ready.sem, ws.lo_ready.count(i + 1))
                if (due := S["psum_read"].count(i * NB + (b - 1))) is not None:
                    pe.wait_ge(S["psum_read"].sem, due)
                project_block(pg, ws, h_hi, h_lo, b_gemm[(slot + b) % 2], i, slot, b)

            def scores(half, i):
                for t in range(2):
                    last = mm(b_s[t][:], swa[:, 2 * half + t], kz[:].rearrange("p k c -> p (k c)"), start=True, stop=True)
                last.then_inc(S[f"scores{half}_full"].sem, 1)

            def turn_p(half, i):
                pe.wait_ge(S[f"p{half}_ready"].sem, S[f"p{half}_ready"].count(i + 1))
                for pc in range(2):
                    for j in range(4):
                        last = nc.tensor.transpose(b_s[pc][:, j * P:(j + 1) * P], p[:, j, pc * WIN:(pc + 1) * WIN], ident[:])
                last.then_inc(S[f"pt{half}_full"].sem, 1)

            def window_out(half, i):
                pe.wait_ge(S[f"pt{half}_read_a"].sem, S[f"pt{half}_read_a"].count(i + 1))
                pe.wait_ge(S[f"pt{half}_read_b"].sem, S[f"pt{half}_read_b"].count(i + 1))
                for t in range(2):
                    for kv in range(2):
                        rows = slice(kv * HALF, (kv + 1) * HALF)
                        for pc in range(2):
                            last = mm(b_w[rows, (2 + t) * P:(3 + t) * P], v_win[:, pc, rows], p_t[:, pc, 2 * t + kv],
                                      start=(pc == 0), stop=(pc == 1))
                last.then_inc(S[f"ow{half}_full"].sem, 1)

            def body(i, pair, slot):
                pe.wait_ge(S["gla_in"].sem, S["gla_in"].count((i + 1) * 16))
                if (due := S["state_end"].count(i)) is not None:
                    pe.wait_ge(S["state_end"].sem, due)
                for hh in range(4):
                    last = nc.tensor.transpose(b_m[:, hh * P:(hh + 1) * P], gla[:, 4 + hh], ident[:])
                last.then_inc(S["v_turned"].sem, 1)
                pe.wait_ge(S["swa_in"].sem, S["swa_in"].count((i + 1) * 16))
                if (due := S["ow1_read"].count(i)) is not None:
                    pe.wait_ge(S["ow1_read"].sem, due)
                nc.tensor.transpose(b_w[:, 0:P], swa[:, 5], ident[:]).then_inc(S["vb_turned"].sem, 1)
                pe.wait_ge(S["kz_ready"].sem, S["kz_ready"].count(i + 1))
                if (due := S["pt1_read_a"].count(i)) is not None:
                    pe.wait_ge(S["pt1_read_a"].sem, due)
                if (due := S["pt1_read_b"].count(i)) is not None:
                    pe.wait_ge(S["pt1_read_b"].sem, due)
                scores(0, i)
                pe.wait_ge(S["v_ready"].sem, S["v_ready"].count(i + 1))
                for t in range(2):
                    last = mm(b_m[:, t * P:(t + 1) * P], w_up[:, t], gla[:, 12], start=True, stop=True)
                last.then_inc(S["logits_full"].sem, 1)
                gemm(i, pair, slot, 0)
                gemm(i, pair, slot, 1)
                pe.wait_ge(S["kt_ready"].sem, S["kt_ready"].count(i + 1))
                pe.wait_ge(S["qz_ready"].sem, S["qz_ready"].count(i + 1))
                if (due := S["rstd_ready"].count(i)) is not None:
                    pe.wait_ge(S["rstd_ready"].sem, due)
                for t in range(2):
                    last = mm(b_att[:, t * 2 * P:(t + 1) * 2 * P], kt[:, t], qz[:, t].rearrange("p h c -> p (h c)"), start=True, stop=True)
                last.then_inc(S["att_full"].sem, 1)
                pe.wait_ge(S["kd_ready"].sem, S["kd_ready"].count(i + 1))
                pe.wait_ge(S["abs_ready"].sem, S["abs_ready"].count(i + 1))
                pe.wait_ge(S["lm_ready"].sem, S["lm_ready"].count(i + 1))
                for t in range(2):
                    last = nc.tensor.transpose(b_m[:, (2 + t) * P:(3 + t) * P], gla[:, 2 + t], ident[:])
                last.then_inc(S["kd_turned"].sem, 1)
                gemm(i, pair, slot, 2)
                turn_p(0, i)
                pe.wait_ge(S["kd_ready_turned"].sem, S["kd_ready_turned"].count(i + 1))
                for c in range(2):
                    for t in range(2):
                        for hh in range(2):
                            rows = slice(hh * HALF, (hh + 1) * HALF)
                            last = mm(b_m[rows, (2 * c + t) * P:(2 * c + t + 1) * P], kdz[:, c, t, rows], v_tok[:, 2 * t + hh],
                                      start=True, stop=True)
                last.then_inc(S["u_full"].sem, 1)
                pe.wait_ge(S["att_ready"].sem, S["att_ready"].count(i + 1))
                if (due := S["gla_out_ready"].count(i)) is not None:
                    pe.wait_ge(S["gla_out_ready"].sem, due)
                for hh in range(4):
                    mm(b_o[:, hh * P:(hh + 1) * P], v_tok[:, hh], att[:, hh], start=(hh == 0), stop=False, skip_group_check=True)
                pe.wait_ge(S["qez_ready"].sem, S["qez_ready"].count(i + 1))
                for c in range(2):
                    if c == 1:
                        gemm(i, pair, slot, 3)
                        window_out(0, i)
                        scores(1, i)
                    if (due := S["state_mid" if c else "state_end"].count(i + c)) is not None:
                        pe.wait_ge(S["state_mid" if c else "state_end"].sem, due)
                    for t in range(2):
                        out = b_o[:].rearrange("p (t h c) -> p t h c", t=2, h=2)[:, t, :, c * CH:(c + 1) * CH]
                        last = mm(out, state[c][:, t], qez[:, t, :, c * CH:(c + 1) * CH],
                                  start=False, stop=(c == 1 and t == 1), skip_group_check=True)
                    last.then_inc(S["o_full" if c else "inter0_done"].sem, 1)
                gemm(i, pair, slot, 4)
                pe.wait_ge(S["o_squared"].sem, S["o_squared"].count(i + 1))
                mm(b_att[:], ones[:], rstd[:].rearrange("p h c -> p (h c)"), start=True, stop=True).then_inc(S["sums_full"].sem, 1)
                turn_p(1, i)
                pe.wait_ge(S["ow0_read"].sem, S["ow0_read"].count(i + 1))
                window_out(1, i)
            pe.wait_ge(S["att_const_in"].sem, S["att_const_in"].count(16 * len(loads)))
            pe.wait_ge(S["zeroed"].sem, S["zeroed"].count(9))
            each_pair_ahead(pe, NWIN, body)

        stores_passed(NWIN)
        for name in STEP_SIGNALS:
            S[name].passed(NWIN)
        S["sink_negated"].passed(1)


def sample_phase(pg):
    nc, dram = pg.nc, pg.dram
    z, o_all = dram["z"], dram["o"]
    S = pg
    HALF = DK
    L2 = 2 * NS
    with ExitStack() as own, nc.Block() as block:
        def sb(name, shape, dt=F32):
            return own.enter_context(nc.sbuf_tensor(f"{name}_smp", shape, dt))
        gla, swa = sb("gla", [P, 13, NS]), sb("swa", [P, 6, NS])
        ident, ones, eps = sb("ident", [P, P]), sb("ones", [P, P]), sb("eps", [P, 1])
        w_up, b_up, g_norm = sb("w_up", [P, 2, P]), sb("b_up", [P, 2]), sb("g_norm", [P, 1])
        keep, causal, own_rows = sb("keep", [P, L2]), sb("causal", [NS, NS]), sb("own_rows", [NS, NSEQ])
        bias, minus_sink = sb("bias", [P, 2, WIN + NS]), sb("minus_sink", [P, 1])
        state_in, state_out = sb("state_in", [P, 2, NSEQ, P]), sb("state_out", [P, 2, NSEQ, P])
        k_cache, v_cache = sb("k_cache", [P, NSEQ, WIN]), sb("v_cache", [P, NSEQ, P])
        a1, a2, a3, a4, e1, e2 = (sb(f"decay{i}", [P, L2]) for i in range(6))
        qz, qez = sb("q_centred", [P, 2, 2, NS]), sb("q_start", [P, 2, 2, NS])
        kt, kd, kdz = sb("k_centred", [P, 2, NS]), sb("k_end", [P, 2, NS]), sb("k_end_turned", [P, NSEQ, 2, P])
        v_tok, att, kv_tok = sb("v_tokens", [P, 4, P]), sb("att", [P, 4, NS]), sb("kv_tokens", [P, 2, P])
        sq, gate, o_out = sb("o_squared", [P, 4, NS]), sb("gate", [P, 4, NS]), sb("o_out", [P, 4, NS])
        qw, p = sb("q_window", [P, NSEQ, 2, 4, SLEN]), sb("probs", [P, 2, WIN + NS])
        pt_cache, pt_new = sb("probs_cache_turned", [P, 2, P]), sb("probs_new_turned", [P, 2, P])
        m, row, den, sink_e = (sb(x, [P, 2]) for x in ("minus_max", "row_sum", "denominator", "sink_exp"))
        o_win = sb("o_window", [P, 4, NSEQ, SLEN])
        bank = pg.bank
        zeroed = (qz, qez, kdz, v_tok, att, kv_tok, qw, pt_new)

        def chunks(ap):
            return ap.rearrange("p (c t) -> p c t", t=SLEN)

        def pair(ap):
            return ap.rearrange("p (t c) -> p t c", t=2)

        tokens = slice(SEQ, T)
        loads = [(gla[:], z[0:13, :, tokens].rearrange("t p c -> p t c")),
                 (swa[:], z[13:19, :, tokens].rearrange("t p c -> p t c")),
                 (ident[:], dram["ident"]), (w_up[:], dram["w_gate_up"].rearrange("r (t c) -> r t c", t=2)),
                 (b_up[:], dram["b_gate"]), (g_norm[:], dram["gla_norm"]), (keep[:], dram["sample_keep"]),
                 (causal[:], dram["sample_causal"]), (own_rows[:], dram["sample_rows"]), (bias[:], dram["sample_bias"]),
                 (minus_sink[:], dram["sample_sinks"]), (k_cache[:], dram["k_cacheT"]),
                 (v_cache[:], dram["v_cache"].rearrange("s k c -> k s c"))]
        loads += [(state_in[:, t], dram["state_gla"][:, 2 * t:2 * t + 2].rearrange("s h d v -> (h d) s v")) for t in range(2)]

        @block.sync
        def _(sp):
            for tile, src in loads:
                sp.dma_start(tile, src).then_inc(S["smp_in"].sem, 16)
            out = [(dram["swa_k_sample"][:, 0:WIN - SLEN], dram["k_cache"][:, SLEN:]),
                   (dram["swa_v_sample"][:, 0:WIN - SLEN], dram["v_cache"][:, SLEN:]),
                   (dram["swa_k_promptT"], z[Z_KB, :, SEQ - WIN:SEQ]), (dram["swa_v_promptT"], z[Z_VB, :, SEQ - WIN:SEQ])]
            for dst, src in out:
                sp.dma_start(dst, src).then_inc(S["smp_out"].sem, 16)
            sp.wait_ge(S["kv_tok_ready"].sem, S["kv_tok_ready"].count(1))
            for i, name in enumerate(("swa_k_sample", "swa_v_sample")):
                for s in range(NSEQ):
                    sp.dma_start(dram[name][s, WIN - SLEN:], kv_tok[s * SLEN:(s + 1) * SLEN, i]).then_inc(S["smp_out"].sem, 16)
            sp.wait_ge(S["state_out_ready"].sem, S["state_out_ready"].count(1))
            for t in range(2):
                sp.dma_start(dram["gla_state_sample"][:, 2 * t:2 * t + 2].rearrange("s h d v -> (h d) s v"), state_out[:, t]
                             ).then_inc(S["smp_out"].sem, 16)
            sp.wait_ge(S["o_win_ready"].sem, S["o_win_ready"].count(1))
            sp.dma_start(o_all[4:8, :, tokens].rearrange("t p c -> p t c"), o_win[:].rearrange("p t s c -> p t (s c)")
                         ).then_inc(S["smp_out"].sem, 16)
            sp.wait_ge(S["o_out_ready"].sem, S["o_out_ready"].count(1))
            sp.dma_start(o_all[0:4, :, tokens].rearrange("t p c -> p t c"), o_out[:]).then_inc(S["smp_out"].sem, 16)
            sp.wait_ge(S["smp_out"].sem, S["smp_out"].count(16 * (len(out) + 2 * NSEQ + 4)))

        @block.gpsimd
        def _(pool):
            for tile in zeroed:
                nc.gpsimd.memset(tile[:], 0.0).then_inc(S["smp_set"].sem, 1)
            nc.gpsimd.memset(ones[:], 1.0).then_inc(S["smp_set"].sem, 1)
            nc.gpsimd.memset(eps[:], EPS).then_inc(S["smp_set"].sem, 1)

        @block.scalar
        def _(act):
            copy = lambda out, in_: nc.scalar.activation(out, in_, ACT.Copy)
            act.wait_ge(S["smp_in"].sem, S["smp_in"].count(16 * len(loads)))
            act.wait_ge(S["smp_set"].sem, S["smp_set"].count(len(zeroed) + 2))
            act.wait_ge(S["logits_full"].sem, S["logits_full"].count(1))
            for t in range(2):
                last = nc.scalar.activation(a1[:, t * NS:(t + 1) * NS], bank[5][:, t * NS:(t + 1) * NS], ACT.Abs, bias=b_up[:, t:t + 1])
            last.then_inc(S["abs_ready"].sem, 1)
            act.wait_ge(S["abs_ready"].sem, S["abs_ready"].count(1))
            nc.scalar.activation(a1[:], a1[:], ACT.Exp, scale=-1.0).then_inc(S["abs_exp"].sem, 1)
            act.wait_ge(S["abs_exp"].sem, S["abs_exp"].count(1))
            nc.scalar.activation(a1[:], a1[:], ACT.Ln, bias=1.0).then_inc(S["softplus_ready"].sem, 1)
            act.wait_ge(S["v_turned"].sem, S["v_turned"].count(1))
            copy(v_tok[0:NS].rearrange("p h c -> p (h c)"), bank[6][0:NS]).then_inc(S["v_ready"].sem, 1)
            copy(kv_tok[0:NS].rearrange("p h c -> p (h c)"), bank[7][0:NS, 0:2 * P]).then_inc(S["kv_tok_ready"].sem, 1)
            act.wait_ge(S["centred"].sem, S["centred"].count(1))
            act.wait_ge(S["tail_ready"].sem, S["tail_ready"].count(1))
            nc.scalar.activation(e1[:], a4[:], ACT.Exp, scale=1.0 / TAU).then_inc(S["eq_ready"].sem, 1)
            act.wait_ge(S["eq_ready"].sem, S["eq_ready"].count(1))
            nc.scalar.activation(a4[:], a4[:], ACT.Exp, scale=-1.0 / TAU).then_inc(S["ek_ready"].sem, 1)
            nc.scalar.activation(a1[:], a1[:], ACT.Exp, scale=1.0 / TAU).then_inc(S["eo_ready"].sem, 1)
            nc.scalar.activation(e2[:], a3[:], ACT.Exp, scale=1.0 / TAU).then_inc(S["ei_ready"].sem, 1)
            act.wait_ge(S["m0_ready"].sem, S["m0_ready"].count(1))
            for g in range(2):
                last = nc.scalar.activation(p[:, g], p[:, g], ACT.Exp, bias=m[:, g:g + 1], accum_out=row[:, g:g + 1])
            last.then_inc(S["exp0_ready"].sem, 1)
            act.wait_ge(S["sink0_ready"].sem, S["sink0_ready"].count(1))
            nc.scalar.activation(sink_e[:], sink_e[:], ACT.Exp).then_inc(S["sinkexp0_ready"].sem, 1)
            act.wait_ge(S["o_full"].sem, S["o_full"].count(1))
            flat = sq[:].rearrange("p h c -> p (h c)")
            nc.scalar.activation(flat, bank[5][:, 0:4 * NS], ACT.Square).then_inc(S["o_squared"].sem, 1)
            nc.scalar.activation(gate[:], gla[:, 8:12], ACT.Exp, scale=-1.0).then_inc(S["gate_exp"].sem, 1)
            act.wait_ge(S["sums_full"].sem, S["sums_full"].count(1))
            nc.scalar.activation(flat, bank[4][:, 0:4 * NS], ACT.Ln, scale=1.0 / DV, bias=eps[:]).then_inc(S["log_ms"].sem, 1)
            act.wait_ge(S["log_ms"].sem, S["log_ms"].count(1))
            nc.scalar.activation(flat, flat, ACT.Exp, scale=-0.5).then_inc(S["rstd_ready"].sem, 1)
            act.wait_ge(S["ow0_full"].sem, S["ow0_full"].count(1))
            for kv in range(2):
                rows = slice(kv * HALF, (kv + 1) * HALF)
                for t in range(4):
                    src = bank[7][rows, 256:512].rearrange("p (s k t c) -> p k t s c", s=NSEQ, k=2, t=4)[:, kv, t]
                    last = copy(o_win[rows, t], src)
            last.then_inc(S["o_win_ready"].sem, 1)

        @block.vector
        def _(dve):
            v = nc.vector
            dve.wait_ge(S["smp_in"].sem, S["smp_in"].count(16 * len(loads)))
            dve.wait_ge(S["smp_set"].sem, S["smp_set"].count(len(zeroed) + 2))
            v.tensor_scalar(minus_sink[:], minus_sink[:], -1.0, None, ALU.mult).then_inc(S["sink_negated"].sem, 1)
            for kv in range(2):
                rows = slice(kv * HALF, (kv + 1) * HALF)
                for t in range(4):
                    last = v.tensor_scalar(qw[rows, :, kv, t], swa[rows, t].rearrange("p (s c) -> p s c", c=SLEN), HD ** -0.5, None, ALU.mult)
            last.then_inc(S["qw_ready"].sem, 1)
            dve.wait_ge(S["abs_ready"].sem, S["abs_ready"].count(1))
            for t in range(2):
                last = v.tensor_scalar(a2[:, t * NS:(t + 1) * NS], bank[5][:, t * NS:(t + 1) * NS], b_up[:, t:t + 1], 0.0, ALU.add, ALU.min)
            last.then_inc(S["lm_ready"].sem, 1)
            dve.wait_ge(S["softplus_ready"].sem, S["softplus_ready"].count(1))
            dve.wait_ge(S["lm_ready"].sem, S["lm_ready"].count(1))
            v.tensor_tensor(a2[:], a2[:], a1[:], ALU.subtract).then_inc(S["log_a_ready"].sem, 1)
            dve.wait_ge(S["log_a_ready"].sem, S["log_a_ready"].count(1))
            v.tensor_tensor_scan(a3[:], keep[:], a2[:], 0.0, ALU.mult, ALU.add).then_inc(S["b_ready"].sem, 1)
            dve.wait_ge(S["b_ready"].sem, S["b_ready"].count(1))
            b = chunks(a3[:])
            n = L2 // SLEN
            v.tensor_tensor(chunks(a4[:]), b, b[:, :, SLEN // 2 - 1:SLEN // 2].to_broadcast([P, n, SLEN]), ALU.subtract).then_inc(S["shifted"].sem, 1)
            v.tensor_tensor(chunks(a1[:]), b[:, :, SLEN - 1:].to_broadcast([P, n, SLEN]), b, ALU.subtract).then_inc(S["tail_ready"].sem, 1)
            dve.wait_ge(S["shifted"].sem, S["shifted"].count(1))
            v.tensor_scalar(a4[:], a4[:], 80.0 * TAU, -80.0 * TAU, ALU.min, ALU.max).then_inc(S["centred"].sem, 1)
            dve.wait_ge(S["ei_ready"].sem, S["ei_ready"].count(1))
            v.tensor_tensor(kt[:], gla[:, 2:4], pair(a4[:]), ALU.mult).then_inc(S["kt_ready"].sem, 1)
            v.tensor_tensor(kd[:], gla[:, 2:4], pair(a1[:]), ALU.mult).then_inc(S["kd_ready"].sem, 1)
            for out, e, name in ((qz, e1, "qz_ready"), (qez, e2, "qez_ready")):
                for hh in range(2):
                    rows = slice(hh * HALF, (hh + 1) * HALF)
                    last = v.scalar_tensor_tensor(out[rows, :, hh], gla[rows, 0:2], DK ** -0.5, pair(e[rows]), ALU.mult, ALU.mult)
                last.then_inc(S[name].sem, 1)
            dve.wait_ge(S["scores0_full"].sem, S["scores0_full"].count(1))
            for g in range(2):
                last = v.tensor_tensor(p[:, g], bank[g][:, 0:WIN + NS], bias[:, g], ALU.add)
            last.then_inc(S["s0_ready"].sem, 1)
            dve.wait_ge(S["s0_ready"].sem, S["s0_ready"].count(1))
            v.tensor_reduce(m[:], p[:], AX.X, ALU.max, negate=True).then_inc(S["max0_ready"].sem, 1)
            dve.wait_ge(S["max0_ready"].sem, S["max0_ready"].count(1))
            dve.wait_ge(S["sink_negated"].sem, S["sink_negated"].count(1))
            v.tensor_scalar(m[:], m[:], minus_sink[:, 0:1], None, ALU.min).then_inc(S["m0_ready"].sem, 1)
            dve.wait_ge(S["m0_ready"].sem, S["m0_ready"].count(1))
            v.tensor_scalar(sink_e[:], m[:], minus_sink[:, 0:1], None, ALU.subtract).then_inc(S["sink0_ready"].sem, 1)
            dve.wait_ge(S["att_full"].sem, S["att_full"].count(1))
            for hh in range(4):
                last = v.copy_predicated(att[0:NS, hh], causal[:].bitcast(I32), bank[4][0:NS, hh * NS:(hh + 1) * NS])
            last.then_inc(S["att_ready"].sem, 1)
            dve.wait_ge(S["kd_turned"].sem, S["kd_turned"].count(1))
            for s in range(NSEQ):
                last = v.tensor_scalar(kdz[0:NS, s].rearrange("p t c -> p (t c)"), bank[6][0:NS, 0:2 * P], own_rows[:, s:s + 1], None, ALU.mult)
            last.then_inc(S["kd_ready_turned"].sem, 1)
            dve.wait_ge(S["exp0_ready"].sem, S["exp0_ready"].count(1))
            dve.wait_ge(S["sinkexp0_ready"].sem, S["sinkexp0_ready"].count(1))
            v.tensor_tensor(den[:], row[:], sink_e[:], ALU.add).then_inc(S["den0_ready"].sem, 1)
            dve.wait_ge(S["den0_ready"].sem, S["den0_ready"].count(1))
            v.reciprocal(den[:], den[:]).then_inc(S["inv0_ready"].sem, 1)
            dve.wait_ge(S["inv0_ready"].sem, S["inv0_ready"].count(1))
            for g in range(2):
                last = v.tensor_scalar(p[:, g], p[:, g], den[:, g:g + 1], None, ALU.mult)
            last.then_inc(S["p0_ready"].sem, 1)
            dve.wait_ge(S["pt0_full"].sem, S["pt0_full"].count(1))
            v.tensor_copy(pt_cache[:].rearrange("p g c -> p (g c)"), bank[7][:, 0:2 * P]).then_inc(S["pt0_read_a"].sem, 1)
            v.tensor_copy(pt_new[0:NS].rearrange("p g c -> p (g c)"), bank[7][0:NS, 2 * P:]).then_inc(S["pt0_read_b"].sem, 1)
            dve.wait_ge(S["u_full"].sem, S["u_full"].count(1))
            for s in range(NSEQ):
                for t in range(2):
                    at = t * NS + s * SLEN + SLEN - 1
                    last = v.scalar_tensor_tensor(state_out[:, t, s], state_in[:, t, s], e2[:, at:at + 1],
                                                  bank[s // 2][:, (s % 2) * 2 * P + t * P:(s % 2) * 2 * P + (t + 1) * P], ALU.mult, ALU.add)
            last.then_inc(S["state_out_ready"].sem, 1)
            dve.wait_ge(S["gate_exp"].sem, S["gate_exp"].count(1))
            v.tensor_scalar(gate[:], gate[:], 1.0, None, ALU.add).then_inc(S["gate_den"].sem, 1)
            dve.wait_ge(S["gate_den"].sem, S["gate_den"].count(1))
            v.reciprocal(gate[:], gate[:]).then_inc(S["sigmoid_ready"].sem, 1)
            dve.wait_ge(S["sigmoid_ready"].sem, S["sigmoid_ready"].count(1))
            v.tensor_tensor(gate[:], gate[:], gla[:, 8:12], ALU.mult).then_inc(S["silu_ready"].sem, 1)
            dve.wait_ge(S["rstd_ready"].sem, S["rstd_ready"].count(1))
            v.scalar_tensor_tensor(o_out[:].rearrange("p h c -> p (h c)"), bank[5][:, 0:4 * NS], g_norm[:, 0:1],
                                   sq[:].rearrange("p h c -> p (h c)"), ALU.mult, ALU.mult).then_inc(S["o_normed"].sem, 1)
            dve.wait_ge(S["o_normed"].sem, S["o_normed"].count(1))
            dve.wait_ge(S["silu_ready"].sem, S["silu_ready"].count(1))
            v.tensor_tensor(o_out[:], o_out[:], gate[:], ALU.mult).then_inc(S["o_out_ready"].sem, 1)

        @block.tensor
        def _(pe):
            mm = nc.tensor.matmul
            pe.wait_ge(S["smp_in"].sem, S["smp_in"].count(16 * len(loads)))
            pe.wait_ge(S["smp_set"].sem, S["smp_set"].count(len(zeroed) + 2))
            for t in range(2):
                last = mm(bank[5][:, t * NS:(t + 1) * NS], w_up[:, t], gla[:, 12], start=True, stop=True)
            last.then_inc(S["logits_full"].sem, 1)
            for hh in range(4):
                nc.tensor.transpose(bank[6][0:NS, hh * P:(hh + 1) * P], gla[:, 4 + hh], ident[:])
            for i in range(2):
                last = nc.tensor.transpose(bank[7][0:NS, i * P:(i + 1) * P], swa[:, 4 + i], ident[:])
            last.then_inc(S["v_turned"].sem, 1)
            pe.wait_ge(S["qw_ready"].sem, S["qw_ready"].count(1))
            for s in range(NSEQ):
                q = qw[:, s].rearrange("p k t c -> p (k t c)")
                rows = slice(32 * (s % 4), 32 * (s % 4) + 32)
                mm(bank[s // 4][rows, 0:WIN], q, k_cache[:, s], start=True, stop=True, tile_position=(0, 32 * (s % 4)))
                last = mm(bank[s // 4][rows, WIN:WIN + NS], q, swa[:, 4], start=True, stop=True, tile_position=(0, 32 * (s % 4)))
            last.then_inc(S["scores0_full"].sem, 1)
            pe.wait_ge(S["qez_ready"].sem, S["qez_ready"].count(1))
            for t in range(2):
                last = mm(bank[4][0:NS, t * 2 * NS:(t + 1) * 2 * NS], kt[:, t], qz[:, t].rearrange("p h c -> p (h c)"), start=True, stop=True)
            last.then_inc(S["att_full"].sem, 1)
            pe.wait_ge(S["v_ready"].sem, S["v_ready"].count(1))
            for t in range(2):
                last = nc.tensor.transpose(bank[6][0:NS, t * P:(t + 1) * P], kd[:, t], ident[:])
            last.then_inc(S["kd_turned"].sem, 1)
            pe.wait_ge(S["att_ready"].sem, S["att_ready"].count(1))
            pe.wait_ge(S["lm_ready"].sem, S["lm_ready"].count(1))
            for hh in range(4):
                mm(bank[5][:, hh * NS:(hh + 1) * NS], v_tok[:, hh], att[:, hh], start=(hh == 0), stop=False, skip_group_check=True)
            out = bank[5][:, 0:4 * NS].rearrange("p (t h c) -> p t h c", t=2, h=2)
            for s in range(NSEQ):
                for t in range(2):
                    cols = slice(s * SLEN, (s + 1) * SLEN)
                    last = mm(out[:, t, :, cols], state_in[:, t, s], qez[:, t, :, cols], start=False,
                              stop=(s == NSEQ - 1 and t == 1), skip_group_check=True)
            last.then_inc(S["o_full"].sem, 1)
            pe.wait_ge(S["kd_ready_turned"].sem, S["kd_ready_turned"].count(1))
            pe.wait_ge(S["s0_ready"].sem, S["s0_ready"].count(1))
            for s in range(NSEQ):
                for t in range(2):
                    for hh in range(2):
                        rows = slice(hh * HALF, (hh + 1) * HALF)
                        at = (s % 2) * 2 * P + t * P
                        last = mm(bank[s // 2][rows, at:at + P], kdz[:, s, t, rows], v_tok[:, 2 * t + hh], start=True, stop=True)
            last.then_inc(S["u_full"].sem, 1)
            pe.wait_ge(S["o_squared"].sem, S["o_squared"].count(1))
            mm(bank[4][:, 0:4 * NS], ones[:], sq[:].rearrange("p h c -> p (h c)"), start=True, stop=True).then_inc(S["sums_full"].sem, 1)
            pe.wait_ge(S["p0_ready"].sem, S["p0_ready"].count(1))
            pe.wait_ge(S["kv_tok_ready"].sem, S["kv_tok_ready"].count(1))
            for g in range(2):
                nc.tensor.transpose(bank[7][:, g * P:(g + 1) * P], p[:, g, 0:WIN], ident[:])
                last = nc.tensor.transpose(bank[7][0:NS, (2 + g) * P:(3 + g) * P], p[:, g, WIN:], ident[:])
            last.then_inc(S["pt0_full"].sem, 1)
            pe.wait_ge(S["pt0_read_a"].sem, S["pt0_read_a"].count(1))
            pe.wait_ge(S["pt0_read_b"].sem, S["pt0_read_b"].count(1))
            for s in range(NSEQ):
                cols = slice(32 * (s % 4), 32 * (s % 4) + 32)
                o = bank[7][:, 256 + 32 * s:256 + 32 * (s + 1)]
                mm(o, v_cache[:, s], pt_cache[:, s // 4, cols], start=True, stop=False)
                last = mm(o, kv_tok[:, 1], pt_new[:, s // 4, cols], start=False, stop=True)
            last.then_inc(S["ow0_full"].sem, 1)

        S["sums_full"].passed(1)


def merge_phase(pg):
    nc, dram = pg.nc, pg.dram
    S = pg
    z, merged = dram["z"], dram["merged"]
    NT = D // P
    with ExitStack() as own, nc.Block() as block:
        def sb(name, shape, dt=F32):
            return own.enter_context(nc.sbuf_tensor(f"{name}_mrg", shape, dt))
        ws = WeightStream(pg, sb, dram["w_branch"], 8, "mrg")
        o_raw, o_hi, o_lo = sb("o_raw", [P, 8, TB]), sb("o_hi", [P, 8, TB], F32R), sb("o_lo", [P, 8, TB], F32R)
        gates = [sb(f"gates{i}", [P, 2, TB]) for i in range(2)]
        part = [sb(f"part{i}", [P, 2, TB]) for i in range(2)]
        out = [sb(f"merged{i}", [P, TB]) for i in range(2)]
        gates_in, stored = [S["gates_in_even"], S["gates_in_odd"]], [S["merged_stored_even"], S["merged_stored_odd"]]

        def tokens(b):
            return slice(b * TB, (b + 1) * TB) if isinstance(b, int) else bass.ds(b * TB, TB)

        @block.sync
        def _(sp):
            def unit(b, n, tail):
                if n == 0:
                    if (due := S["o_lo_ready"].count(b)) is not None:
                        sp.wait_ge(S["o_lo_ready"].sem, due)
                    sp.dma_start(o_raw[:], dram["o"][:, :, tokens(b)].rearrange("t p c -> p t c")).then_inc(S["o_in"].sem, 16)
                if isinstance(b, int) and b == 0 and n == 0:
                    ws.load(sp, 0, 0, 0)
                    ws.load(sp, 1, 0, 1)
                if (due := S["parts_ready"].count(b * NT + (n - 1))) is not None:
                    sp.wait_ge(S["parts_ready"].sem, due)
                for i, tile in enumerate((Z_GATE_A, Z_GATE_B)):
                    sp.dma_start(gates[n % 2][:, i], z[tile + n, :, tokens(b)]).then_inc(gates_in[n % 2].sem, 16)
                if n >= 2 or not (isinstance(b, int) and b == 0):
                    back = b * NT + (n - 1)
                    if (due := S["merged_ready"].count(back)) is not None:
                        sp.wait_ge(S["merged_ready"].sem, due)
                    pb, pn = (b, n - 2) if n >= 2 else (b - 1, n + NT - 2)
                    sp.dma_start(merged[pn, :, tokens(pb)], out[n % 2][:]).then_inc(stored[n % 2].sem, 16)
                if not (tail and n >= NT - 2):
                    sp.wait_ge(ws.lo_ready.sem, ws.lo_ready.count(b * NT + (n + 1)))
                    sp.dma_start(ws.raw[n % 2][:], dram["w_branch"][(n + 2) % NT]).then_inc(ws.w_in[n % 2].sem, 16)
            each_last(sp, NB, lambda b, tail: [unit(b, n, tail) for n in range(NT)])
            for n in range(2):
                sp.wait_ge(S["merged_ready"].sem, S["merged_ready"].count(NB * NT - 1 + n))
                sp.dma_start(merged[NT - 2 + n, :, tokens(NB - 1)], out[n][:]).then_inc(stored[n].sem, 16)
            for n in range(2):
                sp.wait_ge(stored[n].sem, stored[n].count(NB * NT // 2 * 16))

        @block.scalar
        def _(act):
            def split(b, n):
                act.wait_ge(ws.w_in[n % 2].sem, ws.w_in[n % 2].count((b * (NT // 2) + n // 2 + 1) * 16))
                if (due := S["unit_done"].count(b * NT + (n - 1))) is not None:
                    act.wait_ge(S["unit_done"].sem, due)
                nc.scalar.activation(ws.hi[n % 2][:], ws.raw[n % 2][:], ACT.Copy).then_inc(ws.hi_ready.sem, 1)

            def unit(b, n, tail):
                if n == 0:
                    act.wait_ge(S["o_in"].sem, S["o_in"].count((b + 1) * 16))
                    for k in range(8):
                        last = nc.scalar.activation(o_hi[:, k], o_raw[:, k], ACT.Copy)
                        last.then_inc(S["o_hi_ready"].sem, 1)
                act.wait_ge(gates_in[n % 2].sem, gates_in[n % 2].count((b * (NT // 2) + n // 2 + 1) * 32))
                nc.scalar.activation(gates[n % 2][:], gates[n % 2][:], ACT.Sigmoid).then_inc(S["gates_ready"].sem, 1)
                act.wait_ge(S["unit_done"].sem, S["unit_done"].count(b * NT + (n + 1)))
                if not (tail and n >= NT - 2):
                    if n < NT - 2:
                        split(b, n + 2)
                    else:
                        split(b + 1, n + 2 - NT)
            split(0, 0)
            split(0, 1)
            each_last(act, NB, lambda b, tail: [unit(b, n, tail) for n in range(NT)])

        @block.vector
        def _(dve):
            v = nc.vector

            def split(b, n):
                dve.wait_ge(ws.hi_ready.sem, ws.hi_ready.count(b * NT + (n + 1)))
                v.tensor_tensor(ws.lo[n % 2][:], ws.raw[n % 2][:], ws.hi[n % 2][:].bitcast(F32), ALU.subtract).then_inc(ws.lo_ready.sem, 1)

            def unit(b, n, tail):
                if n == 0:
                    for k in range(8):
                        dve.wait_ge(S["o_hi_ready"].sem, S["o_hi_ready"].count(b * 8 + (k + 1)))
                        last = v.tensor_tensor(o_lo[:, k], o_raw[:, k], o_hi[:, k].bitcast(F32), ALU.subtract)
                    last.then_inc(S["o_lo_ready"].sem, 1)
                dve.wait_ge(S["unit_done"].sem, S["unit_done"].count(b * NT + (n + 1)))
                dve.wait_ge(S["gates_ready"].sem, S["gates_ready"].count(b * NT + (n + 1)))
                if (due := S["merged_ready"].count(b * NT + (n - 1))) is not None:
                    dve.wait_ge(S["merged_ready"].sem, due)
                for i in range(2):
                    last = v.tensor_tensor(part[n % 2][:, i], gates[n % 2][:, i], pg.bank[(n % 4) * 2 + i][:, :TB], ALU.mult)
                last.then_inc(S["parts_ready"].sem, 1)
                if not (tail and n >= NT - 2):
                    if n < NT - 2:
                        split(b, n + 2)
                    else:
                        split(b + 1, n + 2 - NT)
            split(0, 0)
            split(0, 1)
            each_last(dve, NB, lambda b, tail: [unit(b, n, tail) for n in range(NT)])

        @block.gpsimd
        def _(pool):
            def unit(b, n):
                pool.wait_ge(S["parts_ready"].sem, S["parts_ready"].count(b * NT + (n + 1)))
                if isinstance(b, int):
                    if (due := stored[n % 2].count((b * NT // 2 + n // 2) * 16)) is not None:
                        pool.wait_ge(stored[n % 2].sem, due)
                else:
                    if (due := stored[n % 2].count((b * (NT // 2) + n // 2) * 16)) is not None:
                        pool.wait_ge(stored[n % 2].sem, due)
                nc.gpsimd.tensor_tensor(out[n % 2][:], part[n % 2][:, 0], part[n % 2][:, 1], ALU.add).then_inc(S["merged_ready"].sem, 1)
            each(pool, NB, lambda b: [unit(b, n) for n in range(NT)])

        @block.tensor
        def _(pe):
            def unit(b, n):
                pe.wait_ge(ws.hi_ready.sem, ws.hi_ready.count(b * NT + (n + 1)))
                pe.wait_ge(ws.lo_ready.sem, ws.lo_ready.count(b * NT + (n + 1)))
                if n == 0:
                    pe.wait_ge(S["o_lo_ready"].sem, S["o_lo_ready"].count(b + 1))
                if (due := S["parts_ready"].count(b * NT + (n - 3))) is not None:
                    pe.wait_ge(S["parts_ready"].sem, due)
                for i in range(2):
                    for k in range(4):
                        kk = 4 * i + k
                        last = pg.split_matmul(pg.bank[(n % 4) * 2 + i][:, :TB], ws.hi[n % 2][:, kk], ws.lo[n % 2][:, kk],
                                               o_hi[:, kk], o_lo[:, kk], k == 0, k == 3)
                last.then_inc(S["unit_done"].sem, 1)
            each(pe, NB, lambda b: [unit(b, n) for n in range(NT)])

        ws.passed(NB * NT)
        S["unit_done"].passed(NB * NT)


def each_last(engine, n, body):
    body(0, n == 1)
    if n > 2:
        with engine.Fori(1, n - 1) as i:
            body(i, False)
    if n > 1:
        body(n - 1, True)


def project_out_phase(pg, tag, src, weights, nk, norm_w, residual, dst):
    nc, dram = pg.nc, pg.dram
    S = pg
    NT = D // P
    KK = nk // 2
    U = 2 * KK
    BANKS = ((1, 2, 3, 0), (4, 5, 6, 0))
    SUMS = pg.bank[7]
    NORM_AT = 2
    with ExitStack() as own, nc.Block() as block:
        def sb(name, shape, dt=F32):
            return own.enter_context(nc.sbuf_tensor(f"{name}_{tag}", shape, dt))
        ws = WeightStream(pg, sb, weights, 8, tag)
        raw = [sb(f"src_raw{i}", [P, 2, TB]) for i in range(2)]
        s_hi, s_lo = sb("src_hi", [P, nk, TB], F32R), sb("src_lo", [P, nk, TB], F32R)
        y, x = sb("y", [P, NT, TB]), sb("x", [P, NT, TB])
        sq = [sb(f"sq{i}", [P, TB]) for i in range(2)]
        acc, rstd = sb("acc", [P, TB]), sb("rstd", [P, TB])
        w, ones, eps = sb("norm_w", [P, NT]), sb("ones", [P, P]), sb("eps", [P, 1])
        src_in = [S["src_in_even"], S["src_in_odd"]]
        src_loads = [(KK + 1) // 2, KK // 2]

        def tokens(b):
            return slice(b * TB, (b + 1) * TB) if isinstance(b, int) else bass.ds(b * TB, TB)

        def first(b):
            return isinstance(b, int) and b == 0

        @block.sync
        def _(sp):
            sp.dma_start(w[:], norm_w).then_inc(S["const_in"].sem, 16)

            def load_src(b, kk):
                before = b * KK + (kk - 1) if kk >= 2 else b * KK - (KK - 1 - max(k for k in range(KK) if k % 2 == kk))
                if (due := S["src_lo_ready"].count(before)) is not None:
                    sp.wait_ge(S["src_lo_ready"].sem, due)
                sp.dma_start(raw[kk % 2][:], src[2 * kk:2 * kk + 2, :, tokens(b)].rearrange("t p c -> p t c")
                             ).then_inc(src_in[kk % 2].sem, 16)

            def load_w(b, un):
                if (due := ws.lo_ready.count(b * U + (un - 1))) is not None:
                    sp.wait_ge(ws.lo_ready.sem, due)
                sp.dma_start(ws.raw[un % 2][:], weights[un]).then_inc(ws.w_in[un % 2].sem, 16)

            def body(b, tail):
                for un in range(U):
                    if un + 2 < U:
                        load_w(b, un + 2)
                    elif not tail:
                        load_w(b + 1, un + 2 - U)
                    if un >= KK and not tail:
                        load_src(b + 1, un - KK)
                    if un == KK - 1 and not first(b):
                        if (due := S["y_added"].count(b)) is not None:
                            sp.wait_ge(S["y_added"].sem, due)
                        sp.dma_start(dst[:, :, tokens(b - 1)].rearrange("k p t -> p k t"), y[:]).then_inc(S["y_stored"].sem, 16)
                    if un == KK - 1:
                        if (due := S["y_added"].count(b)) is not None:
                            sp.wait_ge(S["y_added"].sem, due)
                        sp.dma_start(x[:], residual[:, :, tokens(b)].rearrange("k p t -> p k t")).then_inc(S["residual_in"].sem, 16)
            for kk in range(KK):
                load_src(0, kk)
                if kk < 2:
                    load_w(0, kk)
            each_last(sp, NB, body)
            sp.wait_ge(S["y_added"].sem, S["y_added"].count(NB))
            sp.dma_start(dst[:, :, tokens(NB - 1)].rearrange("k p t -> p k t"), y[:]).then_inc(S["y_stored"].sem, 16)
            sp.wait_ge(S["y_stored"].sem, S["y_stored"].count(NB * 16))

        @block.scalar
        def _(act):
            def copy(out, in_):
                return nc.scalar.activation(out, in_, ACT.Copy)

            def split_w(b, un):
                act.wait_ge(ws.w_in[un % 2].sem, ws.w_in[un % 2].count((b * KK + (un // 2 + 1)) * 16))
                copy(ws.hi[un % 2][:], ws.raw[un % 2][:]).then_inc(ws.hi_ready.sem, 1)

            def split_src(b, kk):
                act.wait_ge(src_in[kk % 2].sem, src_in[kk % 2].count((b * src_loads[kk % 2] + (kk // 2 + 1)) * 16))
                copy(s_hi[:, 2 * kk:2 * kk + 2], raw[kk % 2][:]).then_inc(S["src_hi_ready"].sem, 1)

            def evacuate(b, half):
                if (due := S["y_stored"].count(b * 16)) is not None:
                    act.wait_ge(S["y_stored"].sem, due)
                for j in range(4):
                    n = 4 * half + j
                    if j < 3:
                        act.wait_ge(S["column_full"].sem, S["column_full"].count(b * 6 + (half * 3 + j + 1)))
                    if (due := S["squares_added"].count(b * NT + (n - 1))) is not None:
                        act.wait_ge(S["squares_added"].sem, due)
                    bank = pg.bank[BANKS[half][j]]
                    copy(y[:, n], bank[:, :TB])
                    nc.scalar.activation(sq[n % 2][:], bank[:, :TB], ACT.Square).then_inc(S["column_read"].sem, 1)

            def root(b):
                act.wait_ge(S["sums_full"].sem, S["sums_full"].count(b + 1))
                nc.scalar.activation(rstd[:], SUMS[:, :TB], ACT.Sqrt, bias=eps[:], scale=1.0 / D).then_inc(S["rooted"].sem, 1)

            def body(b, tail):
                for un in range(U):
                    act.wait_ge(S["unit_done"].sem, S["unit_done"].count(b * U + (un + 1)))
                    if un + 2 < U:
                        split_w(b, un + 2)
                    elif not tail:
                        split_w(b + 1, un + 2 - U)
                    if un >= KK and not tail:
                        split_src(b + 1, un - KK)
                    if un == NORM_AT and not first(b):
                        root(b - 1)
                    if un == KK - 1:
                        evacuate(b, 0)
                    if un == U - 1:
                        evacuate(b, 1)
            act.wait_ge(S["const_set"].sem, S["const_set"].count(2))
            for kk in range(KK):
                split_src(0, kk)
                if kk < 2:
                    split_w(0, kk)
            each_last(act, NB, body)
            root(NB - 1)

        @block.vector
        def _(dve):
            v = nc.vector

            def split_w(b, un):
                dve.wait_ge(ws.hi_ready.sem, ws.hi_ready.count(b * U + (un + 1)))
                v.tensor_tensor(ws.lo[un % 2][:], ws.raw[un % 2][:], ws.hi[un % 2][:].bitcast(F32), ALU.subtract).then_inc(ws.lo_ready.sem, 1)

            def split_src(b, kk):
                dve.wait_ge(S["src_hi_ready"].sem, S["src_hi_ready"].count(b * KK + (kk + 1)))
                pair = slice(2 * kk, 2 * kk + 2)
                v.tensor_tensor(s_lo[:, pair], raw[kk % 2][:], s_hi[:, pair].bitcast(F32), ALU.subtract).then_inc(S["src_lo_ready"].sem, 1)

            def norm(b):
                dve.wait_ge(S["rooted"].sem, S["rooted"].count(b + 1))
                v.reciprocal(rstd[:], rstd[:]).then_inc(S["inverted"].sem, 1)
                dve.wait_ge(S["inverted"].sem, S["inverted"].count(b + 1))
                dve.wait_ge(S["column_read"].sem, S["column_read"].count((b + 1) * NT))
                for n in range(NT):
                    v.scalar_tensor_tensor(y[:, n], y[:, n], w[:, n:n + 1], rstd[:], ALU.mult, ALU.mult).then_inc(S["y_normed"].sem, 1)

            def body(b, tail):
                for un in range(U):
                    if un + 2 < U:
                        split_w(b, un + 2)
                    elif not tail:
                        split_w(b + 1, un + 2 - U)
                    if un >= KK and not tail:
                        split_src(b + 1, un - KK)
                    if un == NORM_AT and not first(b):
                        norm(b - 1)
            v.memset(ones[:], 1.0).then_inc(S["const_set"].sem, 1)
            v.memset(eps[:], EPS).then_inc(S["const_set"].sem, 1)
            dve.wait_ge(S["const_in"].sem, S["const_in"].count(16))
            for kk in range(KK):
                split_src(0, kk)
                if kk < 2:
                    split_w(0, kk)
            each_last(dve, NB, body)
            norm(NB - 1)

        @block.gpsimd
        def _(pool):
            g = nc.gpsimd

            def body(b):
                for n in range(NT):
                    if n == 0 and not first(b):
                        add(b - 1)
                    pool.wait_ge(S["column_read"].sem, S["column_read"].count(b * NT + (n + 1)))
                    if n == 1:
                        if (due := S["sums_full"].count(b)) is not None:
                            pool.wait_ge(S["sums_full"].sem, due)
                        g.tensor_tensor(acc[:], sq[0][:], sq[1][:], ALU.add).then_inc(S["squares_added"].sem, 2)
                    elif n > 1:
                        if (due := S["squares_added"].count(b * NT + n)) is not None:
                            pool.wait_ge(S["squares_added"].sem, due)
                        g.tensor_tensor(acc[:], acc[:], sq[n % 2][:], ALU.add).then_inc(S["squares_added"].sem, 1)

            def add(b):
                pool.wait_ge(S["residual_in"].sem, S["residual_in"].count((b + 1) * 16))
                for n in range(NT):
                    pool.wait_ge(S["y_normed"].sem, S["y_normed"].count(b * NT + (n + 1)))
                    last = g.tensor_tensor(y[:, n], y[:, n], x[:, n], ALU.add)
                last.then_inc(S["y_added"].sem, 1)
            each(pool, NB, body)
            add(NB - 1)

        @block.tensor
        def _(pe):
            def sums(b):
                pe.wait_ge(S["squares_added"].sem, S["squares_added"].count((b + 1) * NT))
                if (due := S["rooted"].count(b)) is not None:
                    pe.wait_ge(S["rooted"].sem, due)
                nc.tensor.matmul(SUMS[:, :TB], ones[:], acc[:], start=True, stop=True).then_inc(S["sums_full"].sem, 1)

            def body(b):
                for half in range(2):
                    for kk in range(KK):
                        un = half * KK + kk
                        if un == NORM_AT and not first(b):
                            sums(b - 1)
                        pe.wait_ge(ws.hi_ready.sem, ws.hi_ready.count(b * U + (un + 1)))
                        pe.wait_ge(ws.lo_ready.sem, ws.lo_ready.count(b * U + (un + 1)))
                        if half == 0:
                            pe.wait_ge(S["src_lo_ready"].sem, S["src_lo_ready"].count(b * KK + (kk + 1)))
                        for j in range(4):
                            if kk == 0:
                                n = 4 * half + j
                                if (due := S["column_read"].count(b * NT + (n - 7 if j < 3 else (0, 4)[half]))) is not None:
                                    pe.wait_ge(S["column_read"].sem, due)
                            bank = pg.bank[BANKS[half][j]][:, :TB]
                            for k in range(2):
                                at = k * 4 + j
                                last = pg.split_matmul(bank, ws.hi[un % 2][:, at], ws.lo[un % 2][:, at], s_hi[:, 2 * kk + k], s_lo[:, 2 * kk + k],
                                                       kk == 0 and k == 0, kk == KK - 1 and k == 1)
                            if kk == KK - 1 and j < 3:
                                last.then_inc(S["column_full"].sem, 1)
                        last.then_inc(S["unit_done"].sem, 1)
            pe.wait_ge(S["const_set"].sem, S["const_set"].count(2))
            each(pe, NB, body)
            sums(NB - 1)

        ws.w_in[0].passed(NB * KK * 16)
        ws.w_in[1].passed(NB * KK * 16)
        ws.hi_ready.passed(NB * U)
        ws.lo_ready.passed(NB * U)
        S["unit_done"].passed(NB * U)
        for i in range(2):
            src_in[i].passed(NB * src_loads[i] * 16)
        for name, n in (("src_hi_ready", NB * KK), ("src_lo_ready", NB * KK), ("column_full", NB * 6), ("column_read", NB * NT),
                        ("squares_added", NB * NT), ("y_normed", NB * NT), ("y_added", NB), ("rooted", NB), ("inverted", NB),
                        ("sums_full", NB), ("y_stored", NB * 16), ("residual_in", NB * 16), ("const_in", 16), ("const_set", 2)):
            S[name].passed(n)


def ffn_in_phase(pg):
    nc, dram = pg.nc, pg.dram
    S = pg
    LU = 2 + SEQ + NSEQ * (2 + SLEN)
    LC = LU - 2
    LAST = (NB - 1) * TB
    TAIL = SEQ - LAST
    U_BANKS, G_BANK0 = 2, 2
    with ExitStack() as own, nc.Block() as block:
        def sb(name, shape, dt=F32):
            return own.enter_context(nc.sbuf_tensor(f"{name}_ffn", shape, dt))
        h_hi, h_lo = sb("h_hi", [P, KD, T], F32R), sb("h_lo", [P, KD, T], F32R)
        ws = WeightStream(pg, sb, dram["w_ffn_in"], KD, "ffn")
        consts, norm_sync, norm_scalar, norm_vector, norm_tensor, norm_done, spare = norm_blocks(
            pg, sb, block, dram["x1"].rearrange("k p t -> (k p) t"), dram["norm_ffn_pre"], h_hi, h_lo, "ffn")
        up = spare[0][:].rearrange("p k t -> p (k t)")[:, 0:LU]
        conv = spare[1][:].rearrange("p k t -> p (k t)")[:, 0:LC]
        smp = sb("act_sample", [P, NS])
        taps, states, kept = sb("taps", [P, KF, 4]), sb("states", [P, KF, NSEQ, 2]), sb("kept", [P, KF, 2 + 2 * NSEQ])
        stored = S["act_stored"]

        def sample_cols(ap, start, n, at):
            return ap[:, start:start + NSEQ * (2 + SLEN)].rearrange("p (s c) -> p s c", s=NSEQ)[:, :, at:at + n]

        def reg_tile(t, j):
            return t[:, one(j)]

        @block.sync
        def _(sp):
            consts(sp)
            sp.dma_start(taps[:], dram["conv_taps"]).then_inc(S["ffn_const_in"].sem, 16)
            sp.dma_start(states[:], dram["conv_states"]).then_inc(S["ffn_const_in"].sem, 16)
            norm_sync(sp, 0)
            norm_sync(sp, 1)
            ws.load(sp, 0, 0, 0)
            ws.load(sp, 1, 0, 1)
            for b in range(2, NB):
                norm_sync(sp, b)

            def body(n, j, slot):
                if slot == 1:
                    sp.wait_ge(S["g_read"].sem, S["g_read"].count((j + 1) * NB))
                    a = dram["act"][one(j)].rearrange("o p t -> (o p) t")
                    sp.dma_start(a[:, 0:SEQ], conv[:, 0:SEQ]).then_inc(stored.sem, 16)
                    sp.dma_start(a[:, SEQ:T], smp[:]).then_inc(stored.sem, 16)
                if not isinstance(n, int) or n + 2 < 2 * KF:
                    ws.load(sp, n + 2, j + 1, slot)
            each_pair_ahead(sp, 2 * KF, body)
            sp.wait_ge(S["u_read"].sem, S["u_read"].count(KF * NB))
            sp.dma_start(dram["conv_kept"], kept[:]).then_inc(S["kept_stored"].sem, 16)
            sp.wait_ge(S["kept_stored"].sem, S["kept_stored"].count(16))
            sp.wait_ge(stored.sem, stored.count(KF * 32))

        @block.scalar
        def _(act):
            norm_scalar(act, 0)
            ws.split_hi(act, 0, 0, 0)
            ws.split_hi(act, 1, 0, 1)
            for b in range(1, NB):
                norm_scalar(act, b)
            act.wait_ge(S["h_full"].sem, S["h_full"].count(NB))

            def body(n, j, slot):
                if slot == 0:
                    if (due := S["conv_done"].count(j)) is not None:
                        act.wait_ge(S["conv_done"].sem, due)
                    for b in range(NB):
                        act.wait_ge(S["psum_full"].sem, S["psum_full"].count(n * NB + (b + 1)))
                        src = pg.bank[b % U_BANKS]
                        if b < NB - 1:
                            nc.scalar.activation(up[:, 2 + b * TB:2 + (b + 1) * TB], src[:, :TB], ACT.Copy).then_inc(S["u_read"].sem, 1)
                        else:
                            smp_u = src[:, TAIL:TB].rearrange("p (s c) -> p s c", s=NSEQ)
                            nc.scalar.activation(up[:, 2 + LAST:2 + SEQ], src[:, :TAIL], ACT.Copy)
                            nc.scalar.activation(sample_cols(up, 2 + SEQ, SLEN, 2), smp_u, ACT.Copy)
                            k = kept[:, one(j)].rearrange("p o c -> p (o c)")
                            nc.scalar.activation(k[:, 0:2], src[:, TAIL - 2:TAIL], ACT.Copy)
                            nc.scalar.activation(k[:, 2:].rearrange("p (s c) -> p s c", s=NSEQ), smp_u[:, :, SLEN - 2:], ACT.Copy
                                                 ).then_inc(S["u_read"].sem, 1)
                else:
                    act.wait_ge(S["conv_done"].sem, S["conv_done"].count(j + 1))
                    nc.scalar.activation(conv[:, 0:SEQ], conv[:, 0:SEQ], ACT.Gelu_apprx_tanh)
                    if (due := stored.count(j * 32)) is not None:
                        act.wait_ge(stored.sem, due)
                    nc.scalar.activation(smp[:].rearrange("p (s c) -> p s c", s=NSEQ), sample_cols(conv, SEQ, SLEN, 2),
                                         ACT.Gelu_apprx_tanh).then_inc(S["gelu_done"].sem, 1)
                if not isinstance(n, int) or n + 2 < 2 * KF:
                    ws.split_hi(act, n + 2, j + 1, slot)
            each_pair_ahead(act, 2 * KF, body)

        @block.vector
        def _(dve):
            v = nc.vector
            norm_vector(dve)
            ws.split_lo(dve, 0, 0, 0)
            ws.split_lo(dve, 1, 0, 1)
            dve.wait_ge(S["ffn_const_in"].sem, S["ffn_const_in"].count(32))

            def body(n, j, slot):
                if slot == 0:
                    tap = lambda i: taps[:, one(j), i:i + 1].rearrange("p o c -> p (o c)")
                    dve.wait_ge(S["u_read"].sem, S["u_read"].count((j + 1) * NB))
                    dve.wait_ge(S["heads_set"].sem, S["heads_set"].count(j + 1))
                    if (due := stored.count(j * 32)) is not None:
                        dve.wait_ge(stored.sem, due)
                    v.tensor_scalar(conv, up[:, 2:], tap(2), tap(3), ALU.mult, ALU.add).then_inc(S["tap2_done"].sem, 1)
                    dve.wait_ge(S["tap2_done"].sem, S["tap2_done"].count(j + 1))
                    v.scalar_tensor_tensor(conv, up[:, 1:LU - 1], tap(1), conv, ALU.mult, ALU.add).then_inc(S["tap1_done"].sem, 1)
                    dve.wait_ge(S["tap1_done"].sem, S["tap1_done"].count(j + 1))
                    v.scalar_tensor_tensor(conv, up[:, 0:LU - 2], tap(0), conv, ALU.mult, ALU.add).then_inc(S["conv_done"].sem, 1)
                else:
                    dve.wait_ge(S["gelu_done"].sem, S["gelu_done"].count(j + 1))
                    for b in range(NB):
                        dve.wait_ge(S["psum_full"].sem, S["psum_full"].count(n * NB + (b + 1)))
                        g = pg.bank[G_BANK0 + b]
                        cols = slice(b * TB, min((b + 1) * TB, SEQ))
                        last = v.tensor_tensor(conv[:, cols], conv[:, cols], g[:, :cols.stop - cols.start], ALU.mult)
                        if b == NB - 1:
                            last = v.tensor_tensor(smp[:], smp[:], g[:, TAIL:TB], ALU.mult)
                        last.then_inc(S["g_read"].sem, 1)
                if not isinstance(n, int) or n + 2 < 2 * KF:
                    ws.split_lo(dve, n + 2, j + 1, slot)
            each_pair_ahead(dve, 2 * KF, body)

        @block.gpsimd
        def _(pool):
            pool.wait_ge(S["ffn_const_in"].sem, S["ffn_const_in"].count(32))
            pool.wait_ge(S["h_full"].sem, S["h_full"].count(NB))
            nc.gpsimd.memset(up[:, 0:2], 0.0).then_inc(S["u_front_zeroed"].sem, 1)
            pool.wait_ge(S["u_front_zeroed"].sem, S["u_front_zeroed"].count(1))

            def body(j):
                if (due := S["conv_done"].count(j)) is not None:
                    pool.wait_ge(S["conv_done"].sem, due)
                pool.wait_ge(S["u_front_zeroed"].sem, S["u_front_zeroed"].count(1))
                nc.gpsimd.tensor_copy(sample_cols(up, 2 + SEQ, 2, 0), states[:, one(j)].rearrange("p o s c -> p (o s) c")
                                      ).then_inc(S["heads_set"].sem, 1)
            each(pool, KF, body)

        @block.tensor
        def _(pe):
            norm_tensor(pe)

            def body(n, j, slot):
                pe.wait_ge(ws.hi_ready.sem, ws.hi_ready.count(n + 1))
                pe.wait_ge(ws.lo_ready.sem, ws.lo_ready.count(n + 1))
                for b in range(NB):
                    if isinstance(n, int) and n == 0:
                        pe.wait_ge(S["h_lo_ready"].sem, S["h_lo_ready"].count(b + 1))
                    if slot == 0:
                        if (due := S["u_read"].count(j * NB + (b - 1))) is not None:
                            pe.wait_ge(S["u_read"].sem, due)
                        bank = pg.bank[b % U_BANKS]
                    else:
                        if (due := S["g_read"].count((j - 1) * NB + (b + 1))) is not None:
                            pe.wait_ge(S["g_read"].sem, due)
                        bank = pg.bank[G_BANK0 + b]
                    project_block(pg, ws, h_hi, h_lo, bank, n, slot, b)
            each_pair(pe, 2 * KF, body)

        norm_done()
        ws.passed(2 * KF)


def build(nc, dram):
    with ExitStack() as ctx:
        pg = Program(nc, ctx, dram)
        mixer_phases(pg)
        sample_phase(pg)
        merge_phase(pg)
        project_out_phase(pg, "mix", dram["merged"], dram["w_out"], KD, dram["norm_mix_post"],
                          dram["xT"].rearrange("(k p) t -> k p t", p=P), dram["x1"])
        ffn_in_phase(pg)
        project_out_phase(pg, "out", dram["act"], dram["w_ffn_out"], KF, dram["norm_ffn_post"], dram["x1"], dram["yT"])


def tiles(w, columns):
    w = w[:, columns].reshape(w.shape[0] // P, P, len(columns) // P, P)
    return np.ascontiguousarray(w.transpose(2, 1, 0, 3))


def by_partition(v):
    return np.ascontiguousarray(v.reshape(-1, P).T)


def units(w):
    w = w.reshape(w.shape[0] // (2 * P), 2, P, 2, 4, P)
    return np.ascontiguousarray(w.transpose(3, 0, 2, 1, 4, 5)).reshape(-1, P, 8, P)


def sample_bias(slopes):
    s4, kv, t, tok, g, key = np.meshgrid(*[np.arange(n) for n in (4, KVH, 4, SLEN, 2, WIN + NS)], indexing="ij")
    new = key - WIN
    rel = np.where(key < WIN, tok + WIN - key, tok - new % SLEN)
    seen = (rel >= 0) & (rel < WIN) & ((key < WIN) | (new // SLEN == 4 * g + s4))
    return np.where(seen, -slopes[kv * 4 + t] * rel, NEG).astype(np.float32).reshape(P, 2, WIN + NS)


def host_arrays(a):
    w_in = a["w_in"][0]
    edges = np.cumsum([0, 256, 256, 512, RANK, 512, 512, 128, 128, D, D])
    qa, ka, va, r, ga, qb, kb, vb, gate_a, gate_b = (np.arange(x, y) for x, y in zip(edges[:-1], edges[1:]))
    head_rows = np.concatenate([np.r_[t * HD:(t + 1) * HD, (t + 4) * HD:(t + 5) * HD] for t in range(4)])
    columns = np.concatenate([qa, ka, va, ga, np.full(P, edges[-1]), qb[head_rows], kb, vb, gate_a, gate_b])
    columns[12 * P:12 * P + RANK] = r
    w_in = np.concatenate([w_in, np.zeros((D, 1), w_in.dtype)], axis=1)
    x = np.concatenate([a["x_prompt"][0], a["x_sample"].reshape(NS, D)], axis=0)
    w_up = np.zeros((P, H * DK), np.float32)
    w_up[:RANK] = a["w_gate_up"][0]
    head = np.arange(4)[:, None] + 4 * np.arange(2)[None, :]
    q, key = np.arange(WIN)[:, None] + WIN, np.arange(2 * WIN)[None, :]
    rel = np.where((q >= key) & (q - key < WIN), key - q, NEG).astype(np.float32)
    t = np.arange(P)
    out = {
        "xT": np.ascontiguousarray(x.T),
        "w_in": tiles(w_in, columns),
        "norm_mix_pre": by_partition(a["norm_mix_pre"]),
        "w_gate_up": w_up, "b_gate": by_partition(a["b_gate"]), "gla_norm": by_partition(a["gla_norm"]),
        "sinks": np.ascontiguousarray(np.broadcast_to(a["sinks"][0][head], (P, 4, 2))),
        "ident": np.eye(P, dtype=np.float32),
        "rel": rel, "rel_first": np.where(key < WIN, NEG, rel).astype(np.float32),
        "scan_keep": np.ascontiguousarray(np.broadcast_to((np.arange(2 * P) % CH != 0).astype(np.float32), (P, 2 * P))),
        "causal": ((t[:, None] // CH == t[None] // CH) & (t[:, None] <= t[None])).astype(np.float32),
    }
    s = np.arange(NS)
    w_ffn_in = a["w_ffn_in"][0]
    ffn_columns = np.concatenate([np.arange(j * P, (j + 1) * P) + half * FF for j in range(KF) for half in range(2)])
    taps = np.concatenate([a["conv_w"][0], a["conv_b"]], axis=0)
    caches = {n: a[f"cache_swa_{n}"][0].reshape(NSEQ, WIN, P) for n in ("k", "v")}
    out.update({
        "k_cache": np.ascontiguousarray(caches["k"]), "v_cache": np.ascontiguousarray(caches["v"]),
        "k_cacheT": np.ascontiguousarray(caches["k"].transpose(2, 0, 1)),
        "state_gla": np.ascontiguousarray(a["state_gla"][0]),
        "sample_keep": np.ascontiguousarray(np.broadcast_to((np.arange(2 * NS) % SLEN != 0).astype(np.float32), (P, 2 * NS))),
        "sample_causal": ((s[:, None] // SLEN == s[None] // SLEN) & (s[:, None] <= s[None])).astype(np.float32),
        "sample_rows": (s[:, None] // SLEN == np.arange(NSEQ)[None]).astype(np.float32),
        "sample_bias": sample_bias(np.array([slope(n) for n in range(QH)])),
        "sample_sinks": np.ascontiguousarray(np.tile(np.repeat(a["sinks"][0], SLEN), 4)[:, None]),
        "w_branch": np.concatenate([tiles(a["w_branch_a"][0], np.arange(D)),
                                    tiles(a["w_branch_b"][0][head_rows], np.arange(D))], axis=2),
        "w_out": units(a["w_out"][0]), "w_ffn_out": units(a["w_ffn_out"][0]),
        "w_ffn_in": tiles(w_ffn_in, ffn_columns),
        "norm_mix_post": by_partition(a["norm_mix_post"]), "norm_ffn_pre": by_partition(a["norm_ffn_pre"]),
        "norm_ffn_post": by_partition(a["norm_ffn_post"]),
        "conv_taps": np.ascontiguousarray(taps.reshape(4, KF, P).transpose(2, 1, 0)),
        "conv_states": np.ascontiguousarray(a["state_ffn_conv"][0].reshape(NSEQ, 2, KF, P).transpose(3, 2, 0, 1)),
    })
    return out


SCRATCH = {"z": (N_Z, P, T), "o": (8, P, T), "merged": (KD, P, T), "x1": (KD, P, T), "act": (KF, P, T)}
OUTPUTS = {"gla_state_prompt": (H, DK, DV), "yT": (KD, P, T), "gla_state_sample": (NSEQ, H, DK, DV),
           "swa_k_promptT": (P, WIN), "swa_v_promptT": (P, WIN),
           "swa_k_sample": (NSEQ, WIN, P), "swa_v_sample": (NSEQ, WIN, P), "conv_kept": (P, KF, 2 + 2 * NSEQ)}


def kernel(**inputs):
    import concourse.bacc as bacc
    from concourse.bass_utils import run_bass_kernel_spmd

    arrays = host_arrays({name: np.asarray(value) for name, value in inputs.items()})
    nc = bacc.Bacc("TRN2", target_bir_lowering=False, num_devices=1)
    dram = {name: nc.dram_tensor(name, a.shape, F32, kind="ExternalInput").ap() for name, a in arrays.items()}
    for name, shape in SCRATCH.items():
        dram[name] = nc.dram_tensor(name, shape, F32, kind="Internal").ap()
    for name, shape in OUTPUTS.items():
        dram[name] = nc.dram_tensor(name, shape, F32, kind="ExternalOutput").ap()
    build(nc, dram)
    out = run_bass_kernel_spmd(nc, [arrays], core_ids=[0]).results[0]

    y = np.asarray(out["yT"]).reshape(D, T).T
    kept = np.asarray(out["conv_kept"]).transpose(2, 1, 0).reshape(1 + NSEQ, 2, FF)
    windows = [np.ascontiguousarray(np.asarray(out[f"swa_{n}_promptT"]).T).reshape(1, 1, WIN, KVH, HD) for n in "kv"]
    caches = [np.asarray(out[f"swa_{n}_sample"]).reshape(1, NSEQ, WIN, KVH, HD) for n in "kv"]
    return (np.ascontiguousarray(y[:SEQ])[None], np.ascontiguousarray(y[SEQ:]).reshape(NSEQ, SLEN, D),
            np.asarray(out["gla_state_prompt"]).reshape(1, 1, H, DK, DV),
            np.asarray(out["gla_state_sample"]).reshape(1, NSEQ, H, DK, DV),
            *windows, *caches, kept[None, :1], kept[None, 1:])
```

```python
import math
from contextlib import ExitStack

import numpy as np

import concourse.bass as bass
from concourse import mybir

ALU = mybir.AluOpType
ACT = mybir.ActivationFunctionType
AX = mybir.AxisListType
F32 = mybir.dt.float32
F32R = mybir.dt.float32r
I32 = mybir.dt.int32

P = 128
D = 1024
SEQ = 2048
NSEQ, SLEN = 8, 4
NS = NSEQ * SLEN
T = SEQ + NS
NB = 5
TB = T // NB
KD = D // P
FF = 2816
KF = FF // P
H, DK, DV, RANK = 4, 64, 128, 16
CH = 64
WIN = 128
NWIN = SEQ // WIN
QH, KVH, HD = 8, 2, 64
EPS = 1e-6
TAU = 16.0
NEG = -1.0e30

Z_QA, Z_KA, Z_VA, Z_GA, Z_R, Z_QB, Z_KB, Z_VB, Z_GATE_A, Z_GATE_B = 0, 2, 4, 8, 12, 13, 17, 18, 19, 27
N_MIX = 19
N_Z = 35

STEP_SIGNALS = """
    abs_exp abs_ready att_full att_ready b_ready centred ei_ready ek_ready eo_ready eq_ready gate_den gate_exp kd_ready
    kd_ready_turned kd_turned kt_ready lm_ready log_a_ready log_ms logits_full o_full o_normed o_squared ow0_full pt0_full
    pt0_read_a pt0_read_b qez_ready qz_ready rstd_ready shifted sigmoid_ready silu_ready softplus_ready sums_full tail_ready
    u_full v_ready v_turned m0_ready exp0_ready sink0_ready sinkexp0_ready s0_ready max0_ready den0_ready inv0_ready p0_ready
    scores0_full
""".split()


class Signal:

    def __init__(self, nc, ctx, name):
        self.sem = ctx.enter_context(nc.semaphore(name))
        self.base = 0

    def count(self, n):
        return None if isinstance(n, int) and n <= 0 else n + self.base

    def passed(self, n):
        self.base += n


def later_pairs(engine, n, body):
    with engine.Fori(1, n // 2) as t:
        body(t * 2, t, 0)
        body(t * 2 + 1, t, 1)
    if n % 2:
        body(n - 1, n // 2, 0)


def later_pairs_ahead(engine, n, body):
    pairs = (n - 2) // 2
    with engine.Fori(1, pairs) as t:
        body(t * 2, t, 0)
        body(t * 2 + 1, t, 1)
    for i in range(pairs * 2, n):
        body(i, i // 2, i % 2)


def each_pair_ahead(engine, n, body):
    for i in range(2):
        body(i, 0, i)
    later_pairs_ahead(engine, n, body)


def each(engine, n, body):
    body(0)
    if n > 1:
        with engine.Fori(1, n) as i:
            body(i)


def one(i):
    return slice(i, i + 1) if isinstance(i, int) else bass.ds(i, 1)


def span(i, size):
    return slice(i * size, i * size + size) if isinstance(i, int) else bass.ds(i * size, size)


class Program:
    def __init__(self, nc, ctx, dram):
        self.nc, self.ctx, self.dram = nc, ctx, dram
        self.signals = {}
        self.bank = [ctx.enter_context(nc.psum_tensor(f"bank{i}", [P, 512], F32)) for i in range(8)]

    def __getitem__(self, name):
        if name not in self.signals:
            self.signals[name] = Signal(self.nc, self.ctx, name)
        return self.signals[name]

    def split_matmul(self, out, w_hi, w_lo, x_hi, x_lo, first, last):
        pe = self.nc.tensor
        pe.matmul(out, w_hi, x_hi, start=first, stop=False)
        pe.matmul(out, w_lo, x_hi, start=False, stop=False)
        return pe.matmul(out, w_hi, x_lo, start=False, stop=last)


class NormParts:

    def __init__(self, sync, square, add, sum_rows, root, high, constants, vector, ready, used, done, x):
        self.sync, self.square, self.add, self.sum_rows, self.root, self.high = sync, square, add, sum_rows, root, high
        self.constants, self.vector, self.ready, self.used, self.done, self.x = constants, vector, ready, used, done, x


def norm_blocks(pg, sb, src, norm_w, h_hi, h_lo, tag):
    nc = pg.nc
    PAIRS = KD // 2
    ADDS = KD - 1
    x = [sb(f"x{i}_{tag}", [P, KD, TB], F32) for i in range(2)]
    sq = [sb(f"sq{i}_{tag}", [P, 2, TB], F32) for i in range(2)]
    h = [sb(f"h{i}_{tag}", [P, 2, TB], F32) for i in range(2)]
    acc, rstd = sb(f"acc_{tag}", [P, TB], F32), sb(f"rstd_{tag}", [P, TB], F32)
    w = sb(f"normw_{tag}", [P, KD], F32)
    ones = sb(f"ones_{tag}", [P, P], F32)
    eps = sb(f"eps_{tag}", [P, 1], F32)
    sums = pg.bank[7]
    x_in = [[pg["x_in_even_first"], pg["x_in_even_last"]], [pg["x_in_odd_first"], pg["x_in_odd_last"]]]
    HALF = KD // 2
    const_in, const_set = pg["const_in"], pg["const_set"]
    squared, added, summed, rooted, inverted = pg["squared"], pg["added"], pg["summed"], pg["rooted"], pg["inverted"]
    h_full, h_hi_ready, h_lo_ready = pg["h_full"], pg["h_hi_ready"], pg["h_lo_ready"]
    xT = src.rearrange("(k p) t -> p k t", p=P)

    def of(t, b, p):
        return t[:, 2 * p:2 * p + 2, b * TB:(b + 1) * TB]

    def sync(sp, b):
        if b == 0:
            sp.dma_start(w[:], norm_w).then_inc(const_in.sem, 16)
        for half in range(2):
            if (due := h_full.count(PAIRS * (b - 2) + PAIRS // 2 * (half + 1))) is not None:
                sp.wait_ge(h_full.sem, due)
            rows = slice(half * HALF, (half + 1) * HALF)
            sp.dma_start(x[b % 2][:, rows], xT[:, rows, b * TB:(b + 1) * TB]).then_inc(x_in[b % 2][half].sem, 16)

    def loaded(engine, b, half):
        came = x_in[b % 2][half]
        engine.wait_ge(came.sem, came.count(16 * (b // 2 + 1)))

    def square(act, b):
        for p in range(PAIRS):
            if p % (PAIRS // 2) == 0:
                loaded(act, b, p // (PAIRS // 2))
            before = ADDS * b + 2 * p - 3 if p >= 2 else ADDS * b - 2 * (1 - p)
            if (due := added.count(before)) is not None:
                act.wait_ge(added.sem, due)
            nc.scalar.activation(sq[p % 2][:], x[b % 2][:, 2 * p:2 * p + 2], ACT.Square).then_inc(squared.sem, 1)

    def add(pool, b):
        for r in range(ADDS):
            if r == 0:
                if (due := summed.count(b)) is not None:
                    pool.wait_ge(summed.sem, due)
                pool.wait_ge(squared.sem, squared.count(PAIRS * b + 1))
                nc.gpsimd.tensor_tensor(acc[:], sq[0][:, 0], sq[0][:, 1], ALU.add).then_inc(added.sem, 1)
            else:
                p = (r + 1) // 2
                pool.wait_ge(squared.sem, squared.count(PAIRS * b + (p + 1)))
                pool.wait_ge(added.sem, added.count(ADDS * b + r))
                nc.gpsimd.tensor_tensor(acc[:], acc[:], sq[p % 2][:, (r + 1) % 2], ALU.add).then_inc(added.sem, 1)

    def sum_rows(pe, b):
        pe.wait_ge(added.sem, added.count(ADDS * (b + 1)))
        pe.wait_ge(const_set.sem, const_set.count(1))
        if (due := rooted.count(b)) is not None:
            pe.wait_ge(rooted.sem, due)
        nc.tensor.matmul(sums[:, :TB], ones[:], acc[:], start=True, stop=True).then_inc(summed.sem, 1)

    def root(act, b):
        act.wait_ge(summed.sem, summed.count(b + 1))
        if (due := h_full.count(PAIRS * b)) is not None:
            act.wait_ge(h_full.sem, due)
        act.wait_ge(const_set.sem, const_set.count(2))
        nc.scalar.activation(rstd[:], sums[:, :TB], ACT.Sqrt, bias=eps[:], scale=1.0 / D).then_inc(rooted.sem, 1)

    def high(act, b):
        for p in range(PAIRS):
            act.wait_ge(h_full.sem, h_full.count(PAIRS * b + (p + 1)))
            nc.scalar.activation(of(h_hi, b, p), h[p % 2][:], ACT.Copy).then_inc(h_hi_ready.sem, 1)

    def constants(dve):
        nc.vector.memset(ones[:], 1.0).then_inc(const_set.sem, 1)
        nc.vector.memset(eps[:], EPS).then_inc(const_set.sem, 1)

    def low(dve, b, p):
        step = PAIRS * b + p
        dve.wait_ge(h_hi_ready.sem, h_hi_ready.count(step + 1))
        dve.wait_ge(h_full.sem, h_full.count(step + 1))
        nc.vector.tensor_tensor(of(h_lo, b, p), h[p % 2][:], of(h_hi, b, p).bitcast(F32), ALU.subtract).then_inc(h_lo_ready.sem, 1)

    def vector(dve):
        dve.wait_ge(const_in.sem, const_in.count(16))
        for b in range(NB):
            dve.wait_ge(rooted.sem, rooted.count(b + 1))
            nc.vector.reciprocal(rstd[:], rstd[:]).then_inc(inverted.sem, 1)
            loaded(dve, b, 0)
            loaded(dve, b, 1)
            for p in range(PAIRS):
                step = PAIRS * b + p
                if p == 1 and b > 0:
                    low(dve, b - 1, PAIRS - 1)
                elif p > 1:
                    low(dve, b, p - 2)
                if p == 0:
                    dve.wait_ge(inverted.sem, inverted.count(b + 1))
                if (due := h_lo_ready.count(step - 1)) is not None:
                    dve.wait_ge(h_lo_ready.sem, due)
                for k in (2 * p, 2 * p + 1):
                    last = nc.vector.scalar_tensor_tensor(h[p % 2][:, k % 2], x[b % 2][:, k], w[:, k:k + 1], rstd[:], ALU.mult, ALU.mult)
                last.then_inc(h_full.sem, 1)
            low(dve, b, PAIRS - 2)
        low(dve, NB - 1, PAIRS - 1)

    def ready(pe, b):
        pe.wait_ge(h_lo_ready.sem, h_lo_ready.count(PAIRS * (b + 1)))
        pe.wait_ge(h_hi_ready.sem, h_hi_ready.count(PAIRS * (b + 1)))

    def used(engine, blocks):
        engine.wait_ge(h_full.sem, h_full.count(PAIRS * blocks))
        engine.wait_ge(squared.sem, squared.count(PAIRS * blocks))

    def done():
        for half in range(2):
            x_in[0][half].passed(16 * 3)
            x_in[1][half].passed(16 * 2)
        const_in.passed(16)
        const_set.passed(2)
        added.passed(ADDS * NB)
        for s in (summed, rooted, inverted):
            s.passed(NB)
        for s in (squared, h_full, h_hi_ready, h_lo_ready):
            s.passed(PAIRS * NB)

    return NormParts(sync, square, add, sum_rows, root, high, constants, vector, ready, used, done, x)


class WeightStream:

    def __init__(self, pg, sb, src, nk, tag):
        self.pg, self.nc, self.src, self.nk = pg, pg.nc, src, nk
        self.raw = [sb(f"w_raw{i}_{tag}", [P, nk, P], F32) for i in range(2)]
        self.hi = [sb(f"w_hi{i}_{tag}", [P, nk, P], F32R) for i in range(2)]
        self.lo = [sb(f"w_lo{i}_{tag}", [P, nk, P], F32R) for i in range(2)]
        self.w_in = [pg["w_in_even"], pg["w_in_odd"]]
        self.hi_ready, self.lo_ready, self.psum_full = pg["w_hi_ready"], pg["w_lo_ready"], pg["psum_full"]

    def load(self, sp, n, pair, slot, at=None):
        if (due := self.lo_ready.count(n - 1)) is not None:
            sp.wait_ge(self.lo_ready.sem, due)
        sp.dma_start(self.raw[slot][:], self.src[one(n if at is None else at)].rearrange("o p k c -> p (o k) c")
                     ).then_inc(self.w_in[slot].sem, 16)

    def split_hi(self, act, n, pair, slot, used=None):
        act.wait_ge(self.w_in[slot].sem, self.w_in[slot].count((pair + 1) * 16))
        if (due := self.psum_full.count((n - 1) * NB if used is None else used)) is not None:
            act.wait_ge(self.psum_full.sem, due)
        self.nc.scalar.activation(self.hi[slot][:], self.raw[slot][:], ACT.Copy).then_inc(self.hi_ready.sem, 1)

    def split_lo(self, dve, n, pair, slot):
        dve.wait_ge(self.hi_ready.sem, self.hi_ready.count(n + 1))
        self.nc.vector.tensor_tensor(self.lo[slot][:], self.raw[slot][:], self.hi[slot][:].bitcast(F32),
                                     ALU.subtract).then_inc(self.lo_ready.sem, 1)

    def passed(self, n):
        self.w_in[0].passed((n + 1) // 2 * 16)
        self.w_in[1].passed(n // 2 * 16)
        self.hi_ready.passed(n)
        self.lo_ready.passed(n)


def project_block(pg, ws, h_hi, h_lo, bank, n, slot, b):
    for k in range(KD):
        last = pg.split_matmul(bank[:, :TB], ws.hi[slot][:, k], ws.lo[slot][:, k],
                               h_hi[:, k, b * TB:(b + 1) * TB], h_lo[:, k, b * TB:(b + 1) * TB],
                               k == 0, k == KD - 1)
    last.then_inc(ws.psum_full.sem, 1)


def mixer_phases(pg):
    nc, dram = pg.nc, pg.dram
    with ExitStack() as keep:
        def sb_keep(name, shape, dt):
            return keep.enter_context(nc.sbuf_tensor(f"{name}_sb", shape, dt))
        h_hi = sb_keep("h_hi", [P, KD, T], F32R)
        h_lo = sb_keep("h_lo", [P, KD, T], F32R)
        stage = [sb_keep(f"z_stage{i}", [P, TB], F32) for i in range(2)]
        ws = WeightStream(pg, sb_keep, dram["w_in"], KD, "in")
        z = dram["z"]
        psum_full, psum_read = pg["psum_full"], pg["psum_read"]
        stored = [pg["z_stored_even"], pg["z_stored_odd"]]

        def store_index(pair, slot, b):
            return pair * 5 + (slot * NB + b) // 2

        def evacuate(act, n, pair, slot, b, bank, tile0):
            s = (slot + b) % 2
            act.wait_ge(psum_full.sem, psum_full.count(n * NB + (b + 1)))
            if (due := stored[s].count(store_index(pair, slot, b) * 16)) is not None:
                act.wait_ge(stored[s].sem, due)
            nc.scalar.activation(stage[s][:], bank[:, :TB], ACT.Copy).then_inc(psum_read.sem, 1)

        def store(sp, n, pair, slot, b, tile0):
            s = (slot + b) % 2
            sp.wait_ge(psum_read.sem, psum_read.count(n * NB + (b + 1)))
            sp.dma_start(z[one(n + tile0), :, b * TB:(b + 1) * TB].rearrange("o p t -> (o p) t"), stage[s][:]
                         ).then_inc(stored[s].sem, 16)

        def stores_passed(n):
            stored[0].passed((n * NB + 1) // 2 * 16)
            stored[1].passed(n * NB // 2 * 16)
            psum_full.passed(n * NB)
            psum_read.passed(n * NB)
            ws.passed(n)

        with ExitStack() as own, nc.Block() as block:
            def sb(name, shape, dt):
                return own.enter_context(nc.sbuf_tensor(f"{name}_sb", shape, dt))
            norm = norm_blocks(pg, sb, dram["xT"], dram["norm_mix_pre"], h_hi, h_lo, "pre")

            def first_bank(b, tile):
                return pg.bank[b if tile == 0 else 5 + b % 2]

            def first_evacuate(act, b):
                for tile in range(2):
                    step = 2 * b + tile
                    act.wait_ge(psum_full.sem, psum_full.count(step + 1))
                    if (due := stored[tile].count(b * 16)) is not None:
                        act.wait_ge(stored[tile].sem, due)
                    nc.scalar.activation(stage[tile][:], first_bank(b, tile)[:, :TB], ACT.Copy).then_inc(psum_read.sem, 1)

            def first_store(sp, b):
                for tile in range(2):
                    step = 2 * b + tile
                    sp.wait_ge(psum_read.sem, psum_read.count(step + 1))
                    sp.dma_start(z[tile, :, b * TB:(b + 1) * TB], stage[tile][:]).then_inc(stored[tile].sem, 16)

            @block.sync
            def _(sp):
                norm.sync(sp, 0)
                ws.load(sp, 0, 0, 0)
                ws.load(sp, 1, 0, 1)
                norm.sync(sp, 1)
                for b in range(NB):
                    if b + 2 < NB:
                        norm.sync(sp, b + 2)
                    first_store(sp, b)
                    if b < 2:
                        ws.load(sp, b + 2, 1, b)

                def body(n, pair, slot):
                    for b in range(NB):
                        store(sp, n, pair, slot, b, 0)
                    if not isinstance(n, int) or n + 2 < N_MIX:
                        ws.load(sp, n + 2, pair + 1, slot)
                later_pairs_ahead(sp, N_MIX, body)

            @block.scalar
            def _(act):
                norm.square(act, 0)
                ws.split_hi(act, 0, 0, 0)
                ws.split_hi(act, 1, 0, 1)
                norm.root(act, 0)
                for b in range(NB):
                    if b + 1 < NB:
                        norm.square(act, b + 1)
                    norm.high(act, b)
                    if b + 1 < NB:
                        norm.root(act, b + 1)
                    if b > 0:
                        first_evacuate(act, b - 1)
                ws.split_hi(act, 2, 1, 0, used=2 * NB - 1)
                first_evacuate(act, NB - 1)
                ws.split_hi(act, 3, 1, 1, used=2 * NB)

                def body(n, pair, slot):
                    for b in range(NB):
                        evacuate(act, n, pair, slot, b, pg.bank[b], 0)
                    if not isinstance(n, int) or n + 2 < N_MIX:
                        ws.split_hi(act, n + 2, pair + 1, slot)
                later_pairs_ahead(act, N_MIX, body)

            @block.gpsimd
            def _(pool):
                for b in range(NB):
                    norm.add(pool, b)

            @block.vector
            def _(dve):
                norm.constants(dve)
                ws.split_lo(dve, 0, 0, 0)
                ws.split_lo(dve, 1, 0, 1)
                norm.vector(dve)
                later_pairs(dve, N_MIX, lambda n, pair, slot: ws.split_lo(dve, n, pair, slot))

            @block.tensor
            def _(pe):
                def weights(n):
                    pe.wait_ge(ws.hi_ready.sem, ws.hi_ready.count(n + 1))
                    pe.wait_ge(ws.lo_ready.sem, ws.lo_ready.count(n + 1))

                norm.sum_rows(pe, 0)
                weights(1)
                for b in range(NB):
                    if b + 1 < NB:
                        norm.sum_rows(pe, b + 1)
                    norm.ready(pe, b)
                    for tile in range(2):
                        if (due := psum_read.count(2 * (b - 1))) is not None and tile == 1:
                            pe.wait_ge(psum_read.sem, due)
                        project_block(pg, ws, h_hi, h_lo, first_bank(b, tile), tile, tile, b)

                def body(n, pair, slot):
                    weights(n)
                    for b in range(NB):
                        pe.wait_ge(psum_read.sem, psum_read.count((n - 1) * NB + (b + 1)))
                        project_block(pg, ws, h_hi, h_lo, pg.bank[b], n, slot, b)
                later_pairs(pe, N_MIX, body)

            norm.done()
            stores_passed(N_MIX)
        attention_phase(pg, ws, h_hi, h_lo, evacuate, store, stores_passed)


def slope(head):
    return 2.0 ** (-8.0 / QH * (head + 1))


def attention_phase(pg, ws, h_hi, h_lo, evacuate, store, stores_passed):
    nc, dram = pg.nc, pg.dram
    z, o_all = dram["z"], dram["o"]
    HALF = DK
    S = pg
    with ExitStack() as own, nc.Block() as block:
        def sb(name, shape, dt=F32):
            return own.enter_context(nc.sbuf_tensor(f"{name}_sb", shape, dt))
        gla = sb("gla_z", [P, 13, P])
        swa = sb("swa_z", [P, 6, P])
        ident, ones = sb("ident", [P, P]), sb("ones_dv", [P, P])
        rel = sb("rel", [P, 2 * WIN])
        w_up, b_up, g_norm = sb("w_up", [P, 2, P]), sb("b_up", [P, 2]), sb("g_norm", [P, 1])
        minus_sink = sb("minus_sink", [P, 4, 2])
        keep, causal = sb("keep", [P, 2 * P]), sb("causal", [P, P])
        eps, key_scale = sb("eps_dv", [P, 1]), sb("key_scale", [P, P])
        a1, a2, a3, a4 = (sb(f"decay{i}", [P, 2 * P]) for i in range(4))
        e1, e2 = sb("exp_centred", [P, 2 * P]), sb("exp_start", [P, 2 * P])
        qz, qez = sb("q_centred", [P, 2, 2, P]), sb("q_start", [P, 2, 2, P])
        kt, kdz = sb("k_centred", [P, 2, P]), sb("k_end_turned", [P, 2, 2, P])
        v_tok, att = sb("v_tokens", [P, 4, P]), sb("att", [P, 4, P])
        state = [sb(f"state{i}", [P, 2, P]) for i in range(2)]
        rstd = sb("rstd_dv", [P, 4, P])
        kz, v_win = sb("k_window", [P, 2, 2 * WIN]), sb("v_window", [P, 2, P])
        p = sb("probs", [P, 4, 2 * WIN])
        p_t = sb("probs_turned", [P, 2, 4, P])
        o_win = sb("o_window", [P, 4, P])
        m, row, den, sink_e = (sb(x, [P, 2, 4]) for x in ("minus_max", "row_sum", "denominator", "sink_exp"))
        b_gemm, b_s, b_att, b_o, b_m, b_w = pg.bank[0:2], pg.bank[2:4], pg.bank[4], pg.bank[5], pg.bank[6], pg.bank[7]
        gate_v = att

        def chunks(ap):
            return ap.rearrange("p (c t) -> p c t", t=CH)

        loads = [(ident, dram["ident"]), (w_up, dram["w_gate_up"].rearrange("r (t c) -> r t c", t=2)),
                 (b_up, dram["b_gate"]), (g_norm, dram["gla_norm"]),
                 (minus_sink, dram["sinks"]), (keep, dram["scan_keep"]), (causal, dram["causal"]), (rel, dram["rel_first"])]

        @block.sync
        def _(sp):
            for tile, src in loads:
                sp.dma_start(tile[:], src).then_inc(S["att_const_in"].sem, 16)

            def load_gla(i):
                sp.dma_start(gla[:, 0:8], z[0:8, :, span(i, P)].rearrange("t p c -> p t c")).then_inc(S["gla_in"].sem, 16)
                sp.dma_start(gla[:, 12:], z[12:13, :, span(i, P)].rearrange("t p c -> p t c")).then_inc(S["gla_in"].sem, 16)

            def load_gates(i):
                sp.dma_start(gla[:, 8:12], z[8:12, :, span(i, P)].rearrange("t p c -> p t c")).then_inc(S["out_gate_in"].sem, 16)

            def load_window(i):
                sp.dma_start(swa[:], z[13:19, :, span(i, P)].rearrange("t p c -> p t c")).then_inc(S["swa_in"].sem, 16)

            def body(i, pair, slot):
                more = not isinstance(i, int) or i + 1 < NWIN
                if more:
                    sp.wait_ge(S["logits_full"].sem, S["logits_full"].count(i + 1))
                    sp.wait_ge(S["v_turned"].sem, S["v_turned"].count(i + 1))
                    sp.wait_ge(S["kt_ready"].sem, S["kt_ready"].count(i + 1))
                    sp.wait_ge(S["qez_ready"].sem, S["qez_ready"].count(i + 1))
                    sp.wait_ge(S["qz_ready"].sem, S["qz_ready"].count(i + 1))
                    sp.wait_ge(S["kd_turned"].sem, S["kd_turned"].count(i + 1))
                    load_gla(i + 1)
                store(sp, i, pair, slot, 0, N_MIX)
                store(sp, i, pair, slot, 1, N_MIX)
                if more:
                    sp.wait_ge(S["vb_turned"].sem, S["vb_turned"].count(i + 1))
                    sp.wait_ge(S["kz_ready"].sem, S["kz_ready"].count(i + 1))
                    sp.wait_ge(S["scores1_full"].sem, S["scores1_full"].count(i + 1))
                    load_window(i + 1)
                if isinstance(i, int) and i == 0:
                    sp.wait_ge(S["s1_ready"].sem, S["s1_ready"].count(1))
                    sp.dma_start(rel[:], dram["rel"]).then_inc(S["att_const_in"].sem, 16)
                store(sp, i, pair, slot, 2, N_MIX)
                store(sp, i, pair, slot, 3, N_MIX)
                sp.wait_ge(S["gla_out_ready"].sem, S["gla_out_ready"].count(i + 1))
                sp.dma_start(o_all[0:4, :, span(i, P)].rearrange("t p c -> p t c"), rstd[:]).then_inc(S["oa_stored"].sem, 16)
                if more:
                    sp.wait_ge(S["silu_ready"].sem, S["silu_ready"].count(i + 1))
                    load_gates(i + 1)
                store(sp, i, pair, slot, 4, N_MIX)
                if not isinstance(i, int) or i + 2 < NWIN:
                    ws.load(sp, i + 2, pair + 1, slot, i + 2 + N_MIX)
                sp.wait_ge(S["ow1_read"].sem, S["ow1_read"].count(i + 1))
                sp.dma_start(o_all[4:8, :, span(i, P)].rearrange("t p c -> p t c"), o_win[:]).then_inc(S["ob_stored"].sem, 16)
            load_gla(0)
            load_window(0)
            load_gates(0)
            ws.load(sp, 0, 0, 0, N_MIX)
            ws.load(sp, 1, 0, 1, N_MIX + 1)
            each_pair_ahead(sp, NWIN, body)
            sp.wait_ge(S["state_end"].sem, S["state_end"].count(NWIN))
            sp.dma_start(dram["gla_state_prompt"].rearrange("(t h) d v -> (h d) t v", t=2), state[0][:]
                         ).then_inc(S["state_stored"].sem, 16)
            sp.wait_ge(S["state_stored"].sem, S["state_stored"].count(16))
            sp.wait_ge(S["oa_stored"].sem, S["oa_stored"].count(NWIN * 16))
            sp.wait_ge(S["ob_stored"].sem, S["ob_stored"].count(NWIN * 16))

        @block.gpsimd
        def _(pool):
            for zeroed in (kz, v_win, qz, qez, kdz, att, state[0]):
                nc.gpsimd.memset(zeroed[:], 0.0).then_inc(S["zeroed"].sem, 1)
            nc.gpsimd.memset(ones[:], 1.0).then_inc(S["zeroed"].sem, 1)
            nc.gpsimd.memset(eps[:], EPS).then_inc(S["zeroed"].sem, 1)
            nc.gpsimd.memset(key_scale[:], HD ** -0.5).then_inc(S["zeroed"].sem, 1)
            pool.wait_ge(S["zeroed"].sem, S["zeroed"].count(10))

            def body(i):
                pool.wait_ge(S["zeroed"].sem, S["zeroed"].count(10))
                if (due := S["scores1_full"].count(i)) is not None:
                    pool.wait_ge(S["scores1_full"].sem, due)
                if (due := S["kz_ready"].count(i)) is not None:
                    pool.wait_ge(S["kz_ready"].sem, due)
                nc.gpsimd.tensor_copy(kz[:, :, 0:WIN], kz[:, :, WIN:2 * WIN]).then_inc(S["kz_shifted"].sem, 1)
                pool.wait_ge(S["kz_shifted"].sem, S["kz_shifted"].count(i + 1))
                pool.wait_ge(S["swa_in"].sem, S["swa_in"].count((i + 1) * 16))
                nc.gpsimd.tensor_tensor(kz[0:HALF, 0, WIN:], swa[0:HALF, 4], key_scale[0:HALF], ALU.mult
                                        ).then_inc(S["kz_low_half"].sem, 1)
                pool.wait_ge(S["kz_low_half"].sem, S["kz_low_half"].count(i + 1))
                nc.gpsimd.tensor_tensor(kz[HALF:, 1, WIN:], swa[HALF:, 4], key_scale[HALF:], ALU.mult
                                        ).then_inc(S["kz_ready"].sem, 1)
                pool.wait_ge(S["zeroed"].sem, S["zeroed"].count(10))
                pool.wait_ge(S["kz_ready"].sem, S["kz_ready"].count(i + 1))
                if (due := S["ow1_full"].count(i)) is not None:
                    pool.wait_ge(S["ow1_full"].sem, due)
                if (due := S["vb_ready"].count(i)) is not None:
                    pool.wait_ge(S["vb_ready"].sem, due)
                nc.gpsimd.tensor_copy(v_win[:, 0], v_win[:, 1]).then_inc(S["vb_shifted"].sem, 1)
                pool.wait_ge(S["ek_ready"].sem, S["ek_ready"].count(i + 1))
                pool.wait_ge(S["gla_in"].sem, S["gla_in"].count((i + 1) * 32))
                if (due := S["att_full"].count(i)) is not None:
                    pool.wait_ge(S["att_full"].sem, due)
                nc.gpsimd.tensor_tensor(kt[:], gla[:, 2:4], a4[:].rearrange("p (t c) -> p t c", t=2), ALU.mult
                                        ).then_inc(S["kt_ready"].sem, 1)
                pool.wait_ge(S["eo_ready"].sem, S["eo_ready"].count(i + 1))
                pool.wait_ge(S["kt_ready"].sem, S["kt_ready"].count(i + 1))
                nc.gpsimd.tensor_tensor(gla[:, 2:4], gla[:, 2:4], a1[:].rearrange("p (t c) -> p t c", t=2), ALU.mult
                                        ).then_inc(S["kd_ready"].sem, 1)
                pool.wait_ge(S["sigmoid_ready"].sem, S["sigmoid_ready"].count(i + 1))
                nc.gpsimd.tensor_tensor(gate_v[:], gla[:, 8:12], gate_v[:], ALU.mult).then_inc(S["silu_ready"].sem, 1)
            each(pool, NWIN, body)

        @block.scalar
        def _(act):
            copy = lambda out, in_, **kw: nc.scalar.activation(out, in_, ACT.Copy, **kw)

            def softmax(half, i):
                act.wait_ge(S[f"m{half}_ready"].sem, S[f"m{half}_ready"].count(i + 1))
                for j in range(4):
                    last = nc.scalar.activation(p[:, j], p[:, j], ACT.Exp, bias=m[:, half, j:j + 1],
                                                accum_out=row[:, half, j:j + 1])
                last.then_inc(S[f"exp{half}_ready"].sem, 1)
                act.wait_ge(S[f"sink{half}_ready"].sem, S[f"sink{half}_ready"].count(i + 1))
                nc.scalar.activation(sink_e[:, half], sink_e[:, half], ACT.Exp).then_inc(S[f"sinkexp{half}_ready"].sem, 1)

            def body(i, pair, slot):
                act.wait_ge(S["logits_full"].sem, S["logits_full"].count(i + 1))
                if (due := S["kd_ready"].count(i)) is not None:
                    act.wait_ge(S["kd_ready"].sem, due)
                for t in range(2):
                    last = nc.scalar.activation(a1[:, t * P:(t + 1) * P], b_att[:, t * P:(t + 1) * P], ACT.Abs, bias=b_up[:, t:t + 1])
                last.then_inc(S["abs_ready"].sem, 1)
                act.wait_ge(S["abs_ready"].sem, S["abs_ready"].count(i + 1))
                nc.scalar.activation(a1[:], a1[:], ACT.Exp, scale=-1.0).then_inc(S["abs_exp"].sem, 1)
                act.wait_ge(S["abs_exp"].sem, S["abs_exp"].count(i + 1))
                nc.scalar.activation(a1[:], a1[:], ACT.Ln, bias=1.0).then_inc(S["softplus_ready"].sem, 1)
                act.wait_ge(S["v_turned"].sem, S["v_turned"].count(i + 1))
                if (due := S["o_full"].count(i)) is not None:
                    act.wait_ge(S["o_full"].sem, due)
                copy(v_tok[:].rearrange("p h c -> p (h c)"), b_m[:]).then_inc(S["v_ready"].sem, 1)
                act.wait_ge(S["centred"].sem, S["centred"].count(i + 1))
                if (due := S["qz_ready"].count(i)) is not None:
                    act.wait_ge(S["qz_ready"].sem, due)
                nc.scalar.activation(e1[:], a4[:], ACT.Exp, scale=1.0 / TAU).then_inc(S["eq_ready"].sem, 1)
                act.wait_ge(S["eq_ready"].sem, S["eq_ready"].count(i + 1))
                nc.scalar.activation(a4[:], a4[:], ACT.Exp, scale=-1.0 / TAU).then_inc(S["ek_ready"].sem, 1)
                act.wait_ge(S["tail_ready"].sem, S["tail_ready"].count(i + 1))
                nc.scalar.activation(a1[:], a1[:], ACT.Exp, scale=1.0 / TAU).then_inc(S["eo_ready"].sem, 1)
                if (due := S["state_end"].count(i)) is not None:
                    act.wait_ge(S["state_end"].sem, due)
                nc.scalar.activation(e2[:], a3[:], ACT.Exp, scale=1.0 / TAU).then_inc(S["ei_ready"].sem, 1)
                act.wait_ge(S["vb_turned"].sem, S["vb_turned"].count(i + 1))
                act.wait_ge(S["vb_shifted"].sem, S["vb_shifted"].count(i + 1))
                copy(v_win[:, 1], b_w[:, 0:P]).then_inc(S["vb_ready"].sem, 1)
                act.wait_ge(S["kd_turned"].sem, S["kd_turned"].count(i + 1))
                if (due := S["u_full"].count(i)) is not None:
                    act.wait_ge(S["u_full"].sem, due)
                for c in range(2):
                    last = copy(kdz[c * HALF:(c + 1) * HALF, c].rearrange("p t c -> p (t c)"), b_m[c * HALF:(c + 1) * HALF, 2 * P:])
                last.then_inc(S["kd_ready_turned"].sem, 1)
                softmax(0, i)
                evacuate(act, i, pair, slot, 0, b_gemm[slot], N_MIX)
                if not isinstance(i, int) or 0 < i < NWIN - 1:
                    ws.split_hi(act, i + 1, pair + slot, 1 - slot)
                evacuate(act, i, pair, slot, 1, b_gemm[1 - slot], N_MIX)
                act.wait_ge(S["pt0_full"].sem, S["pt0_full"].count(i + 1))
                if (due := S["ow1_full"].count(i)) is not None:
                    act.wait_ge(S["ow1_full"].sem, due)
                copy(p_t[:, 0].rearrange("p h c -> p (h c)"), b_s[0][:]).then_inc(S["pt0_read_a"].sem, 1)
                softmax(1, i)
                evacuate(act, i, pair, slot, 2, b_gemm[slot], N_MIX)
                act.wait_ge(S["ow0_full"].sem, S["ow0_full"].count(i + 1))
                if (due := S["ob_stored"].count(i * 16)) is not None:
                    act.wait_ge(S["ob_stored"].sem, due)
                copy(o_win[:, 0:2].rearrange("p h c -> p (h c)"), b_w[:, 2 * P:]).then_inc(S["ow0_read"].sem, 1)
                if (due := S["oa_stored"].count(i * 16)) is not None:
                    act.wait_ge(S["oa_stored"].sem, due)
                act.wait_ge(S["o_full"].sem, S["o_full"].count(i + 1))
                if (due := S["gla_out_ready"].count(i)) is not None:
                    act.wait_ge(S["gla_out_ready"].sem, due)
                nc.scalar.activation(rstd[:].rearrange("p h c -> p (h c)"), b_o[:], ACT.Square).then_inc(S["o_squared"].sem, 1)
                act.wait_ge(S["out_gate_in"].sem, S["out_gate_in"].count((i + 1) * 16))
                nc.scalar.activation(gate_v[:], gla[:, 8:12], ACT.Exp, scale=-1.0).then_inc(S["gate_exp"].sem, 1)
                evacuate(act, i, pair, slot, 3, b_gemm[1 - slot], N_MIX)
                act.wait_ge(S["sums_full"].sem, S["sums_full"].count(i + 1))
                flat = rstd[:].rearrange("p h c -> p (h c)")
                nc.scalar.activation(flat, b_att[:], ACT.Ln, scale=1.0 / DV, bias=eps[:]).then_inc(S["log_ms"].sem, 1)
                act.wait_ge(S["log_ms"].sem, S["log_ms"].count(i + 1))
                nc.scalar.activation(flat, flat, ACT.Exp, scale=-0.5).then_inc(S["rstd_ready"].sem, 1)
                act.wait_ge(S["pt1_full"].sem, S["pt1_full"].count(i + 1))
                act.wait_ge(S["ow0_full"].sem, S["ow0_full"].count(i + 1))
                copy(p_t[:, 0].rearrange("p h c -> p (h c)"), b_s[0][:]).then_inc(S["pt1_read_a"].sem, 1)
                evacuate(act, i, pair, slot, 4, b_gemm[slot], N_MIX)
                act.wait_ge(S["ow1_full"].sem, S["ow1_full"].count(i + 1))
                copy(o_win[:, 2:4].rearrange("p h c -> p (h c)"), b_w[:, 2 * P:]).then_inc(S["ow1_read"].sem, 1)
            nc.scalar.preload_act_table_set("natural_log_exp_and_others")
            act.wait_ge(S["att_const_in"].sem, S["att_const_in"].count(16 * len(loads)))
            act.wait_ge(S["zeroed"].sem, S["zeroed"].count(10))
            ws.split_hi(act, 0, 0, 0)
            ws.split_hi(act, 1, 0, 1)
            each_pair_ahead(act, NWIN, body)

        @block.vector
        def _(dve):
            v = nc.vector

            def logits(half, i):
                dve.wait_ge(S[f"scores{half}_full"].sem, S[f"scores{half}_full"].count(i + 1))
                if (due := S["pt1_full" if half == 0 else "pt0_full"].count(i if half == 0 else i + 1)) is not None:
                    dve.wait_ge(S["pt1_full" if half == 0 else "pt0_full"].sem, due)
                for t in range(2):
                    for kv in range(2):
                        last = v.scalar_tensor_tensor(p[:, 2 * t + kv], rel[:], slope(kv * 4 + 2 * half + t),
                                                      b_s[t][:, kv * 256:(kv + 1) * 256], ALU.mult, ALU.add)
                last.then_inc(S[f"s{half}_ready"].sem, 1)
                dve.wait_ge(S[f"s{half}_ready"].sem, S[f"s{half}_ready"].count(i + 1))
                v.tensor_reduce(m[:, half], p[:], AX.X, ALU.max, negate=True).then_inc(S[f"max{half}_ready"].sem, 1)
                dve.wait_ge(S[f"max{half}_ready"].sem, S[f"max{half}_ready"].count(i + 1))
                sink = minus_sink[:, 2 * half:2 * half + 2].rearrange("p t k -> p (t k)")
                v.tensor_tensor(m[:, half], m[:, half], sink, ALU.min).then_inc(S[f"m{half}_ready"].sem, 1)
                dve.wait_ge(S[f"m{half}_ready"].sem, S[f"m{half}_ready"].count(i + 1))
                v.tensor_tensor(sink_e[:, half], m[:, half], sink, ALU.subtract).then_inc(S[f"sink{half}_ready"].sem, 1)

            def normalise(half, i):
                dve.wait_ge(S[f"exp{half}_ready"].sem, S[f"exp{half}_ready"].count(i + 1))
                dve.wait_ge(S[f"sinkexp{half}_ready"].sem, S[f"sinkexp{half}_ready"].count(i + 1))
                v.tensor_tensor(den[:, half], row[:, half], sink_e[:, half], ALU.add).then_inc(S[f"den{half}_ready"].sem, 1)
                dve.wait_ge(S[f"den{half}_ready"].sem, S[f"den{half}_ready"].count(i + 1))
                v.reciprocal(den[:, half], den[:, half]).then_inc(S[f"inv{half}_ready"].sem, 1)
                dve.wait_ge(S[f"inv{half}_ready"].sem, S[f"inv{half}_ready"].count(i + 1))
                for j in range(4):
                    last = v.tensor_scalar(p[:, j], p[:, j], den[:, half, j:j + 1], None, ALU.mult)
                last.then_inc(S[f"p{half}_ready"].sem, 1)

            def body(i, pair, slot):
                if isinstance(i, int) and i == 1:
                    dve.wait_ge(S["att_const_in"].sem, S["att_const_in"].count(16 * (len(loads) + 1)))
                dve.wait_ge(S["abs_ready"].sem, S["abs_ready"].count(i + 1))
                for t in range(2):
                    last = v.tensor_scalar(a2[:, t * P:(t + 1) * P], b_att[:, t * P:(t + 1) * P], b_up[:, t:t + 1], 0.0, ALU.add, ALU.min)
                last.then_inc(S["lm_ready"].sem, 1)
                dve.wait_ge(S["softplus_ready"].sem, S["softplus_ready"].count(i + 1))
                dve.wait_ge(S["lm_ready"].sem, S["lm_ready"].count(i + 1))
                v.tensor_tensor(a2[:], a2[:], a1[:], ALU.subtract).then_inc(S["log_a_ready"].sem, 1)
                dve.wait_ge(S["log_a_ready"].sem, S["log_a_ready"].count(i + 1))
                if (due := S["ei_ready"].count(i)) is not None:
                    dve.wait_ge(S["ei_ready"].sem, due)
                v.tensor_tensor_scan(a3[:], keep[:], a2[:], 0.0, ALU.mult, ALU.add).then_inc(S["b_ready"].sem, 1)
                dve.wait_ge(S["b_ready"].sem, S["b_ready"].count(i + 1))
                if (due := S["kt_ready"].count(i)) is not None:
                    dve.wait_ge(S["kt_ready"].sem, due)
                b = chunks(a3[:])
                v.tensor_tensor(chunks(a4[:]), b, b[:, :, CH // 2 - 1:CH // 2].to_broadcast([P, 4, CH]), ALU.subtract
                                ).then_inc(S["shifted"].sem, 1)
                v.tensor_tensor(chunks(a1[:]), b[:, :, CH - 1:CH].to_broadcast([P, 4, CH]), b, ALU.subtract
                                ).then_inc(S["tail_ready"].sem, 1)
                dve.wait_ge(S["shifted"].sem, S["shifted"].count(i + 1))
                v.tensor_scalar(a4[:], a4[:], 80.0 * TAU, -80.0 * TAU, ALU.min, ALU.max).then_inc(S["centred"].sem, 1)
                dve.wait_ge(S["eq_ready"].sem, S["eq_ready"].count(i + 1))
                dve.wait_ge(S["gla_in"].sem, S["gla_in"].count((i + 1) * 32))
                if (due := S["att_full"].count(i)) is not None:
                    dve.wait_ge(S["att_full"].sem, due)
                for t, e in ((0, e1),):
                    for hh in range(2):
                        rows = slice(hh * HALF, (hh + 1) * HALF)
                        last = v.scalar_tensor_tensor(qz[rows, :, hh], gla[rows, 0:2], DK ** -0.5,
                                                      e[rows].rearrange("p (t c) -> p t c", t=2), ALU.mult, ALU.mult)
                last.then_inc(S["qz_ready"].sem, 1)
                dve.wait_ge(S["ei_ready"].sem, S["ei_ready"].count(i + 1))
                if (due := S["o_full"].count(i)) is not None:
                    dve.wait_ge(S["o_full"].sem, due)
                for hh in range(2):
                    rows = slice(hh * HALF, (hh + 1) * HALF)
                    last = v.scalar_tensor_tensor(qez[rows, :, hh], gla[rows, 0:2], DK ** -0.5,
                                                  e2[rows].rearrange("p (t c) -> p t c", t=2), ALU.mult, ALU.mult)
                last.then_inc(S["qez_ready"].sem, 1)
                logits(0, i)
                dve.wait_ge(S["att_const_in"].sem, S["att_const_in"].count(16 * len(loads)))
                dve.wait_ge(S["att_full"].sem, S["att_full"].count(i + 1))
                if (due := S["gla_out_ready"].count(i)) is not None:
                    dve.wait_ge(S["gla_out_ready"].sem, due)
                dve.wait_ge(S["att_cleared"].sem, S["att_cleared"].count(i + 1))
                for hh in range(4):
                    last = v.copy_predicated(att[:, hh], causal[:].bitcast(I32), b_att[:, hh * P:(hh + 1) * P])
                last.then_inc(S["att_ready"].sem, 1)
                normalise(0, i)
                if not isinstance(i, int) or 0 < i < NWIN - 1:
                    ws.split_lo(dve, i + 1, pair + slot, 1 - slot)
                dve.wait_ge(S["pt0_full"].sem, S["pt0_full"].count(i + 1))
                if (due := S["ow1_full"].count(i)) is not None:
                    dve.wait_ge(S["ow1_full"].sem, due)
                v.tensor_copy(p_t[:, 1].rearrange("p h c -> p (h c)"), b_s[1][:]).then_inc(S["pt0_read_b"].sem, 1)
                dve.wait_ge(S["u_full"].sem, S["u_full"].count(i + 1))
                for c in range(2):
                    if c == 0:
                        if (due := S["o_full"].count(i)) is not None:
                            dve.wait_ge(S["o_full"].sem, due)
                    else:
                        dve.wait_ge(S["inter0_done"].sem, S["inter0_done"].count(i + 1))
                        dve.wait_ge(S["state_mid"].sem, S["state_mid"].count(i + 1))
                    for t in range(2):
                        at = t * P + c * CH + CH - 1
                        last = v.scalar_tensor_tensor(state[1 - c][:, t], state[c][:, t], e2[:, at:at + 1],
                                                      b_m[:, (2 * c + t) * P:(2 * c + t + 1) * P], ALU.mult, ALU.add)
                    last.then_inc(S["state_end" if c else "state_mid"].sem, 1)
                logits(1, i)
                normalise(1, i)
                dve.wait_ge(S["gate_exp"].sem, S["gate_exp"].count(i + 1))
                v.tensor_scalar(gate_v[:], gate_v[:], 1.0, None, ALU.add).then_inc(S["gate_den"].sem, 1)
                dve.wait_ge(S["gate_den"].sem, S["gate_den"].count(i + 1))
                v.reciprocal(gate_v[:], gate_v[:]).then_inc(S["sigmoid_ready"].sem, 1)
                dve.wait_ge(S["pt1_full"].sem, S["pt1_full"].count(i + 1))
                dve.wait_ge(S["ow0_full"].sem, S["ow0_full"].count(i + 1))
                v.tensor_copy(p_t[:, 1].rearrange("p h c -> p (h c)"), b_s[1][:]).then_inc(S["pt1_read_b"].sem, 1)
                dve.wait_ge(S["rstd_ready"].sem, S["rstd_ready"].count(i + 1))
                flat = rstd[:].rearrange("p h c -> p (h c)")
                v.scalar_tensor_tensor(flat, b_o[:], g_norm[:, 0:1], flat, ALU.mult, ALU.mult).then_inc(S["o_normed"].sem, 1)
                dve.wait_ge(S["silu_ready"].sem, S["silu_ready"].count(i + 1))
                dve.wait_ge(S["o_normed"].sem, S["o_normed"].count(i + 1))
                v.tensor_tensor(rstd[:], rstd[:], gate_v[:], ALU.mult).then_inc(S["gla_out_ready"].sem, 1)
                dve.wait_ge(S["gla_out_ready"].sem, S["gla_out_ready"].count(i + 1))
                v.memset(att[:], 0.0).then_inc(S["att_cleared"].sem, 1)
            dve.wait_ge(S["att_const_in"].sem, S["att_const_in"].count(16 * len(loads)))
            dve.wait_ge(S["zeroed"].sem, S["zeroed"].count(9))
            v.memset(att[:], 0.0).then_inc(S["att_cleared"].sem, 1)
            v.tensor_scalar(minus_sink[:], minus_sink[:], -1.0, None, ALU.mult).then_inc(S["sink_negated"].sem, 1)
            dve.wait_ge(S["sink_negated"].sem, S["sink_negated"].count(1))
            ws.split_lo(dve, 0, 0, 0)
            ws.split_lo(dve, 1, 0, 1)
            each_pair_ahead(dve, NWIN, body)

        @block.tensor
        def _(pe):
            mm = nc.tensor.matmul

            def gemm(i, pair, slot, b):
                if b == 0:
                    pe.wait_ge(ws.hi_ready.sem, ws.hi_ready.count(i + 1))
                    pe.wait_ge(ws.lo_ready.sem, ws.lo_ready.count(i + 1))
                if (due := S["psum_read"].count(i * NB + (b - 1))) is not None:
                    pe.wait_ge(S["psum_read"].sem, due)
                project_block(pg, ws, h_hi, h_lo, b_gemm[(slot + b) % 2], i, slot, b)

            def scores(half, i):
                for t in range(2):
                    last = mm(b_s[t][:], swa[:, 2 * half + t], kz[:].rearrange("p k c -> p (k c)"), start=True, stop=True)
                last.then_inc(S[f"scores{half}_full"].sem, 1)

            def turn_p(half, i):
                pe.wait_ge(S[f"p{half}_ready"].sem, S[f"p{half}_ready"].count(i + 1))
                for pc in range(2):
                    for j in range(4):
                        last = nc.tensor.transpose(b_s[pc][:, j * P:(j + 1) * P], p[:, j, pc * WIN:(pc + 1) * WIN], ident[:])
                last.then_inc(S[f"pt{half}_full"].sem, 1)

            def window_out(half, i):
                pe.wait_ge(S[f"pt{half}_read_a"].sem, S[f"pt{half}_read_a"].count(i + 1))
                pe.wait_ge(S[f"pt{half}_read_b"].sem, S[f"pt{half}_read_b"].count(i + 1))
                for t in range(2):
                    for kv in range(2):
                        rows = slice(kv * HALF, (kv + 1) * HALF)
                        for pc in range(2):
                            last = mm(b_w[rows, (2 + t) * P:(3 + t) * P], v_win[:, pc, rows], p_t[:, pc, 2 * t + kv],
                                      start=(pc == 0), stop=(pc == 1))
                last.then_inc(S[f"ow{half}_full"].sem, 1)

            def body(i, pair, slot):
                pe.wait_ge(S["gla_in"].sem, S["gla_in"].count((i + 1) * 32))
                if (due := S["log_ms"].count(i)) is not None:
                    pe.wait_ge(S["log_ms"].sem, due)
                for t in range(2):
                    last = mm(b_att[:, t * P:(t + 1) * P], w_up[:, t], gla[:, 12], start=True, stop=True)
                last.then_inc(S["logits_full"].sem, 1)
                if (due := S["state_end"].count(i)) is not None:
                    pe.wait_ge(S["state_end"].sem, due)
                for hh in range(4):
                    last = nc.tensor.transpose(b_m[:, hh * P:(hh + 1) * P], gla[:, 4 + hh], ident[:])
                last.then_inc(S["v_turned"].sem, 1)
                pe.wait_ge(S["swa_in"].sem, S["swa_in"].count((i + 1) * 16))
                if (due := S["ow1_read"].count(i)) is not None:
                    pe.wait_ge(S["ow1_read"].sem, due)
                nc.tensor.transpose(b_w[:, 0:P], swa[:, 5], ident[:]).then_inc(S["vb_turned"].sem, 1)
                pe.wait_ge(S["kz_ready"].sem, S["kz_ready"].count(i + 1))
                if (due := S["pt1_read_a"].count(i)) is not None:
                    pe.wait_ge(S["pt1_read_a"].sem, due)
                if (due := S["pt1_read_b"].count(i)) is not None:
                    pe.wait_ge(S["pt1_read_b"].sem, due)
                scores(0, i)
                pe.wait_ge(S["kt_ready"].sem, S["kt_ready"].count(i + 1))
                pe.wait_ge(S["qz_ready"].sem, S["qz_ready"].count(i + 1))
                pe.wait_ge(S["abs_ready"].sem, S["abs_ready"].count(i + 1))
                pe.wait_ge(S["lm_ready"].sem, S["lm_ready"].count(i + 1))
                for t in range(2):
                    last = mm(b_att[:, t * 2 * P:(t + 1) * 2 * P], kt[:, t], qz[:, t].rearrange("p h c -> p (h c)"), start=True, stop=True)
                last.then_inc(S["att_full"].sem, 1)
                pe.wait_ge(S["kd_ready"].sem, S["kd_ready"].count(i + 1))
                pe.wait_ge(S["v_ready"].sem, S["v_ready"].count(i + 1))
                for t in range(2):
                    last = nc.tensor.transpose(b_m[:, (2 + t) * P:(3 + t) * P], gla[:, 2 + t], ident[:])
                last.then_inc(S["kd_turned"].sem, 1)
                gemm(i, pair, slot, 0)
                gemm(i, pair, slot, 1)
                turn_p(0, i)
                pe.wait_ge(S["kd_ready_turned"].sem, S["kd_ready_turned"].count(i + 1))
                for c in range(2):
                    for t in range(2):
                        for hh in range(2):
                            rows = slice(hh * HALF, (hh + 1) * HALF)
                            last = mm(b_m[rows, (2 * c + t) * P:(2 * c + t + 1) * P], kdz[:, c, t, rows], v_tok[:, 2 * t + hh],
                                      start=True, stop=True)
                last.then_inc(S["u_full"].sem, 1)
                pe.wait_ge(S["att_ready"].sem, S["att_ready"].count(i + 1))
                if (due := S["gla_out_ready"].count(i)) is not None:
                    pe.wait_ge(S["gla_out_ready"].sem, due)
                for hh in range(4):
                    mm(b_o[:, hh * P:(hh + 1) * P], v_tok[:, hh], att[:, hh], start=(hh == 0), stop=False, skip_group_check=True)
                pe.wait_ge(S["qez_ready"].sem, S["qez_ready"].count(i + 1))
                for c in range(2):
                    if c == 1:
                        pe.wait_ge(S["pt0_read_a"].sem, S["pt0_read_a"].count(i + 1))
                        pe.wait_ge(S["pt0_read_b"].sem, S["pt0_read_b"].count(i + 1))
                        scores(1, i)
                        gemm(i, pair, slot, 2)
                        window_out(0, i)
                    state_before = S["state_mid" if c else "state_end"]
                    if (due := state_before.count(i + c)) is not None:
                        pe.wait_ge(state_before.sem, due)
                    for t in range(2):
                        out = b_o[:].rearrange("p (t h c) -> p t h c", t=2, h=2)[:, t, :, c * CH:(c + 1) * CH]
                        last = mm(out, state[c][:, t], qez[:, t, :, c * CH:(c + 1) * CH],
                                  start=False, stop=(c == 1 and t == 1), skip_group_check=True)
                    last.then_inc(S["o_full" if c else "inter0_done"].sem, 1)
                gemm(i, pair, slot, 3)
                pe.wait_ge(S["o_squared"].sem, S["o_squared"].count(i + 1))
                mm(b_att[:], ones[:], rstd[:].rearrange("p h c -> p (h c)"), start=True, stop=True).then_inc(S["sums_full"].sem, 1)
                turn_p(1, i)
                gemm(i, pair, slot, 4)
                pe.wait_ge(S["ow0_read"].sem, S["ow0_read"].count(i + 1))
                window_out(1, i)
            pe.wait_ge(S["att_const_in"].sem, S["att_const_in"].count(16 * len(loads)))
            pe.wait_ge(S["zeroed"].sem, S["zeroed"].count(9))
            each_pair_ahead(pe, NWIN, body)

        stores_passed(NWIN)
        for name in STEP_SIGNALS:
            S[name].passed(NWIN)
        S["sink_negated"].passed(1)


def sample_phase(pg):
    nc, dram = pg.nc, pg.dram
    z, o_all = dram["z"], dram["o"]
    S = pg
    HALF = DK
    L2 = 2 * NS
    with ExitStack() as own, nc.Block() as block:
        def sb(name, shape, dt=F32):
            return own.enter_context(nc.sbuf_tensor(f"{name}_smp", shape, dt))
        gla, swa = sb("gla", [P, 13, NS]), sb("swa", [P, 6, NS])
        ident, ones, eps = sb("ident", [P, P]), sb("ones", [P, P]), sb("eps", [P, 1])
        w_up, b_up, g_norm = sb("w_up", [P, 2, P]), sb("b_up", [P, 2]), sb("g_norm", [P, 1])
        keep, causal, own_rows = sb("keep", [P, L2]), sb("causal", [NS, NS]), sb("own_rows", [NS, NSEQ])
        bias, minus_sink = sb("bias", [P, 2, WIN + NS]), sb("minus_sink", [P, 1])
        state_in, state_out = sb("state_in", [P, 2, NSEQ, P]), sb("state_out", [P, 2, NSEQ, P])
        k_cache, v_cache = sb("k_cache", [P, NSEQ, WIN]), sb("v_cache", [P, NSEQ, P])
        a1, a2, a3, a4, e1, e2 = (sb(f"decay{i}", [P, L2]) for i in range(6))
        qz, qez = sb("q_centred", [P, 2, 2, NS]), sb("q_start", [P, 2, 2, NS])
        kt, kd, kdz = sb("k_centred", [P, 2, NS]), sb("k_end", [P, 2, NS]), sb("k_end_turned", [P, NSEQ, 2, P])
        v_tok, att, kv_tok = sb("v_tokens", [P, 4, P]), sb("att", [P, 4, NS]), sb("kv_tokens", [P, 2, P])
        sq, gate, o_out = sb("o_squared", [P, 4, NS]), sb("gate", [P, 4, NS]), sb("o_out", [P, 4, NS])
        qw, p = sb("q_window", [P, NSEQ, 2, 4, SLEN]), sb("probs", [P, 2, WIN + NS])
        pt_cache, pt_new = sb("probs_cache_turned", [P, 2, P]), sb("probs_new_turned", [P, 2, P])
        m, row, den, sink_e = (sb(x, [P, 2]) for x in ("minus_max", "row_sum", "denominator", "sink_exp"))
        o_win = sb("o_window", [P, 4, NSEQ, SLEN])
        bank = pg.bank
        zeroed = (qz, qez, kdz, v_tok, att, kv_tok, qw, pt_new)

        def chunks(ap):
            return ap.rearrange("p (c t) -> p c t", t=SLEN)

        def pair(ap):
            return ap.rearrange("p (t c) -> p t c", t=2)

        tokens = slice(SEQ, T)
        loads = [(gla[:], z[0:13, :, tokens].rearrange("t p c -> p t c")),
                 (swa[:], z[13:19, :, tokens].rearrange("t p c -> p t c")),
                 (ident[:], dram["ident"]), (w_up[:], dram["w_gate_up"].rearrange("r (t c) -> r t c", t=2)),
                 (b_up[:], dram["b_gate"]), (g_norm[:], dram["gla_norm"]), (keep[:], dram["sample_keep"]),
                 (causal[:], dram["sample_causal"]), (own_rows[:], dram["sample_rows"]), (bias[:], dram["sample_bias"]),
                 (minus_sink[:], dram["sample_sinks"]), (k_cache[:], dram["k_cacheT"]),
                 (v_cache[:], dram["v_cache"].rearrange("s k c -> k s c"))]
        loads += [(state_in[:, t], dram["state_gla"][:, 2 * t:2 * t + 2].rearrange("s h d v -> (h d) s v")) for t in range(2)]

        @block.sync
        def _(sp):
            for tile, src in loads:
                sp.dma_start(tile, src).then_inc(S["smp_in"].sem, 16)
            out = [(dram["swa_k_sample"][:, 0:WIN - SLEN], dram["k_cache"][:, SLEN:]),
                   (dram["swa_v_sample"][:, 0:WIN - SLEN], dram["v_cache"][:, SLEN:]),
                   (dram["swa_k_promptT"], z[Z_KB, :, SEQ - WIN:SEQ]), (dram["swa_v_promptT"], z[Z_VB, :, SEQ - WIN:SEQ])]
            for dst, src in out:
                sp.dma_start(dst, src).then_inc(S["smp_out"].sem, 16)
            sp.wait_ge(S["kv_tok_ready"].sem, S["kv_tok_ready"].count(1))
            for i, name in enumerate(("swa_k_sample", "swa_v_sample")):
                for s in range(NSEQ):
                    sp.dma_start(dram[name][s, WIN - SLEN:], kv_tok[s * SLEN:(s + 1) * SLEN, i]).then_inc(S["smp_out"].sem, 16)
            sp.wait_ge(S["state_out_ready"].sem, S["state_out_ready"].count(1))
            for t in range(2):
                sp.dma_start(dram["gla_state_sample"][:, 2 * t:2 * t + 2].rearrange("s h d v -> (h d) s v"), state_out[:, t]
                             ).then_inc(S["smp_out"].sem, 16)
            sp.wait_ge(S["o_win_ready"].sem, S["o_win_ready"].count(1))
            sp.dma_start(o_all[4:8, :, tokens].rearrange("t p c -> p t c"), o_win[:].rearrange("p t s c -> p t (s c)")
                         ).then_inc(S["smp_out"].sem, 16)
            sp.wait_ge(S["o_out_ready"].sem, S["o_out_ready"].count(1))
            sp.dma_start(o_all[0:4, :, tokens].rearrange("t p c -> p t c"), o_out[:]).then_inc(S["smp_out"].sem, 16)
            sp.wait_ge(S["smp_out"].sem, S["smp_out"].count(16 * (len(out) + 2 * NSEQ + 4)))

        @block.gpsimd
        def _(pool):
            for tile in zeroed:
                nc.gpsimd.memset(tile[:], 0.0).then_inc(S["smp_set"].sem, 1)
            nc.gpsimd.memset(ones[:], 1.0).then_inc(S["smp_set"].sem, 1)
            nc.gpsimd.memset(eps[:], EPS).then_inc(S["smp_set"].sem, 1)

        @block.scalar
        def _(act):
            copy = lambda out, in_: nc.scalar.activation(out, in_, ACT.Copy)
            act.wait_ge(S["smp_in"].sem, S["smp_in"].count(16 * len(loads)))
            act.wait_ge(S["smp_set"].sem, S["smp_set"].count(len(zeroed) + 2))
            act.wait_ge(S["logits_full"].sem, S["logits_full"].count(1))
            for t in range(2):
                last = nc.scalar.activation(a1[:, t * NS:(t + 1) * NS], bank[5][:, t * NS:(t + 1) * NS], ACT.Abs, bias=b_up[:, t:t + 1])
            last.then_inc(S["abs_ready"].sem, 1)
            act.wait_ge(S["abs_ready"].sem, S["abs_ready"].count(1))
            nc.scalar.activation(a1[:], a1[:], ACT.Exp, scale=-1.0).then_inc(S["abs_exp"].sem, 1)
            act.wait_ge(S["abs_exp"].sem, S["abs_exp"].count(1))
            nc.scalar.activation(a1[:], a1[:], ACT.Ln, bias=1.0).then_inc(S["softplus_ready"].sem, 1)
            act.wait_ge(S["v_turned"].sem, S["v_turned"].count(1))
            copy(v_tok[0:NS].rearrange("p h c -> p (h c)"), bank[6][0:NS]).then_inc(S["v_ready"].sem, 1)
            copy(kv_tok[0:NS].rearrange("p h c -> p (h c)"), bank[7][0:NS, 0:2 * P]).then_inc(S["kv_tok_ready"].sem, 1)
            act.wait_ge(S["centred"].sem, S["centred"].count(1))
            act.wait_ge(S["tail_ready"].sem, S["tail_ready"].count(1))
            nc.scalar.activation(e1[:], a4[:], ACT.Exp, scale=1.0 / TAU).then_inc(S["eq_ready"].sem, 1)
            act.wait_ge(S["eq_ready"].sem, S["eq_ready"].count(1))
            nc.scalar.activation(a4[:], a4[:], ACT.Exp, scale=-1.0 / TAU).then_inc(S["ek_ready"].sem, 1)
            nc.scalar.activation(a1[:], a1[:], ACT.Exp, scale=1.0 / TAU).then_inc(S["eo_ready"].sem, 1)
            nc.scalar.activation(e2[:], a3[:], ACT.Exp, scale=1.0 / TAU).then_inc(S["ei_ready"].sem, 1)
            act.wait_ge(S["m0_ready"].sem, S["m0_ready"].count(1))
            for g in range(2):
                last = nc.scalar.activation(p[:, g], p[:, g], ACT.Exp, bias=m[:, g:g + 1], accum_out=row[:, g:g + 1])
            last.then_inc(S["exp0_ready"].sem, 1)
            act.wait_ge(S["sink0_ready"].sem, S["sink0_ready"].count(1))
            nc.scalar.activation(sink_e[:], sink_e[:], ACT.Exp).then_inc(S["sinkexp0_ready"].sem, 1)
            act.wait_ge(S["o_full"].sem, S["o_full"].count(1))
            flat = sq[:].rearrange("p h c -> p (h c)")
            nc.scalar.activation(flat, bank[5][:, 0:4 * NS], ACT.Square).then_inc(S["o_squared"].sem, 1)
            nc.scalar.activation(gate[:], gla[:, 8:12], ACT.Exp, scale=-1.0).then_inc(S["gate_exp"].sem, 1)
            act.wait_ge(S["sums_full"].sem, S["sums_full"].count(1))
            nc.scalar.activation(flat, bank[4][:, 0:4 * NS], ACT.Ln, scale=1.0 / DV, bias=eps[:]).then_inc(S["log_ms"].sem, 1)
            act.wait_ge(S["log_ms"].sem, S["log_ms"].count(1))
            nc.scalar.activation(flat, flat, ACT.Exp, scale=-0.5).then_inc(S["rstd_ready"].sem, 1)
            act.wait_ge(S["ow0_full"].sem, S["ow0_full"].count(1))
            for kv in range(2):
                rows = slice(kv * HALF, (kv + 1) * HALF)
                for t in range(4):
                    src = bank[7][rows, 256:512].rearrange("p (s k t c) -> p k t s c", s=NSEQ, k=2, t=4)[:, kv, t]
                    last = copy(o_win[rows, t], src)
            last.then_inc(S["o_win_ready"].sem, 1)

        @block.vector
        def _(dve):
            v = nc.vector
            dve.wait_ge(S["smp_in"].sem, S["smp_in"].count(16 * len(loads)))
            dve.wait_ge(S["smp_set"].sem, S["smp_set"].count(len(zeroed) + 2))
            v.tensor_scalar(minus_sink[:], minus_sink[:], -1.0, None, ALU.mult).then_inc(S["sink_negated"].sem, 1)
            for kv in range(2):
                rows = slice(kv * HALF, (kv + 1) * HALF)
                for t in range(4):
                    last = v.tensor_scalar(qw[rows, :, kv, t], swa[rows, t].rearrange("p (s c) -> p s c", c=SLEN), HD ** -0.5, None, ALU.mult)
            last.then_inc(S["qw_ready"].sem, 1)
            dve.wait_ge(S["abs_ready"].sem, S["abs_ready"].count(1))
            for t in range(2):
                last = v.tensor_scalar(a2[:, t * NS:(t + 1) * NS], bank[5][:, t * NS:(t + 1) * NS], b_up[:, t:t + 1], 0.0, ALU.add, ALU.min)
            last.then_inc(S["lm_ready"].sem, 1)
            dve.wait_ge(S["softplus_ready"].sem, S["softplus_ready"].count(1))
            dve.wait_ge(S["lm_ready"].sem, S["lm_ready"].count(1))
            v.tensor_tensor(a2[:], a2[:], a1[:], ALU.subtract).then_inc(S["log_a_ready"].sem, 1)
            dve.wait_ge(S["log_a_ready"].sem, S["log_a_ready"].count(1))
            v.tensor_tensor_scan(a3[:], keep[:], a2[:], 0.0, ALU.mult, ALU.add).then_inc(S["b_ready"].sem, 1)
            dve.wait_ge(S["b_ready"].sem, S["b_ready"].count(1))
            b = chunks(a3[:])
            n = L2 // SLEN
            v.tensor_tensor(chunks(a4[:]), b, b[:, :, SLEN // 2 - 1:SLEN // 2].to_broadcast([P, n, SLEN]), ALU.subtract).then_inc(S["shifted"].sem, 1)
            v.tensor_tensor(chunks(a1[:]), b[:, :, SLEN - 1:].to_broadcast([P, n, SLEN]), b, ALU.subtract).then_inc(S["tail_ready"].sem, 1)
            dve.wait_ge(S["shifted"].sem, S["shifted"].count(1))
            v.tensor_scalar(a4[:], a4[:], 80.0 * TAU, -80.0 * TAU, ALU.min, ALU.max).then_inc(S["centred"].sem, 1)
            dve.wait_ge(S["ei_ready"].sem, S["ei_ready"].count(1))
            v.tensor_tensor(kt[:], gla[:, 2:4], pair(a4[:]), ALU.mult).then_inc(S["kt_ready"].sem, 1)
            v.tensor_tensor(kd[:], gla[:, 2:4], pair(a1[:]), ALU.mult).then_inc(S["kd_ready"].sem, 1)
            for out, e, name in ((qz, e1, "qz_ready"), (qez, e2, "qez_ready")):
                for hh in range(2):
                    rows = slice(hh * HALF, (hh + 1) * HALF)
                    last = v.scalar_tensor_tensor(out[rows, :, hh], gla[rows, 0:2], DK ** -0.5, pair(e[rows]), ALU.mult, ALU.mult)
                last.then_inc(S[name].sem, 1)
            dve.wait_ge(S["scores0_full"].sem, S["scores0_full"].count(1))
            for g in range(2):
                last = v.tensor_tensor(p[:, g], bank[g][:, 0:WIN + NS], bias[:, g], ALU.add)
            last.then_inc(S["s0_ready"].sem, 1)
            dve.wait_ge(S["s0_ready"].sem, S["s0_ready"].count(1))
            v.tensor_reduce(m[:], p[:], AX.X, ALU.max, negate=True).then_inc(S["max0_ready"].sem, 1)
            dve.wait_ge(S["max0_ready"].sem, S["max0_ready"].count(1))
            dve.wait_ge(S["sink_negated"].sem, S["sink_negated"].count(1))
            v.tensor_scalar(m[:], m[:], minus_sink[:, 0:1], None, ALU.min).then_inc(S["m0_ready"].sem, 1)
            dve.wait_ge(S["m0_ready"].sem, S["m0_ready"].count(1))
            v.tensor_scalar(sink_e[:], m[:], minus_sink[:, 0:1], None, ALU.subtract).then_inc(S["sink0_ready"].sem, 1)
            dve.wait_ge(S["att_full"].sem, S["att_full"].count(1))
            for hh in range(4):
                last = v.copy_predicated(att[0:NS, hh], causal[:].bitcast(I32), bank[4][0:NS, hh * NS:(hh + 1) * NS])
            last.then_inc(S["att_ready"].sem, 1)
            dve.wait_ge(S["kd_turned"].sem, S["kd_turned"].count(1))
            for s in range(NSEQ):
                last = v.tensor_scalar(kdz[0:NS, s].rearrange("p t c -> p (t c)"), bank[6][0:NS, 0:2 * P], own_rows[:, s:s + 1], None, ALU.mult)
            last.then_inc(S["kd_ready_turned"].sem, 1)
            dve.wait_ge(S["exp0_ready"].sem, S["exp0_ready"].count(1))
            dve.wait_ge(S["sinkexp0_ready"].sem, S["sinkexp0_ready"].count(1))
            v.tensor_tensor(den[:], row[:], sink_e[:], ALU.add).then_inc(S["den0_ready"].sem, 1)
            dve.wait_ge(S["den0_ready"].sem, S["den0_ready"].count(1))
            v.reciprocal(den[:], den[:]).then_inc(S["inv0_ready"].sem, 1)
            dve.wait_ge(S["inv0_ready"].sem, S["inv0_ready"].count(1))
            for g in range(2):
                last = v.tensor_scalar(p[:, g], p[:, g], den[:, g:g + 1], None, ALU.mult)
            last.then_inc(S["p0_ready"].sem, 1)
            dve.wait_ge(S["pt0_full"].sem, S["pt0_full"].count(1))
            v.tensor_copy(pt_cache[:].rearrange("p g c -> p (g c)"), bank[7][:, 0:2 * P]).then_inc(S["pt0_read_a"].sem, 1)
            v.tensor_copy(pt_new[0:NS].rearrange("p g c -> p (g c)"), bank[7][0:NS, 2 * P:]).then_inc(S["pt0_read_b"].sem, 1)
            dve.wait_ge(S["u_full"].sem, S["u_full"].count(1))
            for s in range(NSEQ):
                for t in range(2):
                    at = t * NS + s * SLEN + SLEN - 1
                    last = v.scalar_tensor_tensor(state_out[:, t, s], state_in[:, t, s], e2[:, at:at + 1],
                                                  bank[s // 2][:, (s % 2) * 2 * P + t * P:(s % 2) * 2 * P + (t + 1) * P], ALU.mult, ALU.add)
            last.then_inc(S["state_out_ready"].sem, 1)
            dve.wait_ge(S["gate_exp"].sem, S["gate_exp"].count(1))
            v.tensor_scalar(gate[:], gate[:], 1.0, None, ALU.add).then_inc(S["gate_den"].sem, 1)
            dve.wait_ge(S["gate_den"].sem, S["gate_den"].count(1))
            v.reciprocal(gate[:], gate[:]).then_inc(S["sigmoid_ready"].sem, 1)
            dve.wait_ge(S["sigmoid_ready"].sem, S["sigmoid_ready"].count(1))
            v.tensor_tensor(gate[:], gate[:], gla[:, 8:12], ALU.mult).then_inc(S["silu_ready"].sem, 1)
            dve.wait_ge(S["rstd_ready"].sem, S["rstd_ready"].count(1))
            v.scalar_tensor_tensor(o_out[:].rearrange("p h c -> p (h c)"), bank[5][:, 0:4 * NS], g_norm[:, 0:1],
                                   sq[:].rearrange("p h c -> p (h c)"), ALU.mult, ALU.mult).then_inc(S["o_normed"].sem, 1)
            dve.wait_ge(S["o_normed"].sem, S["o_normed"].count(1))
            dve.wait_ge(S["silu_ready"].sem, S["silu_ready"].count(1))
            v.tensor_tensor(o_out[:], o_out[:], gate[:], ALU.mult).then_inc(S["o_out_ready"].sem, 1)

        @block.tensor
        def _(pe):
            mm = nc.tensor.matmul
            pe.wait_ge(S["smp_in"].sem, S["smp_in"].count(16 * len(loads)))
            pe.wait_ge(S["smp_set"].sem, S["smp_set"].count(len(zeroed) + 2))
            for t in range(2):
                last = mm(bank[5][:, t * NS:(t + 1) * NS], w_up[:, t], gla[:, 12], start=True, stop=True)
            last.then_inc(S["logits_full"].sem, 1)
            for hh in range(4):
                nc.tensor.transpose(bank[6][0:NS, hh * P:(hh + 1) * P], gla[:, 4 + hh], ident[:])
            for i in range(2):
                last = nc.tensor.transpose(bank[7][0:NS, i * P:(i + 1) * P], swa[:, 4 + i], ident[:])
            last.then_inc(S["v_turned"].sem, 1)
            pe.wait_ge(S["qw_ready"].sem, S["qw_ready"].count(1))
            for s in range(NSEQ):
                q = qw[:, s].rearrange("p k t c -> p (k t c)")
                rows = slice(32 * (s % 4), 32 * (s % 4) + 32)
                mm(bank[s // 4][rows, 0:WIN], q, k_cache[:, s], start=True, stop=True, tile_position=(0, 32 * (s % 4)))
                last = mm(bank[s // 4][rows, WIN:WIN + NS], q, swa[:, 4], start=True, stop=True, tile_position=(0, 32 * (s % 4)))
            last.then_inc(S["scores0_full"].sem, 1)
            pe.wait_ge(S["qez_ready"].sem, S["qez_ready"].count(1))
            for t in range(2):
                last = mm(bank[4][0:NS, t * 2 * NS:(t + 1) * 2 * NS], kt[:, t], qz[:, t].rearrange("p h c -> p (h c)"), start=True, stop=True)
            last.then_inc(S["att_full"].sem, 1)
            pe.wait_ge(S["v_ready"].sem, S["v_ready"].count(1))
            for t in range(2):
                last = nc.tensor.transpose(bank[6][0:NS, t * P:(t + 1) * P], kd[:, t], ident[:])
            last.then_inc(S["kd_turned"].sem, 1)
            pe.wait_ge(S["att_ready"].sem, S["att_ready"].count(1))
            pe.wait_ge(S["lm_ready"].sem, S["lm_ready"].count(1))
            for hh in range(4):
                mm(bank[5][:, hh * NS:(hh + 1) * NS], v_tok[:, hh], att[:, hh], start=(hh == 0), stop=False, skip_group_check=True)
            out = bank[5][:, 0:4 * NS].rearrange("p (t h c) -> p t h c", t=2, h=2)
            for s in range(NSEQ):
                for t in range(2):
                    cols = slice(s * SLEN, (s + 1) * SLEN)
                    last = mm(out[:, t, :, cols], state_in[:, t, s], qez[:, t, :, cols], start=False,
                              stop=(s == NSEQ - 1 and t == 1), skip_group_check=True)
            last.then_inc(S["o_full"].sem, 1)
            pe.wait_ge(S["kd_ready_turned"].sem, S["kd_ready_turned"].count(1))
            pe.wait_ge(S["s0_ready"].sem, S["s0_ready"].count(1))
            for s in range(NSEQ):
                for t in range(2):
                    for hh in range(2):
                        rows = slice(hh * HALF, (hh + 1) * HALF)
                        at = (s % 2) * 2 * P + t * P
                        last = mm(bank[s // 2][rows, at:at + P], kdz[:, s, t, rows], v_tok[:, 2 * t + hh], start=True, stop=True)
            last.then_inc(S["u_full"].sem, 1)
            pe.wait_ge(S["o_squared"].sem, S["o_squared"].count(1))
            mm(bank[4][:, 0:4 * NS], ones[:], sq[:].rearrange("p h c -> p (h c)"), start=True, stop=True).then_inc(S["sums_full"].sem, 1)
            pe.wait_ge(S["p0_ready"].sem, S["p0_ready"].count(1))
            pe.wait_ge(S["kv_tok_ready"].sem, S["kv_tok_ready"].count(1))
            for g in range(2):
                nc.tensor.transpose(bank[7][:, g * P:(g + 1) * P], p[:, g, 0:WIN], ident[:])
                last = nc.tensor.transpose(bank[7][0:NS, (2 + g) * P:(3 + g) * P], p[:, g, WIN:], ident[:])
            last.then_inc(S["pt0_full"].sem, 1)
            pe.wait_ge(S["pt0_read_a"].sem, S["pt0_read_a"].count(1))
            pe.wait_ge(S["pt0_read_b"].sem, S["pt0_read_b"].count(1))
            for s in range(NSEQ):
                cols = slice(32 * (s % 4), 32 * (s % 4) + 32)
                o = bank[7][:, 256 + 32 * s:256 + 32 * (s + 1)]
                mm(o, v_cache[:, s], pt_cache[:, s // 4, cols], start=True, stop=False)
                last = mm(o, kv_tok[:, 1], pt_new[:, s // 4, cols], start=False, stop=True)
            last.then_inc(S["ow0_full"].sem, 1)

        S["sums_full"].passed(1)


def merge_phase(pg):
    nc, dram = pg.nc, pg.dram
    S = pg
    z, merged = dram["z"], dram["merged"]
    NT = D // P
    with ExitStack() as own, nc.Block() as block:
        def sb(name, shape, dt=F32):
            return own.enter_context(nc.sbuf_tensor(f"{name}_mrg", shape, dt))
        ws = WeightStream(pg, sb, dram["w_branch"], 8, "mrg")
        o_raw, o_hi, o_lo = sb("o_raw", [P, 8, TB]), sb("o_hi", [P, 8, TB], F32R), sb("o_lo", [P, 8, TB], F32R)
        gates = [sb(f"gates{i}", [P, 2, TB]) for i in range(2)]
        part = [sb(f"part{i}", [P, 2, TB]) for i in range(2)]
        out = [sb(f"merged{i}", [P, TB]) for i in range(2)]
        gates_in, stored = [S["gates_in_even"], S["gates_in_odd"]], [S["merged_stored_even"], S["merged_stored_odd"]]

        def tokens(b):
            return slice(b * TB, (b + 1) * TB) if isinstance(b, int) else bass.ds(b * TB, TB)

        @block.sync
        def _(sp):
            def unit(b, n, tail):
                if n == 0:
                    if (due := S["o_lo_ready"].count(b)) is not None:
                        sp.wait_ge(S["o_lo_ready"].sem, due)
                    sp.dma_start(o_raw[:], dram["o"][:, :, tokens(b)].rearrange("t p c -> p t c")).then_inc(S["o_in"].sem, 16)
                if isinstance(b, int) and b == 0 and n == 0:
                    ws.load(sp, 0, 0, 0)
                    ws.load(sp, 1, 0, 1)
                if (due := S["parts_ready"].count(b * NT + (n - 1))) is not None:
                    sp.wait_ge(S["parts_ready"].sem, due)
                for i, tile in enumerate((Z_GATE_A, Z_GATE_B)):
                    sp.dma_start(gates[n % 2][:, i], z[tile + n, :, tokens(b)]).then_inc(gates_in[n % 2].sem, 16)
                if n >= 2 or not (isinstance(b, int) and b == 0):
                    back = b * NT + (n - 1)
                    if (due := S["merged_ready"].count(back)) is not None:
                        sp.wait_ge(S["merged_ready"].sem, due)
                    pb, pn = (b, n - 2) if n >= 2 else (b - 1, n + NT - 2)
                    sp.dma_start(merged[pn, :, tokens(pb)], out[n % 2][:]).then_inc(stored[n % 2].sem, 16)
                if not (tail and n >= NT - 2):
                    sp.wait_ge(ws.lo_ready.sem, ws.lo_ready.count(b * NT + (n + 1)))
                    sp.dma_start(ws.raw[n % 2][:], dram["w_branch"][(n + 2) % NT]).then_inc(ws.w_in[n % 2].sem, 16)
            each_last(sp, NB, lambda b, tail: [unit(b, n, tail) for n in range(NT)])
            for n in range(2):
                sp.wait_ge(S["merged_ready"].sem, S["merged_ready"].count(NB * NT - 1 + n))
                sp.dma_start(merged[NT - 2 + n, :, tokens(NB - 1)], out[n][:]).then_inc(stored[n].sem, 16)
            for n in range(2):
                sp.wait_ge(stored[n].sem, stored[n].count(NB * NT // 2 * 16))

        @block.scalar
        def _(act):
            def split(b, n):
                act.wait_ge(ws.w_in[n % 2].sem, ws.w_in[n % 2].count((b * (NT // 2) + n // 2 + 1) * 16))
                if (due := S["unit_done"].count(b * NT + (n - 1))) is not None:
                    act.wait_ge(S["unit_done"].sem, due)
                nc.scalar.activation(ws.hi[n % 2][:], ws.raw[n % 2][:], ACT.Copy).then_inc(ws.hi_ready.sem, 1)

            def unit(b, n, tail):
                if n == 0:
                    act.wait_ge(S["o_in"].sem, S["o_in"].count((b + 1) * 16))
                    for k in range(8):
                        last = nc.scalar.activation(o_hi[:, k], o_raw[:, k], ACT.Copy)
                        last.then_inc(S["o_hi_ready"].sem, 1)
                act.wait_ge(gates_in[n % 2].sem, gates_in[n % 2].count((b * (NT // 2) + n // 2 + 1) * 32))
                nc.scalar.activation(gates[n % 2][:], gates[n % 2][:], ACT.Sigmoid).then_inc(S["gates_ready"].sem, 1)
                act.wait_ge(S["unit_done"].sem, S["unit_done"].count(b * NT + (n + 1)))
                if not (tail and n >= NT - 2):
                    if n < NT - 2:
                        split(b, n + 2)
                    else:
                        split(b + 1, n + 2 - NT)
            split(0, 0)
            split(0, 1)
            each_last(act, NB, lambda b, tail: [unit(b, n, tail) for n in range(NT)])

        @block.vector
        def _(dve):
            v = nc.vector

            def split(b, n):
                dve.wait_ge(ws.hi_ready.sem, ws.hi_ready.count(b * NT + (n + 1)))
                v.tensor_tensor(ws.lo[n % 2][:], ws.raw[n % 2][:], ws.hi[n % 2][:].bitcast(F32), ALU.subtract).then_inc(ws.lo_ready.sem, 1)

            def unit(b, n, tail):
                if n == 0:
                    for k in range(8):
                        dve.wait_ge(S["o_hi_ready"].sem, S["o_hi_ready"].count(b * 8 + (k + 1)))
                        last = v.tensor_tensor(o_lo[:, k], o_raw[:, k], o_hi[:, k].bitcast(F32), ALU.subtract)
                    last.then_inc(S["o_lo_ready"].sem, 1)
                dve.wait_ge(S["unit_done"].sem, S["unit_done"].count(b * NT + (n + 1)))
                dve.wait_ge(S["gates_ready"].sem, S["gates_ready"].count(b * NT + (n + 1)))
                if (due := S["merged_ready"].count(b * NT + (n - 1))) is not None:
                    dve.wait_ge(S["merged_ready"].sem, due)
                for i in range(2):
                    last = v.tensor_tensor(part[n % 2][:, i], gates[n % 2][:, i], pg.bank[(n % 4) * 2 + i][:, :TB], ALU.mult)
                last.then_inc(S["parts_ready"].sem, 1)
                if not (tail and n >= NT - 2):
                    if n < NT - 2:
                        split(b, n + 2)
                    else:
                        split(b + 1, n + 2 - NT)
            split(0, 0)
            split(0, 1)
            each_last(dve, NB, lambda b, tail: [unit(b, n, tail) for n in range(NT)])

        @block.gpsimd
        def _(pool):
            def unit(b, n):
                pool.wait_ge(S["parts_ready"].sem, S["parts_ready"].count(b * NT + (n + 1)))
                if isinstance(b, int):
                    if (due := stored[n % 2].count((b * NT // 2 + n // 2) * 16)) is not None:
                        pool.wait_ge(stored[n % 2].sem, due)
                else:
                    if (due := stored[n % 2].count((b * (NT // 2) + n // 2) * 16)) is not None:
                        pool.wait_ge(stored[n % 2].sem, due)
                nc.gpsimd.tensor_tensor(out[n % 2][:], part[n % 2][:, 0], part[n % 2][:, 1], ALU.add).then_inc(S["merged_ready"].sem, 1)
            each(pool, NB, lambda b: [unit(b, n) for n in range(NT)])

        @block.tensor
        def _(pe):
            def unit(b, n):
                pe.wait_ge(ws.hi_ready.sem, ws.hi_ready.count(b * NT + (n + 1)))
                pe.wait_ge(ws.lo_ready.sem, ws.lo_ready.count(b * NT + (n + 1)))
                if n == 0:
                    pe.wait_ge(S["o_lo_ready"].sem, S["o_lo_ready"].count(b + 1))
                if (due := S["parts_ready"].count(b * NT + (n - 3))) is not None:
                    pe.wait_ge(S["parts_ready"].sem, due)
                for i in range(2):
                    for k in range(4):
                        kk = 4 * i + k
                        last = pg.split_matmul(pg.bank[(n % 4) * 2 + i][:, :TB], ws.hi[n % 2][:, kk], ws.lo[n % 2][:, kk],
                                               o_hi[:, kk], o_lo[:, kk], k == 0, k == 3)
                last.then_inc(S["unit_done"].sem, 1)
            each(pe, NB, lambda b: [unit(b, n) for n in range(NT)])

        ws.passed(NB * NT)
        S["unit_done"].passed(NB * NT)


def each_last(engine, n, body):
    body(0, n == 1)
    if n > 2:
        with engine.Fori(1, n - 1) as i:
            body(i, False)
    if n > 1:
        body(n - 1, True)


def project_out_phase(pg, tag, src, weights, nk, norm_w, residual, dst):
    nc, dram = pg.nc, pg.dram
    S = pg
    NT = D // P
    KK = nk // 2
    U = 2 * KK
    BANKS = ((1, 2, 3, 0), (4, 5, 6, 0))
    SUMS = pg.bank[7]
    NORM_AT = 1
    with ExitStack() as own, nc.Block() as block:
        def sb(name, shape, dt=F32):
            return own.enter_context(nc.sbuf_tensor(f"{name}_{tag}", shape, dt))
        ws = WeightStream(pg, sb, weights, 8, tag)
        raw = [sb(f"src_raw{i}", [P, 2, TB]) for i in range(2)]
        s_hi, s_lo = sb("src_hi", [P, nk, TB], F32R), sb("src_lo", [P, nk, TB], F32R)
        y, x = sb("y", [P, NT, TB]), sb("x", [P, NT, TB])
        yn = sb("y_normed", [P, NT, TB])
        sq = [sb(f"sq{i}", [P, TB]) for i in range(2)]
        acc, rstd = sb("acc", [P, TB]), sb("rstd", [P, TB])
        w, ones, eps = sb("norm_w", [P, NT]), sb("ones", [P, P]), sb("eps", [P, 1])
        src_in = [S["src_in_even"], S["src_in_odd"]]
        src_loads = [(KK + 1) // 2, KK // 2]

        def tokens(b):
            return slice(b * TB, (b + 1) * TB) if isinstance(b, int) else bass.ds(b * TB, TB)

        def first(b):
            return isinstance(b, int) and b == 0

        @block.sync
        def _(sp):
            sp.dma_start(w[:], norm_w).then_inc(S["const_in"].sem, 16)

            def load_src(b, kk):
                before = b * KK + (kk - 1) if kk >= 2 else b * KK - (KK - 1 - max(k for k in range(KK) if k % 2 == kk))
                if (due := S["src_lo_ready"].count(before)) is not None:
                    sp.wait_ge(S["src_lo_ready"].sem, due)
                sp.dma_start(raw[kk % 2][:], src[2 * kk:2 * kk + 2, :, tokens(b)].rearrange("t p c -> p t c")
                             ).then_inc(src_in[kk % 2].sem, 16)

            def load_w(b, un):
                if (due := ws.lo_ready.count(b * U + (un - 1))) is not None:
                    sp.wait_ge(ws.lo_ready.sem, due)
                sp.dma_start(ws.raw[un % 2][:], weights[un]).then_inc(ws.w_in[un % 2].sem, 16)

            def load_residual(b):
                if (due := S["y_stored"].count(b * 32)) is not None:
                    sp.wait_ge(S["y_stored"].sem, due)
                sp.dma_start(x[:], residual[:, :, tokens(b)].rearrange("k p t -> p k t")).then_inc(S["residual_in"].sem, 16)

            def store(b, half):
                sp.wait_ge(S["y_added"].sem, S["y_added"].count(b * 2 + (half + 1)))
                columns = slice(4 * half, 4 * half + 4)
                sp.dma_start(dst[columns, :, tokens(b)].rearrange("k p t -> p k t"), x[:, columns]).then_inc(S["y_stored"].sem, 16)

            def body(b, tail):
                for un in range(U):
                    if un + 2 < U:
                        load_w(b, un + 2)
                    elif not tail:
                        load_w(b + 1, un + 2 - U)
                    if un >= KK and not tail:
                        load_src(b + 1, un - KK)
                    if un == NORM_AT + 5 and not first(b):
                        for half in range(2):
                            store(b - 1, half)
                    if un == U - 1:
                        load_residual(b)
            for kk in range(KK):
                load_src(0, kk)
                if kk < 2:
                    load_w(0, kk)
            each_last(sp, NB, body)
            for half in range(2):
                store(NB - 1, half)
            sp.wait_ge(S["y_stored"].sem, S["y_stored"].count(NB * 32))

        @block.scalar
        def _(act):
            def copy(out, in_):
                return nc.scalar.activation(out, in_, ACT.Copy)

            def split_w(b, un):
                act.wait_ge(ws.w_in[un % 2].sem, ws.w_in[un % 2].count((b * KK + (un // 2 + 1)) * 16))
                copy(ws.hi[un % 2][:], ws.raw[un % 2][:]).then_inc(ws.hi_ready.sem, 1)

            def split_src(b, kk):
                act.wait_ge(src_in[kk % 2].sem, src_in[kk % 2].count((b * src_loads[kk % 2] + (kk // 2 + 1)) * 16))
                copy(s_hi[:, 2 * kk:2 * kk + 2], raw[kk % 2][:]).then_inc(S["src_hi_ready"].sem, 1)

            def evacuate(b, half, columns):
                for j in columns:
                    n = 4 * half + j
                    if j < 3:
                        act.wait_ge(S["column_full"].sem, S["column_full"].count(b * 6 + (half * 3 + j + 1)))
                    if not first(b):
                        act.wait_ge(S["y_normed"].sem, S["y_normed"].count(b * NT + (n + 1 - NT)))
                    if (due := S["squares_added"].count(b * NT + (n - 1))) is not None:
                        act.wait_ge(S["squares_added"].sem, due)
                    bank = pg.bank[BANKS[half][j]]
                    copy(y[:, n], bank[:, :TB])
                    nc.scalar.activation(sq[n % 2][:], bank[:, :TB], ACT.Square).then_inc(S["column_read"].sem, 1)

            def root(b):
                act.wait_ge(S["sums_full"].sem, S["sums_full"].count(b + 1))
                nc.scalar.activation(rstd[:], SUMS[:, :TB], ACT.Sqrt, bias=eps[:], scale=1.0 / D).then_inc(S["rooted"].sem, 1)

            def body(b, tail):
                for un in range(U):
                    if un == NORM_AT and not first(b):
                        root(b - 1)
                    if un in (KK - 1, U - 1):
                        evacuate(b, un // KK, range(3))
                    act.wait_ge(S["unit_done"].sem, S["unit_done"].count(b * U + (un + 1)))
                    if un in (KK - 1, U - 1):
                        evacuate(b, un // KK, (3,))
                    if un + 2 < U:
                        split_w(b, un + 2)
                    elif not tail:
                        split_w(b + 1, un + 2 - U)
                    if un >= KK and not tail:
                        split_src(b + 1, un - KK)
            act.wait_ge(S["const_set"].sem, S["const_set"].count(2))
            for kk in range(KK):
                split_src(0, kk)
                if kk < 2:
                    split_w(0, kk)
            each_last(act, NB, body)
            root(NB - 1)

        @block.vector
        def _(dve):
            v = nc.vector

            def split_w(b, un):
                dve.wait_ge(ws.hi_ready.sem, ws.hi_ready.count(b * U + (un + 1)))
                v.tensor_tensor(ws.lo[un % 2][:], ws.raw[un % 2][:], ws.hi[un % 2][:].bitcast(F32), ALU.subtract).then_inc(ws.lo_ready.sem, 1)

            def split_src(b, kk):
                dve.wait_ge(S["src_hi_ready"].sem, S["src_hi_ready"].count(b * KK + (kk + 1)))
                pair = slice(2 * kk, 2 * kk + 2)
                v.tensor_tensor(s_lo[:, pair], raw[kk % 2][:], s_hi[:, pair].bitcast(F32), ALU.subtract).then_inc(S["src_lo_ready"].sem, 1)

            def invert(b):
                dve.wait_ge(S["rooted"].sem, S["rooted"].count(b + 1))
                v.reciprocal(rstd[:], rstd[:]).then_inc(S["inverted"].sem, 1)

            def norm(b, half):
                dve.wait_ge(S["inverted"].sem, S["inverted"].count(b + 1))
                for n in range(4 * half, 4 * half + 4):
                    v.scalar_tensor_tensor(yn[:, n], y[:, n], w[:, n:n + 1], rstd[:], ALU.mult, ALU.mult).then_inc(S["y_normed"].sem, 1)

            def add(b, half):
                dve.wait_ge(S["residual_in"].sem, S["residual_in"].count((b + 1) * 16))
                dve.wait_ge(S["y_normed"].sem, S["y_normed"].count(b * NT + 4 * (half + 1)))
                columns = slice(4 * half, 4 * half + 4)
                v.tensor_tensor(x[:, columns], x[:, columns], yn[:, columns], ALU.add).then_inc(S["y_added"].sem, 1)

            norm_steps = (invert, lambda b: norm(b, 0), lambda b: norm(b, 1), lambda b: add(b, 0), lambda b: add(b, 1))

            def body(b, tail):
                for un in range(U):
                    if 0 <= un - NORM_AT < 5 and not first(b):
                        norm_steps[un - NORM_AT](b - 1)
                    if un + 2 < U:
                        split_w(b, un + 2)
                    elif not tail:
                        split_w(b + 1, un + 2 - U)
                    if un >= KK and not tail:
                        split_src(b + 1, un - KK)
            v.memset(ones[:], 1.0).then_inc(S["const_set"].sem, 1)
            v.memset(eps[:], EPS).then_inc(S["const_set"].sem, 1)
            dve.wait_ge(S["const_in"].sem, S["const_in"].count(16))
            for kk in range(KK):
                split_src(0, kk)
                if kk < 2:
                    split_w(0, kk)
            each_last(dve, NB, body)
            invert(NB - 1)
            for half in range(2):
                norm(NB - 1, half)
                add(NB - 1, half)

        @block.gpsimd
        def _(pool):
            g = nc.gpsimd

            def body(b):
                for n in range(NT):
                    pool.wait_ge(S["column_read"].sem, S["column_read"].count(b * NT + (n + 1)))
                    if n == 1:
                        if (due := S["sums_full"].count(b)) is not None:
                            pool.wait_ge(S["sums_full"].sem, due)
                        g.tensor_tensor(acc[:], sq[0][:], sq[1][:], ALU.add).then_inc(S["squares_added"].sem, 2)
                    elif n > 1:
                        if (due := S["squares_added"].count(b * NT + n)) is not None:
                            pool.wait_ge(S["squares_added"].sem, due)
                        g.tensor_tensor(acc[:], acc[:], sq[n % 2][:], ALU.add).then_inc(S["squares_added"].sem, 1)

            each(pool, NB, body)

        @block.tensor
        def _(pe):
            def sums(b):
                pe.wait_ge(S["squares_added"].sem, S["squares_added"].count((b + 1) * NT))
                if (due := S["rooted"].count(b)) is not None:
                    pe.wait_ge(S["rooted"].sem, due)
                nc.tensor.matmul(SUMS[:, :TB], ones[:], acc[:], start=True, stop=True).then_inc(S["sums_full"].sem, 1)

            def body(b):
                for half in range(2):
                    for kk in range(KK):
                        un = half * KK + kk
                        if un == NORM_AT and not first(b):
                            sums(b - 1)
                        pe.wait_ge(ws.hi_ready.sem, ws.hi_ready.count(b * U + (un + 1)))
                        pe.wait_ge(ws.lo_ready.sem, ws.lo_ready.count(b * U + (un + 1)))
                        if half == 0:
                            pe.wait_ge(S["src_lo_ready"].sem, S["src_lo_ready"].count(b * KK + (kk + 1)))
                        for j in range(4):
                            if kk == 0:
                                n = 4 * half + j
                                if (due := S["column_read"].count(b * NT + (n - 7 if j < 3 else (0, 4)[half]))) is not None:
                                    pe.wait_ge(S["column_read"].sem, due)
                            bank = pg.bank[BANKS[half][j]][:, :TB]
                            for k in range(2):
                                at = k * 4 + j
                                last = pg.split_matmul(bank, ws.hi[un % 2][:, at], ws.lo[un % 2][:, at], s_hi[:, 2 * kk + k], s_lo[:, 2 * kk + k],
                                                       kk == 0 and k == 0, kk == KK - 1 and k == 1)
                            if kk == KK - 1 and j < 3:
                                last.then_inc(S["column_full"].sem, 1)
                        last.then_inc(S["unit_done"].sem, 1)
            pe.wait_ge(S["const_set"].sem, S["const_set"].count(2))
            each(pe, NB, body)
            sums(NB - 1)

        ws.w_in[0].passed(NB * KK * 16)
        ws.w_in[1].passed(NB * KK * 16)
        ws.hi_ready.passed(NB * U)
        ws.lo_ready.passed(NB * U)
        S["unit_done"].passed(NB * U)
        for i in range(2):
            src_in[i].passed(NB * src_loads[i] * 16)
        for name, n in (("src_hi_ready", NB * KK), ("src_lo_ready", NB * KK), ("column_full", NB * 6), ("column_read", NB * NT),
                        ("squares_added", NB * NT), ("y_normed", NB * NT), ("y_added", NB * 2), ("rooted", NB), ("inverted", NB),
                        ("sums_full", NB), ("y_stored", NB * 32), ("residual_in", NB * 16), ("const_in", 16), ("const_set", 2)):
            S[name].passed(n)


def ffn_in_phase(pg):
    nc, dram = pg.nc, pg.dram
    S = pg
    LU = 2 + SEQ + NSEQ * (2 + SLEN)
    LC = LU - 2
    LAST = (NB - 1) * TB
    TAIL = SEQ - LAST
    U_BANKS, G_BANK0 = 2, 2
    with ExitStack() as own, nc.Block() as block:
        def sb(name, shape, dt=F32):
            return own.enter_context(nc.sbuf_tensor(f"{name}_ffn", shape, dt))
        h_hi, h_lo = sb("h_hi", [P, KD, T], F32R), sb("h_lo", [P, KD, T], F32R)
        ws = WeightStream(pg, sb, dram["w_ffn_in"], KD, "ffn")
        norm = norm_blocks(pg, sb, dram["x1"].rearrange("k p t -> (k p) t"), dram["norm_ffn_pre"], h_hi, h_lo, "ffn")
        up = norm.x[1][:].rearrange("p k t -> p (k t)")[:, 0:LU]
        conv = norm.x[0][:].rearrange("p k t -> p (k t)")[:, 0:LC]
        FIRST = (((0, 0), (1, 0)), ((0, 1), (1, 1)), ((1, 2),), ((1, 3), (0, 2)), ((0, 3), (0, 4), (1, 4)))
        first_order = [product for products in FIRST for product in products]
        U_READY = [first_order.index((0, b)) + 1 for b in range(NB)]
        weights_used = [max(first_order.index((tile, b)) for b in range(NB)) + 1 for tile in range(2)]
        smp = sb("act_sample", [P, NS])
        taps, states, kept = sb("taps", [P, KF, 4]), sb("states", [P, KF, NSEQ, 2]), sb("kept", [P, KF, 2 + 2 * NSEQ])
        stored = S["act_stored"]

        def sample_cols(ap, start, n, at):
            return ap[:, start:start + NSEQ * (2 + SLEN)].rearrange("p (s c) -> p s c", s=NSEQ)[:, :, at:at + n]

        def read_u(act, j, b, products):
            act.wait_ge(S["psum_full"].sem, S["psum_full"].count(products))
            src = pg.bank[b % U_BANKS]
            if b < NB - 1:
                nc.scalar.activation(up[:, 2 + b * TB:2 + (b + 1) * TB], src[:, :TB], ACT.Copy).then_inc(S["u_read"].sem, 1)
            else:
                smp_u = src[:, TAIL:TB].rearrange("p (s c) -> p s c", s=NSEQ)
                nc.scalar.activation(up[:, 2 + LAST:2 + SEQ], src[:, :TAIL], ACT.Copy)
                nc.scalar.activation(sample_cols(up, 2 + SEQ, SLEN, 2), smp_u, ACT.Copy)
                k = kept[:, one(j)].rearrange("p o c -> p (o c)")
                nc.scalar.activation(k[:, 0:2], src[:, TAIL - 2:TAIL], ACT.Copy)
                nc.scalar.activation(k[:, 2:].rearrange("p (s c) -> p s c", s=NSEQ), smp_u[:, :, SLEN - 2:], ACT.Copy
                                     ).then_inc(S["u_read"].sem, 1)

        @block.sync
        def _(sp):
            norm.sync(sp, 0)
            ws.load(sp, 0, 0, 0)
            ws.load(sp, 1, 0, 1)
            norm.sync(sp, 1)
            sp.dma_start(taps[:], dram["conv_taps"]).then_inc(S["ffn_const_in"].sem, 16)
            sp.dma_start(states[:], dram["conv_states"]).then_inc(S["ffn_const_in"].sem, 16)
            for b in range(2, NB):
                norm.sync(sp, b)

            def body(n, j, slot):
                if slot == 1:
                    sp.wait_ge(S["g_read"].sem, S["g_read"].count((j + 1) * NB))
                    a = dram["act"][one(j)].rearrange("o p t -> (o p) t")
                    sp.dma_start(a[:, 0:SEQ], conv[:, 0:SEQ]).then_inc(stored.sem, 16)
                    sp.dma_start(a[:, SEQ:T], smp[:]).then_inc(stored.sem, 16)
                if not isinstance(n, int) or n + 2 < 2 * KF:
                    ws.load(sp, n + 2, j + 1, slot)
            each_pair_ahead(sp, 2 * KF, body)
            sp.wait_ge(S["u_read"].sem, S["u_read"].count(KF * NB))
            sp.dma_start(dram["conv_kept"], kept[:]).then_inc(S["kept_stored"].sem, 16)
            sp.wait_ge(S["kept_stored"].sem, S["kept_stored"].count(16))
            sp.wait_ge(stored.sem, stored.count(KF * 32))

        @block.scalar
        def _(act):
            norm.square(act, 0)
            ws.split_hi(act, 0, 0, 0)
            ws.split_hi(act, 1, 0, 1)
            norm.root(act, 0)
            for b in range(NB):
                if b + 1 < NB:
                    norm.square(act, b + 1)
                norm.high(act, b)
                if b + 1 < NB:
                    norm.root(act, b + 1)
                if b == 3:
                    norm.used(act, 4)
                    for block_u in range(2):
                        read_u(act, 0, block_u, U_READY[block_u])
            for block_u in range(2, NB):
                read_u(act, 0, block_u, U_READY[block_u])
            ws.split_hi(act, 2, 1, 0, used=weights_used[0])

            def body(n, j, slot):
                if slot == 0:
                    act.wait_ge(S["conv_done"].sem, S["conv_done"].count(j))
                    for b in range(NB):
                        read_u(act, j, b, n * NB + (b + 1))
                else:
                    act.wait_ge(S["conv_done"].sem, S["conv_done"].count(j + 1))
                    nc.scalar.activation(conv[:, 0:SEQ], conv[:, 0:SEQ], ACT.Gelu_apprx_tanh)
                    if (due := stored.count(j * 32)) is not None:
                        act.wait_ge(stored.sem, due)
                    nc.scalar.activation(smp[:].rearrange("p (s c) -> p s c", s=NSEQ), sample_cols(conv, SEQ, SLEN, 2),
                                         ACT.Gelu_apprx_tanh).then_inc(S["gelu_done"].sem, 1)
                if not isinstance(n, int) or n + 2 < 2 * KF:
                    ws.split_hi(act, n + 2, j + 1, slot)
            body(1, 0, 1)
            later_pairs_ahead(act, 2 * KF, body)

        @block.vector
        def _(dve):
            v = nc.vector
            norm.constants(dve)
            ws.split_lo(dve, 0, 0, 0)
            ws.split_lo(dve, 1, 0, 1)
            norm.vector(dve)
            dve.wait_ge(S["ffn_const_in"].sem, S["ffn_const_in"].count(32))

            def body(n, j, slot):
                if slot == 0:
                    tap = lambda i: taps[:, one(j), i:i + 1].rearrange("p o c -> p (o c)")
                    dve.wait_ge(S["u_read"].sem, S["u_read"].count((j + 1) * NB))
                    dve.wait_ge(S["heads_set"].sem, S["heads_set"].count(j + 1))
                    if (due := stored.count(j * 32)) is not None:
                        dve.wait_ge(stored.sem, due)
                    v.tensor_scalar(conv, up[:, 2:], tap(2), tap(3), ALU.mult, ALU.add).then_inc(S["tap2_done"].sem, 1)
                    dve.wait_ge(S["tap2_done"].sem, S["tap2_done"].count(j + 1))
                    v.scalar_tensor_tensor(conv, up[:, 1:LU - 1], tap(1), conv, ALU.mult, ALU.add).then_inc(S["tap1_done"].sem, 1)
                    dve.wait_ge(S["tap1_done"].sem, S["tap1_done"].count(j + 1))
                    v.scalar_tensor_tensor(conv, up[:, 0:LU - 2], tap(0), conv, ALU.mult, ALU.add).then_inc(S["conv_done"].sem, 1)
                else:
                    dve.wait_ge(S["gelu_done"].sem, S["gelu_done"].count(j + 1))
                    for b in range(NB):
                        dve.wait_ge(S["psum_full"].sem, S["psum_full"].count(n * NB + (b + 1)))
                        g = pg.bank[G_BANK0 + b]
                        cols = slice(b * TB, min((b + 1) * TB, SEQ))
                        last = v.tensor_tensor(conv[:, cols], conv[:, cols], g[:, :cols.stop - cols.start], ALU.mult)
                        if b == NB - 1:
                            last = v.tensor_tensor(smp[:], smp[:], g[:, TAIL:TB], ALU.mult)
                        last.then_inc(S["g_read"].sem, 1)
                if not isinstance(n, int) or n + 2 < 2 * KF:
                    ws.split_lo(dve, n + 2, j + 1, slot)
            each_pair_ahead(dve, 2 * KF, body)

        @block.gpsimd
        def _(pool):
            for b in range(NB):
                norm.add(pool, b)
            pool.wait_ge(S["ffn_const_in"].sem, S["ffn_const_in"].count(32))
            norm.used(pool, 4)
            nc.gpsimd.memset(up[:, 0:2], 0.0).then_inc(S["u_front_zeroed"].sem, 1)
            pool.wait_ge(S["u_front_zeroed"].sem, S["u_front_zeroed"].count(1))

            def body(j):
                if (due := S["conv_done"].count(j)) is not None:
                    pool.wait_ge(S["conv_done"].sem, due)
                pool.wait_ge(S["u_front_zeroed"].sem, S["u_front_zeroed"].count(1))
                nc.gpsimd.tensor_copy(sample_cols(up, 2 + SEQ, 2, 0), states[:, one(j)].rearrange("p o s c -> p (o s) c")
                                      ).then_inc(S["heads_set"].sem, 1)
            each(pool, KF, body)

        @block.tensor
        def _(pe):
            norm.sum_rows(pe, 0)
            for n in range(2):
                pe.wait_ge(ws.hi_ready.sem, ws.hi_ready.count(n + 1))
                pe.wait_ge(ws.lo_ready.sem, ws.lo_ready.count(n + 1))
            for b in range(NB):
                if b + 1 < NB:
                    norm.sum_rows(pe, b + 1)
                norm.ready(pe, b)
                for tile, block_h in FIRST[b]:
                    if tile == 0 and (due := S["u_read"].count(block_h - 1)) is not None:
                        pe.wait_ge(S["u_read"].sem, due)
                    bank = pg.bank[G_BANK0 + block_h if tile else block_h % U_BANKS]
                    project_block(pg, ws, h_hi, h_lo, bank, tile, tile, block_h)

            def body(n, j, slot):
                pe.wait_ge(ws.hi_ready.sem, ws.hi_ready.count(n + 1))
                pe.wait_ge(ws.lo_ready.sem, ws.lo_ready.count(n + 1))
                for b in range(NB):
                    if slot == 0:
                        pe.wait_ge(S["u_read"].sem, S["u_read"].count(j * NB + (b - 1)))
                        bank = pg.bank[b % U_BANKS]
                    else:
                        pe.wait_ge(S["g_read"].sem, S["g_read"].count((j - 1) * NB + (b + 1)))
                        bank = pg.bank[G_BANK0 + b]
                    project_block(pg, ws, h_hi, h_lo, bank, n, slot, b)
            later_pairs(pe, 2 * KF, body)

        norm.done()
        ws.passed(2 * KF)


def build(nc, dram):
    with ExitStack() as ctx:
        pg = Program(nc, ctx, dram)
        mixer_phases(pg)
        sample_phase(pg)
        merge_phase(pg)
        project_out_phase(pg, "mix", dram["merged"], dram["w_out"], KD, dram["norm_mix_post"],
                          dram["xT"].rearrange("(k p) t -> k p t", p=P), dram["x1"])
        ffn_in_phase(pg)
        project_out_phase(pg, "out", dram["act"], dram["w_ffn_out"], KF, dram["norm_ffn_post"], dram["x1"], dram["yT"])


def tiles(w, columns):
    w = w[:, columns].reshape(w.shape[0] // P, P, len(columns) // P, P)
    return np.ascontiguousarray(w.transpose(2, 1, 0, 3))


def by_partition(v):
    return np.ascontiguousarray(v.reshape(-1, P).T)


def units(w):
    w = w.reshape(w.shape[0] // (2 * P), 2, P, 2, 4, P)
    return np.ascontiguousarray(w.transpose(3, 0, 2, 1, 4, 5)).reshape(-1, P, 8, P)


def sample_bias(slopes):
    s4, kv, t, tok, g, key = np.meshgrid(*[np.arange(n) for n in (4, KVH, 4, SLEN, 2, WIN + NS)], indexing="ij")
    new = key - WIN
    rel = np.where(key < WIN, tok + WIN - key, tok - new % SLEN)
    seen = (rel >= 0) & (rel < WIN) & ((key < WIN) | (new // SLEN == 4 * g + s4))
    return np.where(seen, -slopes[kv * 4 + t] * rel, NEG).astype(np.float32).reshape(P, 2, WIN + NS)


def host_arrays(a):
    w_in = a["w_in"][0]
    edges = np.cumsum([0, 256, 256, 512, RANK, 512, 512, 128, 128, D, D])
    qa, ka, va, r, ga, qb, kb, vb, gate_a, gate_b = (np.arange(x, y) for x, y in zip(edges[:-1], edges[1:]))
    head_rows = np.concatenate([np.r_[t * HD:(t + 1) * HD, (t + 4) * HD:(t + 5) * HD] for t in range(4)])
    columns = np.concatenate([qa, ka, va, ga, np.full(P, edges[-1]), qb[head_rows], kb, vb, gate_a, gate_b])
    columns[12 * P:12 * P + RANK] = r
    w_in = np.concatenate([w_in, np.zeros((D, 1), w_in.dtype)], axis=1)
    x = np.concatenate([a["x_prompt"][0], a["x_sample"].reshape(NS, D)], axis=0)
    w_up = np.zeros((P, H * DK), np.float32)
    w_up[:RANK] = a["w_gate_up"][0]
    head = np.arange(4)[:, None] + 4 * np.arange(2)[None, :]
    q, key = np.arange(WIN)[:, None] + WIN, np.arange(2 * WIN)[None, :]
    rel = np.where((q >= key) & (q - key < WIN), key - q, NEG).astype(np.float32)
    t = np.arange(P)
    out = {
        "xT": np.ascontiguousarray(x.T),
        "w_in": tiles(w_in, columns),
        "norm_mix_pre": by_partition(a["norm_mix_pre"]),
        "w_gate_up": w_up, "b_gate": by_partition(a["b_gate"]), "gla_norm": by_partition(a["gla_norm"]),
        "sinks": np.ascontiguousarray(np.broadcast_to(a["sinks"][0][head], (P, 4, 2))),
        "ident": np.eye(P, dtype=np.float32),
        "rel": rel, "rel_first": np.where(key < WIN, NEG, rel).astype(np.float32),
        "scan_keep": np.ascontiguousarray(np.broadcast_to((np.arange(2 * P) % CH != 0).astype(np.float32), (P, 2 * P))),
        "causal": ((t[:, None] // CH == t[None] // CH) & (t[:, None] <= t[None])).astype(np.float32),
    }
    s = np.arange(NS)
    w_ffn_in = a["w_ffn_in"][0]
    ffn_columns = np.concatenate([np.arange(j * P, (j + 1) * P) + half * FF for j in range(KF) for half in range(2)])
    taps = np.concatenate([a["conv_w"][0], a["conv_b"]], axis=0)
    caches = {n: a[f"cache_swa_{n}"][0].reshape(NSEQ, WIN, P) for n in ("k", "v")}
    out.update({
        "k_cache": np.ascontiguousarray(caches["k"]), "v_cache": np.ascontiguousarray(caches["v"]),
        "k_cacheT": np.ascontiguousarray(caches["k"].transpose(2, 0, 1)),
        "state_gla": np.ascontiguousarray(a["state_gla"][0]),
        "sample_keep": np.ascontiguousarray(np.broadcast_to((np.arange(2 * NS) % SLEN != 0).astype(np.float32), (P, 2 * NS))),
        "sample_causal": ((s[:, None] // SLEN == s[None] // SLEN) & (s[:, None] <= s[None])).astype(np.float32),
        "sample_rows": (s[:, None] // SLEN == np.arange(NSEQ)[None]).astype(np.float32),
        "sample_bias": sample_bias(np.array([slope(n) for n in range(QH)])),
        "sample_sinks": np.ascontiguousarray(np.tile(np.repeat(a["sinks"][0], SLEN), 4)[:, None]),
        "w_branch": np.concatenate([tiles(a["w_branch_a"][0], np.arange(D)),
                                    tiles(a["w_branch_b"][0][head_rows], np.arange(D))], axis=2),
        "w_out": units(a["w_out"][0]), "w_ffn_out": units(a["w_ffn_out"][0]),
        "w_ffn_in": tiles(w_ffn_in, ffn_columns),
        "norm_mix_post": by_partition(a["norm_mix_post"]), "norm_ffn_pre": by_partition(a["norm_ffn_pre"]),
        "norm_ffn_post": by_partition(a["norm_ffn_post"]),
        "conv_taps": np.ascontiguousarray(taps.reshape(4, KF, P).transpose(2, 1, 0)),
        "conv_states": np.ascontiguousarray(a["state_ffn_conv"][0].reshape(NSEQ, 2, KF, P).transpose(3, 2, 0, 1)),
    })
    return out


SCRATCH = {"z": (N_Z, P, T), "o": (8, P, T), "merged": (KD, P, T), "x1": (KD, P, T), "act": (KF, P, T)}
OUTPUTS = {"gla_state_prompt": (H, DK, DV), "yT": (KD, P, T), "gla_state_sample": (NSEQ, H, DK, DV),
           "swa_k_promptT": (P, WIN), "swa_v_promptT": (P, WIN),
           "swa_k_sample": (NSEQ, WIN, P), "swa_v_sample": (NSEQ, WIN, P), "conv_kept": (P, KF, 2 + 2 * NSEQ)}


def kernel(**inputs):
    import concourse.bacc as bacc
    from concourse.bass_utils import run_bass_kernel_spmd

    arrays = host_arrays({name: np.asarray(value) for name, value in inputs.items()})
    nc = bacc.Bacc("TRN2", target_bir_lowering=False, num_devices=1)
    dram = {name: nc.dram_tensor(name, a.shape, F32, kind="ExternalInput").ap() for name, a in arrays.items()}
    for name, shape in SCRATCH.items():
        dram[name] = nc.dram_tensor(name, shape, F32, kind="Internal").ap()
    for name, shape in OUTPUTS.items():
        dram[name] = nc.dram_tensor(name, shape, F32, kind="ExternalOutput").ap()
    build(nc, dram)
    out = run_bass_kernel_spmd(nc, [arrays], core_ids=[0]).results[0]

    y = np.asarray(out["yT"]).reshape(D, T).T
    kept = np.asarray(out["conv_kept"]).transpose(2, 1, 0).reshape(1 + NSEQ, 2, FF)
    windows = [np.ascontiguousarray(np.asarray(out[f"swa_{n}_promptT"]).T).reshape(1, 1, WIN, KVH, HD) for n in "kv"]
    caches = [np.asarray(out[f"swa_{n}_sample"]).reshape(1, NSEQ, WIN, KVH, HD) for n in "kv"]
    return (np.ascontiguousarray(y[:SEQ])[None], np.ascontiguousarray(y[SEQ:]).reshape(NSEQ, SLEN, D),
            np.asarray(out["gla_state_prompt"]).reshape(1, 1, H, DK, DV),
            np.asarray(out["gla_state_sample"]).reshape(1, NSEQ, H, DK, DV),
            *windows, *caches, kept[None, :1], kept[None, 1:])
```

```python
import math
from contextlib import ExitStack

import numpy as np

import concourse.bass as bass
from concourse import mybir

ALU = mybir.AluOpType
ACT = mybir.ActivationFunctionType
AX = mybir.AxisListType
F32 = mybir.dt.float32
F32R = mybir.dt.float32r
I32 = mybir.dt.int32

P = 128
D = 1024
SEQ = 2048
NSEQ, SLEN = 8, 4
NS = NSEQ * SLEN
T = SEQ + NS
NB = 5
TB = T // NB
KD = D // P
FF = 2816
KF = FF // P
H, DK, DV, RANK = 4, 64, 128, 16
CH = 64
WIN = 128
NWIN = SEQ // WIN
QH, KVH, HD = 8, 2, 64
EPS = 1e-6
TAU = 16.0
NEG = -1.0e30

Z_QA, Z_KA, Z_VA, Z_GA, Z_R, Z_QB, Z_KB, Z_VB, Z_GATE_A, Z_GATE_B = 0, 2, 4, 8, 12, 13, 17, 18, 19, 27
N_MIX = 19
N_Z = 35

STEP_SIGNALS = """
    abs_exp abs_ready att_full att_ready b_ready centred ei_ready ek_ready eo_ready eq_ready gate_den gate_exp kd_ready
    kd_ready_turned kd_turned kt_ready lm_ready log_a_ready log_ms logits_full o_full o_normed o_squared ow0_full pt0_full
    pt0_read_a pt0_read_b qez_ready qz_ready rstd_ready shifted sigmoid_ready silu_ready softplus_ready sums_full tail_ready
    u_full v_ready v_turned m0_ready exp0_ready sink0_ready sinkexp0_ready s0_ready max0_ready den0_ready inv0_ready p0_ready
    scores0_full
""".split()


class Signal:

    def __init__(self, nc, ctx, name):
        self.sem = ctx.enter_context(nc.semaphore(name))
        self.base = 0

    def count(self, n):
        return None if isinstance(n, int) and n <= 0 else n + self.base

    def passed(self, n):
        self.base += n


def later_pairs(engine, n, body):
    with engine.Fori(1, n // 2) as t:
        body(t * 2, t, 0)
        body(t * 2 + 1, t, 1)
    if n % 2:
        body(n - 1, n // 2, 0)


def later_pairs_ahead(engine, n, body):
    pairs = (n - 2) // 2
    with engine.Fori(1, pairs) as t:
        body(t * 2, t, 0)
        body(t * 2 + 1, t, 1)
    for i in range(pairs * 2, n):
        body(i, i // 2, i % 2)


def each_pair_ahead(engine, n, body):
    for i in range(2):
        body(i, 0, i)
    later_pairs_ahead(engine, n, body)


def each(engine, n, body):
    body(0)
    if n > 1:
        with engine.Fori(1, n) as i:
            body(i)


def one(i):
    return slice(i, i + 1) if isinstance(i, int) else bass.ds(i, 1)


def span(i, size):
    return slice(i * size, i * size + size) if isinstance(i, int) else bass.ds(i * size, size)


class Program:
    def __init__(self, nc, ctx, dram):
        self.nc, self.ctx, self.dram = nc, ctx, dram
        self.signals = {}
        self.bank = [ctx.enter_context(nc.psum_tensor(f"bank{i}", [P, 512], F32)) for i in range(8)]

    def __getitem__(self, name):
        if name not in self.signals:
            self.signals[name] = Signal(self.nc, self.ctx, name)
        return self.signals[name]

    def split_matmul(self, out, w_hi, w_lo, x_hi, x_lo, first, last):
        pe = self.nc.tensor
        pe.matmul(out, w_hi, x_hi, start=first, stop=False)
        pe.matmul(out, w_lo, x_hi, start=False, stop=False)
        return pe.matmul(out, w_hi, x_lo, start=False, stop=last)


class NormParts:

    def __init__(self, sync, square, add, sum_rows, root, high, constants, vector, low_last, ready, used, done, x):
        self.sync, self.square, self.add, self.sum_rows, self.root, self.high = sync, square, add, sum_rows, root, high
        self.constants, self.vector, self.ready, self.used, self.done, self.x = constants, vector, ready, used, done, x
        self.low_last = low_last
        self.h_hi = self.h_lo = None


def norm_blocks(pg, sb, src, norm_w, tag):
    nc = pg.nc
    PAIRS = KD // 2
    ADDS = KD - 1
    x = [sb(f"x{i}_{tag}", [P, KD, TB], F32) for i in range(2)]
    sq = [sb(f"sq{i}_{tag}", [P, 2, TB], F32) for i in range(2)]
    h = [sb(f"h{i}_{tag}", [P, 2, TB], F32) for i in range(2)]
    acc, rstd = sb(f"acc_{tag}", [P, TB], F32), sb(f"rstd_{tag}", [P, TB], F32)
    w = sb(f"normw_{tag}", [P, KD], F32)
    ones = sb(f"ones_{tag}", [P, P], F32)
    eps = sb(f"eps_{tag}", [P, 1], F32)
    sums = pg.bank[7]
    x_in = [[pg["x_in_even_first"], pg["x_in_even_last"]], [pg["x_in_odd_first"], pg["x_in_odd_last"]]]
    HALF = KD // 2
    const_in, const_set = pg["norm_w_in"], pg["norm_const_set"]
    squared, added, summed, rooted, inverted = pg["squared"], pg["added"], pg["summed"], pg["rooted"], pg["inverted"]
    h_full, h_hi_ready, h_lo_ready = pg["h_full"], pg["h_hi_ready"], pg["h_lo_ready"]
    h_lo_last_ready = pg["h_lo_last_ready"]
    xT = src.rearrange("(k p) t -> p k t", p=P)

    def of(t, b, p):
        return t[:, 2 * p:2 * p + 2, b * TB:(b + 1) * TB]

    def sync(sp, b):
        if b == 0:
            sp.dma_start(w[:], norm_w).then_inc(const_in.sem, 16)
        for half in range(2):
            if (due := h_full.count(PAIRS * (b - 2) + PAIRS // 2 * (half + 1))) is not None:
                sp.wait_ge(h_full.sem, due)
            rows = slice(half * HALF, (half + 1) * HALF)
            sp.dma_start(x[b % 2][:, rows], xT[:, rows, b * TB:(b + 1) * TB]).then_inc(x_in[b % 2][half].sem, 16)

    def loaded(engine, b, half):
        came = x_in[b % 2][half]
        engine.wait_ge(came.sem, came.count(16 * (b // 2 + 1)))

    def square(act, b):
        for p in range(PAIRS):
            if p % (PAIRS // 2) == 0:
                loaded(act, b, p // (PAIRS // 2))
            before = ADDS * b + 2 * p - 3 if p >= 2 else ADDS * b - 2 * (1 - p)
            if (due := added.count(before)) is not None:
                act.wait_ge(added.sem, due)
            nc.scalar.activation(sq[p % 2][:], x[b % 2][:, 2 * p:2 * p + 2], ACT.Square).then_inc(squared.sem, 1)

    def add(pool, b):
        for r in range(ADDS):
            if r == 0:
                if (due := summed.count(b)) is not None:
                    pool.wait_ge(summed.sem, due)
                pool.wait_ge(squared.sem, squared.count(PAIRS * b + 1))
                nc.gpsimd.tensor_tensor(acc[:], sq[0][:, 0], sq[0][:, 1], ALU.add).then_inc(added.sem, 1)
            else:
                p = (r + 1) // 2
                pool.wait_ge(squared.sem, squared.count(PAIRS * b + (p + 1)))
                pool.wait_ge(added.sem, added.count(ADDS * b + r))
                nc.gpsimd.tensor_tensor(acc[:], acc[:], sq[p % 2][:, (r + 1) % 2], ALU.add).then_inc(added.sem, 1)

    def sum_rows(pe, b):
        pe.wait_ge(added.sem, added.count(ADDS * (b + 1)))
        pe.wait_ge(const_set.sem, const_set.count(1))
        if (due := rooted.count(b)) is not None:
            pe.wait_ge(rooted.sem, due)
        nc.tensor.matmul(sums[:, :TB], ones[:], acc[:], start=True, stop=True).then_inc(summed.sem, 1)

    def root(act, b):
        act.wait_ge(summed.sem, summed.count(b + 1))
        if (due := h_full.count(PAIRS * b)) is not None:
            act.wait_ge(h_full.sem, due)
        act.wait_ge(const_set.sem, const_set.count(2))
        nc.scalar.activation(rstd[:], sums[:, :TB], ACT.Sqrt, bias=eps[:], scale=1.0 / D).then_inc(rooted.sem, 1)

    def high(act, b):
        for p in range(PAIRS):
            act.wait_ge(h_full.sem, h_full.count(PAIRS * b + (p + 1)))
            nc.scalar.activation(of(parts.h_hi, b, p), h[p % 2][:], ACT.Copy).then_inc(h_hi_ready.sem, 1)

    def constants(dve):
        nc.vector.memset(ones[:], 1.0).then_inc(const_set.sem, 1)
        nc.vector.memset(eps[:], EPS).then_inc(const_set.sem, 1)

    LOWS = PAIRS - 1

    def low(dve, b, p):
        step = PAIRS * b + p
        dve.wait_ge(h_hi_ready.sem, h_hi_ready.count(step + 1))
        dve.wait_ge(h_full.sem, h_full.count(step + 1))
        nc.vector.tensor_tensor(of(parts.h_lo, b, p), h[p % 2][:], of(parts.h_hi, b, p).bitcast(F32), ALU.subtract
                                ).then_inc(h_lo_ready.sem, 1)

    def low_last(pool, b):
        pool.wait_ge(h_hi_ready.sem, h_hi_ready.count(PAIRS * (b + 1)))
        pool.wait_ge(h_full.sem, h_full.count(PAIRS * (b + 1)))
        nc.gpsimd.tensor_tensor(of(parts.h_lo, b, LOWS), h[LOWS % 2][:], of(parts.h_hi, b, LOWS).bitcast(F32), ALU.subtract
                                ).then_inc(h_lo_last_ready.sem, 1)

    def vector(dve):
        dve.wait_ge(const_in.sem, const_in.count(16))
        for b in range(NB):
            dve.wait_ge(rooted.sem, rooted.count(b + 1))
            nc.vector.reciprocal(rstd[:], rstd[:]).then_inc(inverted.sem, 1)
            loaded(dve, b, 0)
            loaded(dve, b, 1)
            for p in range(PAIRS):
                if p > 1:
                    low(dve, b, p - 2)
                if p == 0:
                    dve.wait_ge(inverted.sem, inverted.count(b + 1))
                    if (due := h_lo_ready.count(LOWS * b)) is not None:
                        dve.wait_ge(h_lo_ready.sem, due)
                elif p == 1:
                    if (due := h_lo_last_ready.count(b)) is not None:
                        dve.wait_ge(h_lo_last_ready.sem, due)
                else:
                    dve.wait_ge(h_lo_ready.sem, h_lo_ready.count(LOWS * b + (p - 1)))
                for k in (2 * p, 2 * p + 1):
                    last = nc.vector.scalar_tensor_tensor(h[p % 2][:, k % 2], x[b % 2][:, k], w[:, k:k + 1], rstd[:], ALU.mult, ALU.mult)
                last.then_inc(h_full.sem, 1)
            low(dve, b, LOWS - 1)

    def ready(pe, b):
        pe.wait_ge(h_lo_ready.sem, h_lo_ready.count(LOWS * (b + 1)))
        pe.wait_ge(h_lo_last_ready.sem, h_lo_last_ready.count(b + 1))
        pe.wait_ge(h_hi_ready.sem, h_hi_ready.count(PAIRS * (b + 1)))

    def used(engine, blocks):
        engine.wait_ge(h_full.sem, h_full.count(PAIRS * blocks))
        engine.wait_ge(squared.sem, squared.count(PAIRS * blocks))

    def done():
        for half in range(2):
            x_in[0][half].passed(16 * 3)
            x_in[1][half].passed(16 * 2)
        const_in.passed(16)
        const_set.passed(2)
        added.passed(ADDS * NB)
        h_lo_ready.passed(LOWS * NB)
        for s in (summed, rooted, inverted, h_lo_last_ready):
            s.passed(NB)
        for s in (squared, h_full, h_hi_ready):
            s.passed(PAIRS * NB)

    parts = NormParts(sync, square, add, sum_rows, root, high, constants, vector, low_last, ready, used, done, x)
    return parts


class WeightStream:

    def __init__(self, pg, sb):
        self.pg, self.nc = pg, pg.nc
        self.raw = [sb(f"w_raw{i}", [P, 8, P], F32) for i in range(2)]
        self.hi = [sb(f"w_hi{i}", [P, 8, P], F32R) for i in range(2)]
        self.lo = [sb(f"w_lo{i}", [P, 8, P], F32R) for i in range(2)]
        self.w_in = [pg["w_in_even"], pg["w_in_odd"]]
        self.hi_ready, self.lo_ready, self.psum_full = pg["w_hi_ready"], pg["w_lo_ready"], pg["psum_full"]

    def tiles(self, src, count, following=None):
        self.src, self.count, self.following = src, count, following

    def load(self, sp, n, pair, slot):
        if (due := self.lo_ready.count(n - 1)) is not None:
            sp.wait_ge(self.lo_ready.sem, due)
        src = self.src[one(n)] if not isinstance(n, int) or n < self.count else self.following[one(n - self.count)]
        sp.dma_start(self.raw[slot][:], src.rearrange("o p k c -> p (o k) c")).then_inc(self.w_in[slot].sem, 16)

    def split_hi(self, act, n, pair, slot, used=None):
        act.wait_ge(self.w_in[slot].sem, self.w_in[slot].count((pair + 1) * 16))
        if (due := self.psum_full.count((n - 1) * NB if used is None else used)) is not None:
            act.wait_ge(self.psum_full.sem, due)
        self.nc.scalar.activation(self.hi[slot][:], self.raw[slot][:], ACT.Copy).then_inc(self.hi_ready.sem, 1)

    def split_lo(self, dve, n, pair, slot):
        dve.wait_ge(self.hi_ready.sem, self.hi_ready.count(n + 1))
        self.nc.vector.tensor_tensor(self.lo[slot][:], self.raw[slot][:], self.hi[slot][:].bitcast(F32),
                                     ALU.subtract).then_inc(self.lo_ready.sem, 1)

    def passed(self, n):
        self.w_in[0].passed((n + 1) // 2 * 16)
        self.w_in[1].passed(n // 2 * 16)
        self.hi_ready.passed(n)
        self.lo_ready.passed(n)


def project_block(pg, ws, h_hi, h_lo, bank, n, slot, b):
    for k in range(KD):
        last = pg.split_matmul(bank[:, :TB], ws.hi[slot][:, k], ws.lo[slot][:, k],
                               h_hi[:, k, b * TB:(b + 1) * TB], h_lo[:, k, b * TB:(b + 1) * TB],
                               k == 0, k == KD - 1)
    last.then_inc(ws.psum_full.sem, 1)


def mixer_phases(pg, ws):
    nc, dram = pg.nc, pg.dram
    with ExitStack() as keep:
        def sb_keep(name, shape, dt):
            return keep.enter_context(nc.sbuf_tensor(f"{name}_sb", shape, dt))
        h_hi = sb_keep("h_hi", [P, KD, T], F32R)
        h_lo = sb_keep("h_lo", [P, KD, T], F32R)
        stage = [sb_keep(f"z_stage{i}", [P, TB], F32) for i in range(2)]
        z = dram["z"]
        psum_full, psum_read = pg["psum_full"], pg["psum_read"]
        stored = [pg["z_stored_even"], pg["z_stored_odd"]]

        def store_index(pair, slot, b):
            return pair * 5 + (slot * NB + b) // 2

        def evacuate(act, n, pair, slot, b, bank, tile0):
            s = (slot + b) % 2
            act.wait_ge(psum_full.sem, psum_full.count(n * NB + (b + 1)))
            if (due := stored[s].count(store_index(pair, slot, b) * 16)) is not None:
                act.wait_ge(stored[s].sem, due)
            nc.scalar.activation(stage[s][:], bank[:, :TB], ACT.Copy).then_inc(psum_read.sem, 1)

        def store(sp, n, pair, slot, b, tile0):
            s = (slot + b) % 2
            sp.wait_ge(psum_read.sem, psum_read.count(n * NB + (b + 1)))
            sp.dma_start(z[one(n + tile0), :, b * TB:(b + 1) * TB].rearrange("o p t -> (o p) t"), stage[s][:]
                         ).then_inc(stored[s].sem, 16)

        def stores_passed(n):
            stored[0].passed((n * NB + 1) // 2 * 16)
            stored[1].passed(n * NB // 2 * 16)
            psum_full.passed(n * NB)
            psum_read.passed(n * NB)
            ws.passed(n)

        with ExitStack() as own, nc.Block() as block:
            def sb(name, shape, dt):
                return own.enter_context(nc.sbuf_tensor(f"{name}_sb", shape, dt))
            ws.tiles(dram["w_in"], N_MIX)
            norm = norm_blocks(pg, sb, dram["xT"], dram["norm_mix_pre"], "pre")
            norm.h_hi, norm.h_lo = h_hi, h_lo

            def first_bank(b, tile):
                return pg.bank[b if tile == 0 else 5 + b % 2]

            def first_evacuate(act, b):
                for tile in range(2):
                    step = 2 * b + tile
                    act.wait_ge(psum_full.sem, psum_full.count(step + 1))
                    if (due := stored[tile].count(b * 16)) is not None:
                        act.wait_ge(stored[tile].sem, due)
                    nc.scalar.activation(stage[tile][:], first_bank(b, tile)[:, :TB], ACT.Copy).then_inc(psum_read.sem, 1)

            def first_store(sp, b):
                for tile in range(2):
                    step = 2 * b + tile
                    sp.wait_ge(psum_read.sem, psum_read.count(step + 1))
                    sp.dma_start(z[tile, :, b * TB:(b + 1) * TB], stage[tile][:]).then_inc(stored[tile].sem, 16)

            @block.sync
            def _(sp):
                norm.sync(sp, 0)
                ws.load(sp, 0, 0, 0)
                ws.load(sp, 1, 0, 1)
                norm.sync(sp, 1)
                for b in range(NB):
                    if b + 2 < NB:
                        norm.sync(sp, b + 2)
                    first_store(sp, b)
                    if b < 2:
                        ws.load(sp, b + 2, 1, b)

                def body(n, pair, slot):
                    for b in range(NB):
                        store(sp, n, pair, slot, b, 0)
                    if not isinstance(n, int) or n + 2 < N_MIX:
                        ws.load(sp, n + 2, pair + 1, slot)
                later_pairs_ahead(sp, N_MIX, body)

            @block.scalar
            def _(act):
                norm.square(act, 0)
                ws.split_hi(act, 0, 0, 0)
                ws.split_hi(act, 1, 0, 1)
                norm.root(act, 0)
                for b in range(NB):
                    if b + 1 < NB:
                        norm.square(act, b + 1)
                    norm.high(act, b)
                    if b + 1 < NB:
                        norm.root(act, b + 1)
                    if b > 0:
                        first_evacuate(act, b - 1)
                ws.split_hi(act, 2, 1, 0, used=2 * NB - 1)
                first_evacuate(act, NB - 1)
                ws.split_hi(act, 3, 1, 1, used=2 * NB)

                def body(n, pair, slot):
                    for b in range(NB):
                        evacuate(act, n, pair, slot, b, pg.bank[b], 0)
                    if not isinstance(n, int) or n + 2 < N_MIX:
                        ws.split_hi(act, n + 2, pair + 1, slot)
                later_pairs_ahead(act, N_MIX, body)

            @block.gpsimd
            def _(pool):
                norm.add(pool, 0)
                for b in range(NB):
                    if b + 1 < NB:
                        norm.add(pool, b + 1)
                    norm.low_last(pool, b)

            @block.vector
            def _(dve):
                norm.constants(dve)
                ws.split_lo(dve, 0, 0, 0)
                ws.split_lo(dve, 1, 0, 1)
                norm.vector(dve)
                later_pairs(dve, N_MIX, lambda n, pair, slot: ws.split_lo(dve, n, pair, slot))

            @block.tensor
            def _(pe):
                def weights(n):
                    pe.wait_ge(ws.hi_ready.sem, ws.hi_ready.count(n + 1))
                    pe.wait_ge(ws.lo_ready.sem, ws.lo_ready.count(n + 1))

                norm.sum_rows(pe, 0)
                weights(1)
                for b in range(NB):
                    if b + 1 < NB:
                        norm.sum_rows(pe, b + 1)
                    norm.ready(pe, b)
                    for tile in range(2):
                        if (due := psum_read.count(2 * (b - 1))) is not None and tile == 1:
                            pe.wait_ge(psum_read.sem, due)
                        project_block(pg, ws, h_hi, h_lo, first_bank(b, tile), tile, tile, b)

                def body(n, pair, slot):
                    weights(n)
                    for b in range(NB):
                        pe.wait_ge(psum_read.sem, psum_read.count((n - 1) * NB + (b + 1)))
                        project_block(pg, ws, h_hi, h_lo, pg.bank[b], n, slot, b)
                later_pairs(pe, N_MIX, body)

            norm.done()
            stores_passed(N_MIX)
        attention_phase(pg, ws, h_hi, h_lo, evacuate, store, stores_passed)


def slope(head):
    return 2.0 ** (-8.0 / QH * (head + 1))


def attention_phase(pg, ws, h_hi, h_lo, evacuate, store, stores_passed):
    nc, dram = pg.nc, pg.dram
    z, o_all = dram["z"], dram["o"]
    HALF = DK
    S = pg
    with ExitStack() as own, nc.Block() as block:
        def sb(name, shape, dt=F32):
            return own.enter_context(nc.sbuf_tensor(f"{name}_sb", shape, dt))
        gla = sb("gla_z", [P, 13, P])
        swa = sb("swa_z", [P, 6, P])
        ident, ones = sb("ident", [P, P]), sb("ones_dv", [P, P])
        rel = sb("rel", [P, 2 * WIN])
        w_up, b_up, g_norm = sb("w_up", [P, 2, P]), sb("b_up", [P, 2]), sb("g_norm", [P, 1])
        minus_sink = sb("minus_sink", [P, 4, 2])
        keep, causal = sb("keep", [P, 2 * P]), sb("causal", [P, P])
        eps, key_scale = sb("eps_dv", [P, 1]), sb("key_scale", [P, P])
        a1, a2, a3, a4 = (sb(f"decay{i}", [P, 2 * P]) for i in range(4))
        e1, e2 = sb("exp_centred", [P, 2 * P]), sb("exp_start", [P, 2 * P])
        qz, qez = sb("q_centred", [P, 2, 2, P]), sb("q_start", [P, 2, 2, P])
        kt, kdz = sb("k_centred", [P, 2, P]), sb("k_end_turned", [P, 2, 2, P])
        v_tok, att = sb("v_tokens", [P, 4, P]), sb("att", [P, 4, P])
        state = [sb(f"state{i}", [P, 2, P]) for i in range(2)]
        rstd = sb("rstd_dv", [P, 4, P])
        kz, v_win = sb("k_window", [P, 2, 2 * WIN]), sb("v_window", [P, 2, P])
        p = sb("probs", [P, 4, 2 * WIN])
        p_t = sb("probs_turned", [P, 2, 4, P])
        o_win = sb("o_window", [P, 4, P])
        m, row, den, sink_e = (sb(x, [P, 2, 4]) for x in ("minus_max", "row_sum", "denominator", "sink_exp"))
        b_gemm, b_s, b_att, b_o, b_m, b_w = pg.bank[0:2], pg.bank[2:4], pg.bank[4], pg.bank[5], pg.bank[6], pg.bank[7]
        gate_v = att

        ws.tiles(dram["w_in"][N_MIX:N_Z], NWIN, dram["w_branch"])

        def chunks(ap):
            return ap.rearrange("p (c t) -> p c t", t=CH)

        loads = [(ident, dram["ident"]), (w_up, dram["w_gate_up"].rearrange("r (t c) -> r t c", t=2)),
                 (b_up, dram["b_gate"]), (g_norm, dram["gla_norm"]),
                 (minus_sink, dram["sinks"]), (keep, dram["scan_keep"]), (causal, dram["causal"]), (rel, dram["rel_first"])]

        @block.sync
        def _(sp):
            for tile, src in loads:
                sp.dma_start(tile[:], src).then_inc(S["att_const_in"].sem, 16)

            def load_gla(i):
                sp.dma_start(gla[:, 0:8], z[0:8, :, span(i, P)].rearrange("t p c -> p t c")).then_inc(S["gla_in"].sem, 16)
                sp.dma_start(gla[:, 12:], z[12:13, :, span(i, P)].rearrange("t p c -> p t c")).then_inc(S["gla_in"].sem, 16)

            def load_gates(i):
                sp.dma_start(gla[:, 8:12], z[8:12, :, span(i, P)].rearrange("t p c -> p t c")).then_inc(S["out_gate_in"].sem, 16)

            def load_window(i):
                sp.dma_start(swa[:], z[13:19, :, span(i, P)].rearrange("t p c -> p t c")).then_inc(S["swa_in"].sem, 16)

            def body(i, pair, slot):
                more = not isinstance(i, int) or i + 1 < NWIN
                if more:
                    sp.wait_ge(S["logits_full"].sem, S["logits_full"].count(i + 1))
                    sp.wait_ge(S["v_turned"].sem, S["v_turned"].count(i + 1))
                    sp.wait_ge(S["kt_ready"].sem, S["kt_ready"].count(i + 1))
                    sp.wait_ge(S["qez_ready"].sem, S["qez_ready"].count(i + 1))
                    sp.wait_ge(S["qz_ready"].sem, S["qz_ready"].count(i + 1))
                    sp.wait_ge(S["kd_turned"].sem, S["kd_turned"].count(i + 1))
                    load_gla(i + 1)
                store(sp, i, pair, slot, 0, N_MIX)
                store(sp, i, pair, slot, 1, N_MIX)
                if more:
                    sp.wait_ge(S["vb_turned"].sem, S["vb_turned"].count(i + 1))
                    sp.wait_ge(S["kz_ready"].sem, S["kz_ready"].count(i + 1))
                    sp.wait_ge(S["scores1_full"].sem, S["scores1_full"].count(i + 1))
                    load_window(i + 1)
                if isinstance(i, int) and i == 0:
                    sp.wait_ge(S["s1_ready"].sem, S["s1_ready"].count(1))
                    sp.dma_start(rel[:], dram["rel"]).then_inc(S["att_const_in"].sem, 16)
                store(sp, i, pair, slot, 2, N_MIX)
                store(sp, i, pair, slot, 3, N_MIX)
                sp.wait_ge(S["gla_out_ready"].sem, S["gla_out_ready"].count(i + 1))
                sp.dma_start(o_all[0:4, :, span(i, P)].rearrange("t p c -> p t c"), rstd[:]).then_inc(S["oa_stored"].sem, 16)
                if more:
                    sp.wait_ge(S["silu_ready"].sem, S["silu_ready"].count(i + 1))
                    load_gates(i + 1)
                store(sp, i, pair, slot, 4, N_MIX)
                ws.load(sp, i + 2, pair + 1, slot)
                sp.wait_ge(S["ow1_read"].sem, S["ow1_read"].count(i + 1))
                sp.dma_start(o_all[4:8, :, span(i, P)].rearrange("t p c -> p t c"), o_win[:]).then_inc(S["ob_stored"].sem, 16)
            load_gla(0)
            load_window(0)
            load_gates(0)
            ws.load(sp, 0, 0, 0)
            ws.load(sp, 1, 0, 1)
            each_pair_ahead(sp, NWIN, body)
            sp.wait_ge(S["state_end"].sem, S["state_end"].count(NWIN))
            sp.dma_start(dram["gla_state_prompt"].rearrange("(t h) d v -> (h d) t v", t=2), state[0][:]
                         ).then_inc(S["state_stored"].sem, 16)
            sp.wait_ge(S["state_stored"].sem, S["state_stored"].count(16))
            sp.wait_ge(S["oa_stored"].sem, S["oa_stored"].count(NWIN * 16))
            sp.wait_ge(S["ob_stored"].sem, S["ob_stored"].count(NWIN * 16))

        @block.gpsimd
        def _(pool):
            for zeroed in (kz, v_win, qz, qez, kdz, att, state[0]):
                nc.gpsimd.memset(zeroed[:], 0.0).then_inc(S["zeroed"].sem, 1)
            nc.gpsimd.memset(ones[:], 1.0).then_inc(S["zeroed"].sem, 1)
            nc.gpsimd.memset(eps[:], EPS).then_inc(S["zeroed"].sem, 1)
            nc.gpsimd.memset(key_scale[:], HD ** -0.5).then_inc(S["zeroed"].sem, 1)
            pool.wait_ge(S["zeroed"].sem, S["zeroed"].count(10))

            def body(i):
                pool.wait_ge(S["zeroed"].sem, S["zeroed"].count(10))
                if (due := S["scores1_full"].count(i)) is not None:
                    pool.wait_ge(S["scores1_full"].sem, due)
                if (due := S["kz_ready"].count(i)) is not None:
                    pool.wait_ge(S["kz_ready"].sem, due)
                nc.gpsimd.tensor_copy(kz[:, :, 0:WIN], kz[:, :, WIN:2 * WIN]).then_inc(S["kz_shifted"].sem, 1)
                pool.wait_ge(S["kz_shifted"].sem, S["kz_shifted"].count(i + 1))
                pool.wait_ge(S["swa_in"].sem, S["swa_in"].count((i + 1) * 16))
                nc.gpsimd.tensor_tensor(kz[0:HALF, 0, WIN:], swa[0:HALF, 4], key_scale[0:HALF], ALU.mult
                                        ).then_inc(S["kz_low_half"].sem, 1)
                pool.wait_ge(S["kz_low_half"].sem, S["kz_low_half"].count(i + 1))
                nc.gpsimd.tensor_tensor(kz[HALF:, 1, WIN:], swa[HALF:, 4], key_scale[HALF:], ALU.mult
                                        ).then_inc(S["kz_ready"].sem, 1)
                pool.wait_ge(S["zeroed"].sem, S["zeroed"].count(10))
                pool.wait_ge(S["kz_ready"].sem, S["kz_ready"].count(i + 1))
                if (due := S["ow1_full"].count(i)) is not None:
                    pool.wait_ge(S["ow1_full"].sem, due)
                if (due := S["vb_ready"].count(i)) is not None:
                    pool.wait_ge(S["vb_ready"].sem, due)
                nc.gpsimd.tensor_copy(v_win[:, 0], v_win[:, 1]).then_inc(S["vb_shifted"].sem, 1)
                pool.wait_ge(S["ek_ready"].sem, S["ek_ready"].count(i + 1))
                pool.wait_ge(S["gla_in"].sem, S["gla_in"].count((i + 1) * 32))
                if (due := S["att_full"].count(i)) is not None:
                    pool.wait_ge(S["att_full"].sem, due)
                nc.gpsimd.tensor_tensor(kt[:], gla[:, 2:4], a4[:].rearrange("p (t c) -> p t c", t=2), ALU.mult
                                        ).then_inc(S["kt_ready"].sem, 1)
                pool.wait_ge(S["eo_ready"].sem, S["eo_ready"].count(i + 1))
                pool.wait_ge(S["kt_ready"].sem, S["kt_ready"].count(i + 1))
                nc.gpsimd.tensor_tensor(gla[:, 2:4], gla[:, 2:4], a1[:].rearrange("p (t c) -> p t c", t=2), ALU.mult
                                        ).then_inc(S["kd_ready"].sem, 1)
                pool.wait_ge(S["sigmoid_ready"].sem, S["sigmoid_ready"].count(i + 1))
                nc.gpsimd.tensor_tensor(gate_v[:], gla[:, 8:12], gate_v[:], ALU.mult).then_inc(S["silu_ready"].sem, 1)
            each(pool, NWIN, body)

        @block.scalar
        def _(act):
            copy = lambda out, in_, **kw: nc.scalar.activation(out, in_, ACT.Copy, **kw)

            def softmax(half, i):
                act.wait_ge(S[f"m{half}_ready"].sem, S[f"m{half}_ready"].count(i + 1))
                for j in range(4):
                    last = nc.scalar.activation(p[:, j], p[:, j], ACT.Exp, bias=m[:, half, j:j + 1],
                                                accum_out=row[:, half, j:j + 1])
                last.then_inc(S[f"exp{half}_ready"].sem, 1)
                act.wait_ge(S[f"sink{half}_ready"].sem, S[f"sink{half}_ready"].count(i + 1))
                nc.scalar.activation(sink_e[:, half], sink_e[:, half], ACT.Exp).then_inc(S[f"sinkexp{half}_ready"].sem, 1)

            def body(i, pair, slot):
                act.wait_ge(S["logits_full"].sem, S["logits_full"].count(i + 1))
                if (due := S["kd_ready"].count(i)) is not None:
                    act.wait_ge(S["kd_ready"].sem, due)
                for t in range(2):
                    last = nc.scalar.activation(a1[:, t * P:(t + 1) * P], b_att[:, t * P:(t + 1) * P], ACT.Abs, bias=b_up[:, t:t + 1])
                last.then_inc(S["abs_ready"].sem, 1)
                act.wait_ge(S["abs_ready"].sem, S["abs_ready"].count(i + 1))
                nc.scalar.activation(a1[:], a1[:], ACT.Exp, scale=-1.0).then_inc(S["abs_exp"].sem, 1)
                act.wait_ge(S["abs_exp"].sem, S["abs_exp"].count(i + 1))
                nc.scalar.activation(a1[:], a1[:], ACT.Ln, bias=1.0).then_inc(S["softplus_ready"].sem, 1)
                act.wait_ge(S["v_turned"].sem, S["v_turned"].count(i + 1))
                if (due := S["o_full"].count(i)) is not None:
                    act.wait_ge(S["o_full"].sem, due)
                copy(v_tok[:].rearrange("p h c -> p (h c)"), b_m[:]).then_inc(S["v_ready"].sem, 1)
                act.wait_ge(S["centred"].sem, S["centred"].count(i + 1))
                if (due := S["qz_ready"].count(i)) is not None:
                    act.wait_ge(S["qz_ready"].sem, due)
                nc.scalar.activation(e1[:], a4[:], ACT.Exp, scale=1.0 / TAU).then_inc(S["eq_ready"].sem, 1)
                act.wait_ge(S["eq_ready"].sem, S["eq_ready"].count(i + 1))
                nc.scalar.activation(a4[:], a4[:], ACT.Exp, scale=-1.0 / TAU).then_inc(S["ek_ready"].sem, 1)
                act.wait_ge(S["tail_ready"].sem, S["tail_ready"].count(i + 1))
                nc.scalar.activation(a1[:], a1[:], ACT.Exp, scale=1.0 / TAU).then_inc(S["eo_ready"].sem, 1)
                if (due := S["state_end"].count(i)) is not None:
                    act.wait_ge(S["state_end"].sem, due)
                nc.scalar.activation(e2[:], a3[:], ACT.Exp, scale=1.0 / TAU).then_inc(S["ei_ready"].sem, 1)
                act.wait_ge(S["vb_turned"].sem, S["vb_turned"].count(i + 1))
                act.wait_ge(S["vb_shifted"].sem, S["vb_shifted"].count(i + 1))
                copy(v_win[:, 1], b_w[:, 0:P]).then_inc(S["vb_ready"].sem, 1)
                act.wait_ge(S["kd_turned"].sem, S["kd_turned"].count(i + 1))
                if (due := S["u_full"].count(i)) is not None:
                    act.wait_ge(S["u_full"].sem, due)
                for c in range(2):
                    last = copy(kdz[c * HALF:(c + 1) * HALF, c].rearrange("p t c -> p (t c)"), b_m[c * HALF:(c + 1) * HALF, 2 * P:])
                last.then_inc(S["kd_ready_turned"].sem, 1)
                softmax(0, i)
                evacuate(act, i, pair, slot, 0, b_gemm[slot], N_MIX)
                if not isinstance(i, int) or i > 0:
                    ws.split_hi(act, i + 1, pair + slot, 1 - slot)
                evacuate(act, i, pair, slot, 1, b_gemm[1 - slot], N_MIX)
                act.wait_ge(S["pt0_full"].sem, S["pt0_full"].count(i + 1))
                if (due := S["ow1_full"].count(i)) is not None:
                    act.wait_ge(S["ow1_full"].sem, due)
                copy(p_t[:, 0].rearrange("p h c -> p (h c)"), b_s[0][:]).then_inc(S["pt0_read_a"].sem, 1)
                softmax(1, i)
                evacuate(act, i, pair, slot, 2, b_gemm[slot], N_MIX)
                act.wait_ge(S["ow0_full"].sem, S["ow0_full"].count(i + 1))
                if (due := S["ob_stored"].count(i * 16)) is not None:
                    act.wait_ge(S["ob_stored"].sem, due)
                copy(o_win[:, 0:2].rearrange("p h c -> p (h c)"), b_w[:, 2 * P:]).then_inc(S["ow0_read"].sem, 1)
                if (due := S["oa_stored"].count(i * 16)) is not None:
                    act.wait_ge(S["oa_stored"].sem, due)
                act.wait_ge(S["o_full"].sem, S["o_full"].count(i + 1))
                if (due := S["gla_out_ready"].count(i)) is not None:
                    act.wait_ge(S["gla_out_ready"].sem, due)
                nc.scalar.activation(rstd[:].rearrange("p h c -> p (h c)"), b_o[:], ACT.Square).then_inc(S["o_squared"].sem, 1)
                act.wait_ge(S["out_gate_in"].sem, S["out_gate_in"].count((i + 1) * 16))
                nc.scalar.activation(gate_v[:], gla[:, 8:12], ACT.Exp, scale=-1.0).then_inc(S["gate_exp"].sem, 1)
                evacuate(act, i, pair, slot, 3, b_gemm[1 - slot], N_MIX)
                act.wait_ge(S["sums_full"].sem, S["sums_full"].count(i + 1))
                flat = rstd[:].rearrange("p h c -> p (h c)")
                nc.scalar.activation(flat, b_att[:], ACT.Ln, scale=1.0 / DV, bias=eps[:]).then_inc(S["log_ms"].sem, 1)
                act.wait_ge(S["log_ms"].sem, S["log_ms"].count(i + 1))
                nc.scalar.activation(flat, flat, ACT.Exp, scale=-0.5).then_inc(S["rstd_ready"].sem, 1)
                act.wait_ge(S["pt1_full"].sem, S["pt1_full"].count(i + 1))
                act.wait_ge(S["ow0_full"].sem, S["ow0_full"].count(i + 1))
                copy(p_t[:, 0].rearrange("p h c -> p (h c)"), b_s[0][:]).then_inc(S["pt1_read_a"].sem, 1)
                evacuate(act, i, pair, slot, 4, b_gemm[slot], N_MIX)
                act.wait_ge(S["ow1_full"].sem, S["ow1_full"].count(i + 1))
                copy(o_win[:, 2:4].rearrange("p h c -> p (h c)"), b_w[:, 2 * P:]).then_inc(S["ow1_read"].sem, 1)
            nc.scalar.preload_act_table_set("natural_log_exp_and_others")
            act.wait_ge(S["att_const_in"].sem, S["att_const_in"].count(16 * len(loads)))
            act.wait_ge(S["zeroed"].sem, S["zeroed"].count(10))
            ws.split_hi(act, 0, 0, 0)
            ws.split_hi(act, 1, 0, 1)
            each_pair_ahead(act, NWIN, body)
            ws.split_hi(act, NWIN + 1, NWIN // 2, 1)

        @block.vector
        def _(dve):
            v = nc.vector

            def logits(half, i):
                dve.wait_ge(S[f"scores{half}_full"].sem, S[f"scores{half}_full"].count(i + 1))
                if (due := S["pt1_full" if half == 0 else "pt0_full"].count(i if half == 0 else i + 1)) is not None:
                    dve.wait_ge(S["pt1_full" if half == 0 else "pt0_full"].sem, due)
                for t in range(2):
                    for kv in range(2):
                        last = v.scalar_tensor_tensor(p[:, 2 * t + kv], rel[:], slope(kv * 4 + 2 * half + t),
                                                      b_s[t][:, kv * 256:(kv + 1) * 256], ALU.mult, ALU.add)
                last.then_inc(S[f"s{half}_ready"].sem, 1)

            def maximum(half, i):
                dve.wait_ge(S[f"s{half}_ready"].sem, S[f"s{half}_ready"].count(i + 1))
                v.tensor_reduce(m[:, half], p[:], AX.X, ALU.max, negate=True).then_inc(S[f"max{half}_ready"].sem, 1)
                dve.wait_ge(S[f"max{half}_ready"].sem, S[f"max{half}_ready"].count(i + 1))
                sink = minus_sink[:, 2 * half:2 * half + 2].rearrange("p t k -> p (t k)")
                v.tensor_tensor(m[:, half], m[:, half], sink, ALU.min).then_inc(S[f"m{half}_ready"].sem, 1)
                dve.wait_ge(S[f"m{half}_ready"].sem, S[f"m{half}_ready"].count(i + 1))
                v.tensor_tensor(sink_e[:, half], m[:, half], sink, ALU.subtract).then_inc(S[f"sink{half}_ready"].sem, 1)

            def normalise(half, i):
                dve.wait_ge(S[f"exp{half}_ready"].sem, S[f"exp{half}_ready"].count(i + 1))
                dve.wait_ge(S[f"sinkexp{half}_ready"].sem, S[f"sinkexp{half}_ready"].count(i + 1))
                v.tensor_tensor(den[:, half], row[:, half], sink_e[:, half], ALU.add).then_inc(S[f"den{half}_ready"].sem, 1)
                dve.wait_ge(S[f"den{half}_ready"].sem, S[f"den{half}_ready"].count(i + 1))
                v.reciprocal(den[:, half], den[:, half]).then_inc(S[f"inv{half}_ready"].sem, 1)
                dve.wait_ge(S[f"inv{half}_ready"].sem, S[f"inv{half}_ready"].count(i + 1))
                for j in range(4):
                    last = v.tensor_scalar(p[:, j], p[:, j], den[:, half, j:j + 1], None, ALU.mult)
                last.then_inc(S[f"p{half}_ready"].sem, 1)

            def body(i, pair, slot):
                if isinstance(i, int) and i == 1:
                    dve.wait_ge(S["att_const_in"].sem, S["att_const_in"].count(16 * (len(loads) + 1)))
                dve.wait_ge(S["abs_ready"].sem, S["abs_ready"].count(i + 1))
                for t in range(2):
                    last = v.tensor_scalar(a2[:, t * P:(t + 1) * P], b_att[:, t * P:(t + 1) * P], b_up[:, t:t + 1], 0.0, ALU.add, ALU.min)
                last.then_inc(S["lm_ready"].sem, 1)
                dve.wait_ge(S["softplus_ready"].sem, S["softplus_ready"].count(i + 1))
                dve.wait_ge(S["lm_ready"].sem, S["lm_ready"].count(i + 1))
                v.tensor_tensor(a2[:], a2[:], a1[:], ALU.subtract).then_inc(S["log_a_ready"].sem, 1)
                dve.wait_ge(S["log_a_ready"].sem, S["log_a_ready"].count(i + 1))
                if (due := S["ei_ready"].count(i)) is not None:
                    dve.wait_ge(S["ei_ready"].sem, due)
                v.tensor_tensor_scan(a3[:], keep[:], a2[:], 0.0, ALU.mult, ALU.add).then_inc(S["b_ready"].sem, 1)
                dve.wait_ge(S["b_ready"].sem, S["b_ready"].count(i + 1))
                if (due := S["kt_ready"].count(i)) is not None:
                    dve.wait_ge(S["kt_ready"].sem, due)
                b = chunks(a3[:])
                v.tensor_tensor(chunks(a4[:]), b, b[:, :, CH // 2 - 1:CH // 2].to_broadcast([P, 4, CH]), ALU.subtract
                                ).then_inc(S["shifted"].sem, 1)
                v.tensor_tensor(chunks(a1[:]), b[:, :, CH - 1:CH].to_broadcast([P, 4, CH]), b, ALU.subtract
                                ).then_inc(S["tail_ready"].sem, 1)
                dve.wait_ge(S["shifted"].sem, S["shifted"].count(i + 1))
                v.tensor_scalar(a4[:], a4[:], 80.0 * TAU, -80.0 * TAU, ALU.min, ALU.max).then_inc(S["centred"].sem, 1)
                logits(0, i)
                dve.wait_ge(S["eq_ready"].sem, S["eq_ready"].count(i + 1))
                dve.wait_ge(S["gla_in"].sem, S["gla_in"].count((i + 1) * 32))
                if (due := S["att_full"].count(i)) is not None:
                    dve.wait_ge(S["att_full"].sem, due)
                for t, e in ((0, e1),):
                    for hh in range(2):
                        rows = slice(hh * HALF, (hh + 1) * HALF)
                        last = v.scalar_tensor_tensor(qz[rows, :, hh], gla[rows, 0:2], DK ** -0.5,
                                                      e[rows].rearrange("p (t c) -> p t c", t=2), ALU.mult, ALU.mult)
                last.then_inc(S["qz_ready"].sem, 1)
                maximum(0, i)
                dve.wait_ge(S["ei_ready"].sem, S["ei_ready"].count(i + 1))
                if (due := S["o_full"].count(i)) is not None:
                    dve.wait_ge(S["o_full"].sem, due)
                for hh in range(2):
                    rows = slice(hh * HALF, (hh + 1) * HALF)
                    last = v.scalar_tensor_tensor(qez[rows, :, hh], gla[rows, 0:2], DK ** -0.5,
                                                  e2[rows].rearrange("p (t c) -> p t c", t=2), ALU.mult, ALU.mult)
                last.then_inc(S["qez_ready"].sem, 1)
                dve.wait_ge(S["att_const_in"].sem, S["att_const_in"].count(16 * len(loads)))
                dve.wait_ge(S["att_full"].sem, S["att_full"].count(i + 1))
                if (due := S["gla_out_ready"].count(i)) is not None:
                    dve.wait_ge(S["gla_out_ready"].sem, due)
                dve.wait_ge(S["att_cleared"].sem, S["att_cleared"].count(i + 1))
                for hh in range(4):
                    last = v.copy_predicated(att[:, hh], causal[:].bitcast(I32), b_att[:, hh * P:(hh + 1) * P])
                last.then_inc(S["att_ready"].sem, 1)
                normalise(0, i)
                if not isinstance(i, int) or i > 0:
                    ws.split_lo(dve, i + 1, pair + slot, 1 - slot)
                dve.wait_ge(S["pt0_full"].sem, S["pt0_full"].count(i + 1))
                if (due := S["ow1_full"].count(i)) is not None:
                    dve.wait_ge(S["ow1_full"].sem, due)
                v.tensor_copy(p_t[:, 1].rearrange("p h c -> p (h c)"), b_s[1][:]).then_inc(S["pt0_read_b"].sem, 1)
                dve.wait_ge(S["u_full"].sem, S["u_full"].count(i + 1))
                for c in range(2):
                    if c == 0:
                        if (due := S["o_full"].count(i)) is not None:
                            dve.wait_ge(S["o_full"].sem, due)
                    else:
                        dve.wait_ge(S["inter0_done"].sem, S["inter0_done"].count(i + 1))
                        dve.wait_ge(S["state_mid"].sem, S["state_mid"].count(i + 1))
                    for t in range(2):
                        at = t * P + c * CH + CH - 1
                        last = v.scalar_tensor_tensor(state[1 - c][:, t], state[c][:, t], e2[:, at:at + 1],
                                                      b_m[:, (2 * c + t) * P:(2 * c + t + 1) * P], ALU.mult, ALU.add)
                    last.then_inc(S["state_end" if c else "state_mid"].sem, 1)
                logits(1, i)
                maximum(1, i)
                normalise(1, i)
                dve.wait_ge(S["gate_exp"].sem, S["gate_exp"].count(i + 1))
                v.tensor_scalar(gate_v[:], gate_v[:], 1.0, None, ALU.add).then_inc(S["gate_den"].sem, 1)
                dve.wait_ge(S["gate_den"].sem, S["gate_den"].count(i + 1))
                v.reciprocal(gate_v[:], gate_v[:]).then_inc(S["sigmoid_ready"].sem, 1)
                dve.wait_ge(S["pt1_full"].sem, S["pt1_full"].count(i + 1))
                dve.wait_ge(S["ow0_full"].sem, S["ow0_full"].count(i + 1))
                v.tensor_copy(p_t[:, 1].rearrange("p h c -> p (h c)"), b_s[1][:]).then_inc(S["pt1_read_b"].sem, 1)
                dve.wait_ge(S["rstd_ready"].sem, S["rstd_ready"].count(i + 1))
                flat = rstd[:].rearrange("p h c -> p (h c)")
                v.scalar_tensor_tensor(flat, b_o[:], g_norm[:, 0:1], flat, ALU.mult, ALU.mult).then_inc(S["o_normed"].sem, 1)
                dve.wait_ge(S["silu_ready"].sem, S["silu_ready"].count(i + 1))
                dve.wait_ge(S["o_normed"].sem, S["o_normed"].count(i + 1))
                v.tensor_tensor(rstd[:], rstd[:], gate_v[:], ALU.mult).then_inc(S["gla_out_ready"].sem, 1)
                dve.wait_ge(S["gla_out_ready"].sem, S["gla_out_ready"].count(i + 1))
                v.memset(att[:], 0.0).then_inc(S["att_cleared"].sem, 1)
            dve.wait_ge(S["att_const_in"].sem, S["att_const_in"].count(16 * len(loads)))
            dve.wait_ge(S["zeroed"].sem, S["zeroed"].count(9))
            v.memset(att[:], 0.0).then_inc(S["att_cleared"].sem, 1)
            v.tensor_scalar(minus_sink[:], minus_sink[:], -1.0, None, ALU.mult).then_inc(S["sink_negated"].sem, 1)
            dve.wait_ge(S["sink_negated"].sem, S["sink_negated"].count(1))
            ws.split_lo(dve, 0, 0, 0)
            ws.split_lo(dve, 1, 0, 1)
            each_pair_ahead(dve, NWIN, body)
            ws.split_lo(dve, NWIN + 1, NWIN // 2, 1)

        @block.tensor
        def _(pe):
            mm = nc.tensor.matmul

            def gemm(i, pair, slot, b):
                if b == 0:
                    pe.wait_ge(ws.hi_ready.sem, ws.hi_ready.count(i + 1))
                    pe.wait_ge(ws.lo_ready.sem, ws.lo_ready.count(i + 1))
                if (due := S["psum_read"].count(i * NB + (b - 1))) is not None:
                    pe.wait_ge(S["psum_read"].sem, due)
                project_block(pg, ws, h_hi, h_lo, b_gemm[(slot + b) % 2], i, slot, b)

            def scores(half, i):
                for t in range(2):
                    last = mm(b_s[t][:], swa[:, 2 * half + t], kz[:].rearrange("p k c -> p (k c)"), start=True, stop=True)
                last.then_inc(S[f"scores{half}_full"].sem, 1)

            def turn_p(half, i):
                pe.wait_ge(S[f"p{half}_ready"].sem, S[f"p{half}_ready"].count(i + 1))
                for pc in range(2):
                    for j in range(4):
                        last = nc.tensor.transpose(b_s[pc][:, j * P:(j + 1) * P], p[:, j, pc * WIN:(pc + 1) * WIN], ident[:])
                last.then_inc(S[f"pt{half}_full"].sem, 1)

            def window_out(half, i):
                pe.wait_ge(S[f"pt{half}_read_a"].sem, S[f"pt{half}_read_a"].count(i + 1))
                pe.wait_ge(S[f"pt{half}_read_b"].sem, S[f"pt{half}_read_b"].count(i + 1))
                for t in range(2):
                    for kv in range(2):
                        rows = slice(kv * HALF, (kv + 1) * HALF)
                        for pc in range(2):
                            last = mm(b_w[rows, (2 + t) * P:(3 + t) * P], v_win[:, pc, rows], p_t[:, pc, 2 * t + kv],
                                      start=(pc == 0), stop=(pc == 1))
                last.then_inc(S[f"ow{half}_full"].sem, 1)

            def body(i, pair, slot):
                pe.wait_ge(S["gla_in"].sem, S["gla_in"].count((i + 1) * 32))
                if (due := S["log_ms"].count(i)) is not None:
                    pe.wait_ge(S["log_ms"].sem, due)
                for t in range(2):
                    last = mm(b_att[:, t * P:(t + 1) * P], w_up[:, t], gla[:, 12], start=True, stop=True)
                last.then_inc(S["logits_full"].sem, 1)
                if (due := S["state_end"].count(i)) is not None:
                    pe.wait_ge(S["state_end"].sem, due)
                for hh in range(4):
                    last = nc.tensor.transpose(b_m[:, hh * P:(hh + 1) * P], gla[:, 4 + hh], ident[:])
                last.then_inc(S["v_turned"].sem, 1)
                pe.wait_ge(S["swa_in"].sem, S["swa_in"].count((i + 1) * 16))
                if (due := S["ow1_read"].count(i)) is not None:
                    pe.wait_ge(S["ow1_read"].sem, due)
                nc.tensor.transpose(b_w[:, 0:P], swa[:, 5], ident[:]).then_inc(S["vb_turned"].sem, 1)
                pe.wait_ge(S["kz_ready"].sem, S["kz_ready"].count(i + 1))
                if (due := S["pt1_read_a"].count(i)) is not None:
                    pe.wait_ge(S["pt1_read_a"].sem, due)
                if (due := S["pt1_read_b"].count(i)) is not None:
                    pe.wait_ge(S["pt1_read_b"].sem, due)
                scores(0, i)
                gemm(i, pair, slot, 0)
                pe.wait_ge(S["kt_ready"].sem, S["kt_ready"].count(i + 1))
                pe.wait_ge(S["qz_ready"].sem, S["qz_ready"].count(i + 1))
                pe.wait_ge(S["abs_ready"].sem, S["abs_ready"].count(i + 1))
                pe.wait_ge(S["lm_ready"].sem, S["lm_ready"].count(i + 1))
                for t in range(2):
                    last = mm(b_att[:, t * 2 * P:(t + 1) * 2 * P], kt[:, t], qz[:, t].rearrange("p h c -> p (h c)"), start=True, stop=True)
                last.then_inc(S["att_full"].sem, 1)
                pe.wait_ge(S["kd_ready"].sem, S["kd_ready"].count(i + 1))
                pe.wait_ge(S["v_ready"].sem, S["v_ready"].count(i + 1))
                for t in range(2):
                    last = nc.tensor.transpose(b_m[:, (2 + t) * P:(3 + t) * P], gla[:, 2 + t], ident[:])
                last.then_inc(S["kd_turned"].sem, 1)
                gemm(i, pair, slot, 1)
                turn_p(0, i)
                pe.wait_ge(S["kd_ready_turned"].sem, S["kd_ready_turned"].count(i + 1))
                for c in range(2):
                    for t in range(2):
                        for hh in range(2):
                            rows = slice(hh * HALF, (hh + 1) * HALF)
                            last = mm(b_m[rows, (2 * c + t) * P:(2 * c + t + 1) * P], kdz[:, c, t, rows], v_tok[:, 2 * t + hh],
                                      start=True, stop=True)
                last.then_inc(S["u_full"].sem, 1)
                pe.wait_ge(S["att_ready"].sem, S["att_ready"].count(i + 1))
                if (due := S["gla_out_ready"].count(i)) is not None:
                    pe.wait_ge(S["gla_out_ready"].sem, due)
                for hh in range(4):
                    mm(b_o[:, hh * P:(hh + 1) * P], v_tok[:, hh], att[:, hh], start=(hh == 0), stop=False, skip_group_check=True)
                pe.wait_ge(S["qez_ready"].sem, S["qez_ready"].count(i + 1))
                for c in range(2):
                    if c == 1:
                        pe.wait_ge(S["pt0_read_a"].sem, S["pt0_read_a"].count(i + 1))
                        pe.wait_ge(S["pt0_read_b"].sem, S["pt0_read_b"].count(i + 1))
                        scores(1, i)
                        gemm(i, pair, slot, 2)
                        window_out(0, i)
                    state_before = S["state_mid" if c else "state_end"]
                    if (due := state_before.count(i + c)) is not None:
                        pe.wait_ge(state_before.sem, due)
                    for t in range(2):
                        out = b_o[:].rearrange("p (t h c) -> p t h c", t=2, h=2)[:, t, :, c * CH:(c + 1) * CH]
                        last = mm(out, state[c][:, t], qez[:, t, :, c * CH:(c + 1) * CH],
                                  start=False, stop=(c == 1 and t == 1), skip_group_check=True)
                    last.then_inc(S["o_full" if c else "inter0_done"].sem, 1)
                gemm(i, pair, slot, 3)
                pe.wait_ge(S["o_squared"].sem, S["o_squared"].count(i + 1))
                mm(b_att[:], ones[:], rstd[:].rearrange("p h c -> p (h c)"), start=True, stop=True).then_inc(S["sums_full"].sem, 1)
                turn_p(1, i)
                gemm(i, pair, slot, 4)
                pe.wait_ge(S["ow0_read"].sem, S["ow0_read"].count(i + 1))
                window_out(1, i)
            pe.wait_ge(S["att_const_in"].sem, S["att_const_in"].count(16 * len(loads)))
            pe.wait_ge(S["zeroed"].sem, S["zeroed"].count(9))
            each_pair_ahead(pe, NWIN, body)

        stores_passed(NWIN)
        for name in STEP_SIGNALS:
            S[name].passed(NWIN)
        S["sink_negated"].passed(1)


def load_branches(pg, sp, o_raw, b):
    came, slot = pg["o_in_odd" if b % 2 else "o_in_even"], o_raw[b % 2]
    sp.dma_start(slot[:], pg.dram["o"][:, :, b * TB:(b + 1) * TB].rearrange("t p c -> p t c")).then_inc(came.sem, 16)


def sample_phase(pg, o_raw):
    nc, dram = pg.nc, pg.dram
    z, o_all = dram["z"], dram["o"]
    S = pg
    HALF = DK
    L2 = 2 * NS
    with ExitStack() as own, nc.Block() as block:
        def sb(name, shape, dt=F32):
            return own.enter_context(nc.sbuf_tensor(f"{name}_smp", shape, dt))
        gla, swa = sb("gla", [P, 13, NS]), sb("swa", [P, 6, NS])
        ident, ones, eps = sb("ident", [P, P]), sb("ones", [P, P]), sb("eps", [P, 1])
        w_up, b_up, g_norm = sb("w_up", [P, 2, P]), sb("b_up", [P, 2]), sb("g_norm", [P, 1])
        keep, causal, own_rows = sb("keep", [P, L2]), sb("causal", [NS, NS]), sb("own_rows", [NS, NSEQ])
        bias, minus_sink = sb("bias", [P, 2, WIN + NS]), sb("minus_sink", [P, 1])
        state_in, state_out = sb("state_in", [P, 2, NSEQ, P]), sb("state_out", [P, 2, NSEQ, P])
        k_cache, v_cache = sb("k_cache", [P, NSEQ, WIN]), sb("v_cache", [P, NSEQ, P])
        a1, a2, a3, a4, e1, e2 = (sb(f"decay{i}", [P, L2]) for i in range(6))
        qz, qez = sb("q_centred", [P, 2, 2, NS]), sb("q_start", [P, 2, 2, NS])
        kt, kd, kdz = sb("k_centred", [P, 2, NS]), sb("k_end", [P, 2, NS]), sb("k_end_turned", [P, NSEQ, 2, P])
        v_tok, att, kv_tok = sb("v_tokens", [P, 4, P]), sb("att", [P, 4, NS]), sb("kv_tokens", [P, 2, P])
        sq, gate, o_out = sb("o_squared", [P, 4, NS]), sb("gate", [P, 4, NS]), sb("o_out", [P, 4, NS])
        qw, p = sb("q_window", [P, NSEQ, 2, 4, SLEN]), sb("probs", [P, 2, WIN + NS])
        pt_cache, pt_new = sb("probs_cache_turned", [P, 2, P]), sb("probs_new_turned", [P, 2, P])
        m, row, den, sink_e = (sb(x, [P, 2]) for x in ("minus_max", "row_sum", "denominator", "sink_exp"))
        o_win = sb("o_window", [P, 4, NSEQ, SLEN])
        bank = pg.bank
        zeroed = (qz, qez, kdz, v_tok, att, kv_tok, qw, pt_new)

        def chunks(ap):
            return ap.rearrange("p (c t) -> p c t", t=SLEN)

        def pair(ap):
            return ap.rearrange("p (t c) -> p t c", t=2)

        tokens = slice(SEQ, T)
        loads = [(gla[:], z[0:13, :, tokens].rearrange("t p c -> p t c")),
                 (swa[:], z[13:19, :, tokens].rearrange("t p c -> p t c")),
                 (ident[:], dram["ident"]), (w_up[:], dram["w_gate_up"].rearrange("r (t c) -> r t c", t=2)),
                 (b_up[:], dram["b_gate"]), (g_norm[:], dram["gla_norm"]), (keep[:], dram["sample_keep"]),
                 (causal[:], dram["sample_causal"]), (own_rows[:], dram["sample_rows"]), (bias[:], dram["sample_bias"]),
                 (minus_sink[:], dram["sample_sinks"])]
        k_load = (k_cache[:], dram["k_cacheT"])
        late_loads = [(v_cache[:], dram["v_cache"].rearrange("s k c -> k s c"))]
        late_loads += [(state_in[:, t], dram["state_gla"][:, 2 * t:2 * t + 2].rearrange("s h d v -> (h d) s v")) for t in range(2)]

        @block.sync
        def _(sp):
            for tile, src in loads:
                sp.dma_start(tile, src).then_inc(S["smp_in"].sem, 16)
            sp.dma_start(*k_load).then_inc(S["k_cache_in"].sem, 16)
            for tile, src in late_loads:
                sp.dma_start(tile, src).then_inc(S["smp_late_in"].sem, 16)
            load_branches(pg, sp, o_raw, 0)
            load_branches(pg, sp, o_raw, 1)
            out = [(dram["swa_k_sample"][:, 0:WIN - SLEN], dram["k_cache"][:, SLEN:]),
                   (dram["swa_v_sample"][:, 0:WIN - SLEN], dram["v_cache"][:, SLEN:]),
                   (dram["swa_k_promptT"], z[Z_KB, :, SEQ - WIN:SEQ]), (dram["swa_v_promptT"], z[Z_VB, :, SEQ - WIN:SEQ])]
            for dst, src in out:
                sp.dma_start(dst, src).then_inc(S["smp_out"].sem, 16)
            sp.wait_ge(S["kv_tok_ready"].sem, S["kv_tok_ready"].count(1))
            for i, name in enumerate(("swa_k_sample", "swa_v_sample")):
                sp.dma_start(dram[name][:, WIN - SLEN:], kv_tok[0:NS, i]).then_inc(S["smp_out"].sem, 16)
            sp.wait_ge(S["state_out_ready"].sem, S["state_out_ready"].count(1))
            for t in range(2):
                sp.dma_start(dram["gla_state_sample"][:, 2 * t:2 * t + 2].rearrange("s h d v -> (h d) s v"), state_out[:, t]
                             ).then_inc(S["smp_out"].sem, 16)
            sp.wait_ge(S["o_win_ready"].sem, S["o_win_ready"].count(1))
            sp.dma_start(o_all[4:8, :, tokens].rearrange("t p c -> p t c"), o_win[:].rearrange("p t s c -> p t (s c)")
                         ).then_inc(S["smp_out"].sem, 16)
            sp.wait_ge(S["o_out_ready"].sem, S["o_out_ready"].count(1))
            sp.dma_start(o_all[0:4, :, tokens].rearrange("t p c -> p t c"), o_out[:]).then_inc(S["smp_out"].sem, 16)
            sp.wait_ge(S["smp_out"].sem, S["smp_out"].count(16 * (len(out) + 2 + 4)))

        @block.gpsimd
        def _(pool):
            for tile in zeroed:
                nc.gpsimd.memset(tile[:], 0.0).then_inc(S["smp_set"].sem, 1)
            nc.gpsimd.memset(ones[:], 1.0).then_inc(S["smp_set"].sem, 1)
            nc.gpsimd.memset(eps[:], EPS).then_inc(S["smp_set"].sem, 1)

        @block.scalar
        def _(act):
            copy = lambda out, in_: nc.scalar.activation(out, in_, ACT.Copy)
            act.wait_ge(S["smp_in"].sem, S["smp_in"].count(16 * len(loads)))
            act.wait_ge(S["smp_set"].sem, S["smp_set"].count(len(zeroed) + 2))
            act.wait_ge(S["logits_full"].sem, S["logits_full"].count(1))
            for t in range(2):
                last = nc.scalar.activation(a1[:, t * NS:(t + 1) * NS], bank[5][:, t * NS:(t + 1) * NS], ACT.Abs, bias=b_up[:, t:t + 1])
            last.then_inc(S["abs_ready"].sem, 1)
            act.wait_ge(S["abs_ready"].sem, S["abs_ready"].count(1))
            nc.scalar.activation(a1[:], a1[:], ACT.Exp, scale=-1.0).then_inc(S["abs_exp"].sem, 1)
            act.wait_ge(S["abs_exp"].sem, S["abs_exp"].count(1))
            nc.scalar.activation(a1[:], a1[:], ACT.Ln, bias=1.0).then_inc(S["softplus_ready"].sem, 1)
            act.wait_ge(S["v_turned"].sem, S["v_turned"].count(1))
            copy(v_tok[0:NS].rearrange("p h c -> p (h c)"), bank[6][0:NS]).then_inc(S["v_ready"].sem, 1)
            copy(kv_tok[0:NS].rearrange("p h c -> p (h c)"), bank[7][0:NS, 0:2 * P]).then_inc(S["kv_tok_ready"].sem, 1)
            act.wait_ge(S["centred"].sem, S["centred"].count(1))
            act.wait_ge(S["tail_ready"].sem, S["tail_ready"].count(1))
            nc.scalar.activation(e1[:], a4[:], ACT.Exp, scale=1.0 / TAU).then_inc(S["eq_ready"].sem, 1)
            act.wait_ge(S["eq_ready"].sem, S["eq_ready"].count(1))
            nc.scalar.activation(a4[:], a4[:], ACT.Exp, scale=-1.0 / TAU).then_inc(S["ek_ready"].sem, 1)
            nc.scalar.activation(a1[:], a1[:], ACT.Exp, scale=1.0 / TAU).then_inc(S["eo_ready"].sem, 1)
            nc.scalar.activation(e2[:], a3[:], ACT.Exp, scale=1.0 / TAU).then_inc(S["ei_ready"].sem, 1)
            act.wait_ge(S["m0_ready"].sem, S["m0_ready"].count(1))
            for g in range(2):
                last = nc.scalar.activation(p[:, g], p[:, g], ACT.Exp, bias=m[:, g:g + 1], accum_out=row[:, g:g + 1])
            last.then_inc(S["exp0_ready"].sem, 1)
            act.wait_ge(S["sink0_ready"].sem, S["sink0_ready"].count(1))
            nc.scalar.activation(sink_e[:], sink_e[:], ACT.Exp).then_inc(S["sinkexp0_ready"].sem, 1)
            act.wait_ge(S["o_full"].sem, S["o_full"].count(1))
            flat = sq[:].rearrange("p h c -> p (h c)")
            nc.scalar.activation(flat, bank[5][:, 0:4 * NS], ACT.Square).then_inc(S["o_squared"].sem, 1)
            nc.scalar.activation(gate[:], gla[:, 8:12], ACT.Exp, scale=-1.0).then_inc(S["gate_exp"].sem, 1)
            act.wait_ge(S["sums_full"].sem, S["sums_full"].count(1))
            nc.scalar.activation(flat, bank[4][:, 0:4 * NS], ACT.Ln, scale=1.0 / DV, bias=eps[:]).then_inc(S["log_ms"].sem, 1)
            act.wait_ge(S["log_ms"].sem, S["log_ms"].count(1))
            nc.scalar.activation(flat, flat, ACT.Exp, scale=-0.5).then_inc(S["rstd_ready"].sem, 1)
            act.wait_ge(S["ow0_full"].sem, S["ow0_full"].count(1))
            for kv in range(2):
                rows = slice(kv * HALF, (kv + 1) * HALF)
                for t in range(4):
                    src = bank[7][rows, 256:512].rearrange("p (s k t c) -> p k t s c", s=NSEQ, k=2, t=4)[:, kv, t]
                    last = copy(o_win[rows, t], src)
            last.then_inc(S["o_win_ready"].sem, 1)

        @block.vector
        def _(dve):
            v = nc.vector
            dve.wait_ge(S["smp_in"].sem, S["smp_in"].count(16 * len(loads)))
            dve.wait_ge(S["smp_set"].sem, S["smp_set"].count(len(zeroed) + 2))
            v.tensor_scalar(minus_sink[:], minus_sink[:], -1.0, None, ALU.mult).then_inc(S["sink_negated"].sem, 1)
            for kv in range(2):
                rows = slice(kv * HALF, (kv + 1) * HALF)
                for t in range(4):
                    last = v.tensor_scalar(qw[rows, :, kv, t], swa[rows, t].rearrange("p (s c) -> p s c", c=SLEN), HD ** -0.5, None, ALU.mult)
            last.then_inc(S["qw_ready"].sem, 1)
            dve.wait_ge(S["abs_ready"].sem, S["abs_ready"].count(1))
            for t in range(2):
                last = v.tensor_scalar(a2[:, t * NS:(t + 1) * NS], bank[5][:, t * NS:(t + 1) * NS], b_up[:, t:t + 1], 0.0, ALU.add, ALU.min)
            last.then_inc(S["lm_ready"].sem, 1)
            dve.wait_ge(S["softplus_ready"].sem, S["softplus_ready"].count(1))
            dve.wait_ge(S["lm_ready"].sem, S["lm_ready"].count(1))
            v.tensor_tensor(a2[:], a2[:], a1[:], ALU.subtract).then_inc(S["log_a_ready"].sem, 1)
            dve.wait_ge(S["log_a_ready"].sem, S["log_a_ready"].count(1))
            v.tensor_tensor_scan(a3[:], keep[:], a2[:], 0.0, ALU.mult, ALU.add).then_inc(S["b_ready"].sem, 1)
            dve.wait_ge(S["b_ready"].sem, S["b_ready"].count(1))
            b = chunks(a3[:])
            n = L2 // SLEN
            v.tensor_tensor(chunks(a4[:]), b, b[:, :, SLEN // 2 - 1:SLEN // 2].to_broadcast([P, n, SLEN]), ALU.subtract).then_inc(S["shifted"].sem, 1)
            v.tensor_tensor(chunks(a1[:]), b[:, :, SLEN - 1:].to_broadcast([P, n, SLEN]), b, ALU.subtract).then_inc(S["tail_ready"].sem, 1)
            dve.wait_ge(S["shifted"].sem, S["shifted"].count(1))
            v.tensor_scalar(a4[:], a4[:], 80.0 * TAU, -80.0 * TAU, ALU.min, ALU.max).then_inc(S["centred"].sem, 1)
            dve.wait_ge(S["ei_ready"].sem, S["ei_ready"].count(1))
            v.tensor_tensor(kt[:], gla[:, 2:4], pair(a4[:]), ALU.mult).then_inc(S["kt_ready"].sem, 1)
            v.tensor_tensor(kd[:], gla[:, 2:4], pair(a1[:]), ALU.mult).then_inc(S["kd_ready"].sem, 1)
            for out, e, name in ((qz, e1, "qz_ready"), (qez, e2, "qez_ready")):
                for hh in range(2):
                    rows = slice(hh * HALF, (hh + 1) * HALF)
                    last = v.scalar_tensor_tensor(out[rows, :, hh], gla[rows, 0:2], DK ** -0.5, pair(e[rows]), ALU.mult, ALU.mult)
                last.then_inc(S[name].sem, 1)
            dve.wait_ge(S["scores0_full"].sem, S["scores0_full"].count(1))
            for g in range(2):
                last = v.tensor_tensor(p[:, g], bank[g][:, 0:WIN + NS], bias[:, g], ALU.add)
            last.then_inc(S["s0_ready"].sem, 1)
            dve.wait_ge(S["s0_ready"].sem, S["s0_ready"].count(1))
            v.tensor_reduce(m[:], p[:], AX.X, ALU.max, negate=True).then_inc(S["max0_ready"].sem, 1)
            dve.wait_ge(S["max0_ready"].sem, S["max0_ready"].count(1))
            dve.wait_ge(S["sink_negated"].sem, S["sink_negated"].count(1))
            v.tensor_scalar(m[:], m[:], minus_sink[:, 0:1], None, ALU.min).then_inc(S["m0_ready"].sem, 1)
            dve.wait_ge(S["m0_ready"].sem, S["m0_ready"].count(1))
            v.tensor_scalar(sink_e[:], m[:], minus_sink[:, 0:1], None, ALU.subtract).then_inc(S["sink0_ready"].sem, 1)
            dve.wait_ge(S["att_full"].sem, S["att_full"].count(1))
            for hh in range(4):
                last = v.copy_predicated(att[0:NS, hh], causal[:].bitcast(I32), bank[4][0:NS, hh * NS:(hh + 1) * NS])
            last.then_inc(S["att_ready"].sem, 1)
            dve.wait_ge(S["kd_turned"].sem, S["kd_turned"].count(1))
            for s in range(NSEQ):
                last = v.tensor_scalar(kdz[0:NS, s].rearrange("p t c -> p (t c)"), bank[6][0:NS, 0:2 * P], own_rows[:, s:s + 1], None, ALU.mult)
            last.then_inc(S["kd_ready_turned"].sem, 1)
            dve.wait_ge(S["exp0_ready"].sem, S["exp0_ready"].count(1))
            dve.wait_ge(S["sinkexp0_ready"].sem, S["sinkexp0_ready"].count(1))
            v.tensor_tensor(den[:], row[:], sink_e[:], ALU.add).then_inc(S["den0_ready"].sem, 1)
            dve.wait_ge(S["den0_ready"].sem, S["den0_ready"].count(1))
            v.reciprocal(den[:], den[:]).then_inc(S["inv0_ready"].sem, 1)
            dve.wait_ge(S["inv0_ready"].sem, S["inv0_ready"].count(1))
            for g in range(2):
                last = v.tensor_scalar(p[:, g], p[:, g], den[:, g:g + 1], None, ALU.mult)
            last.then_inc(S["p0_ready"].sem, 1)
            dve.wait_ge(S["pt0_full"].sem, S["pt0_full"].count(1))
            v.tensor_copy(pt_cache[:].rearrange("p g c -> p (g c)"), bank[7][:, 0:2 * P]).then_inc(S["pt0_read_a"].sem, 1)
            v.tensor_copy(pt_new[0:NS].rearrange("p g c -> p (g c)"), bank[7][0:NS, 2 * P:]).then_inc(S["pt0_read_b"].sem, 1)
            dve.wait_ge(S["smp_late_in"].sem, S["smp_late_in"].count(16 * len(late_loads)))
            dve.wait_ge(S["u_full"].sem, S["u_full"].count(1))
            for s in range(NSEQ):
                for t in range(2):
                    at = t * NS + s * SLEN + SLEN - 1
                    last = v.scalar_tensor_tensor(state_out[:, t, s], state_in[:, t, s], e2[:, at:at + 1],
                                                  bank[s // 2][:, (s % 2) * 2 * P + t * P:(s % 2) * 2 * P + (t + 1) * P], ALU.mult, ALU.add)
            last.then_inc(S["state_out_ready"].sem, 1)
            dve.wait_ge(S["gate_exp"].sem, S["gate_exp"].count(1))
            v.tensor_scalar(gate[:], gate[:], 1.0, None, ALU.add).then_inc(S["gate_den"].sem, 1)
            dve.wait_ge(S["gate_den"].sem, S["gate_den"].count(1))
            v.reciprocal(gate[:], gate[:]).then_inc(S["sigmoid_ready"].sem, 1)
            dve.wait_ge(S["sigmoid_ready"].sem, S["sigmoid_ready"].count(1))
            v.tensor_tensor(gate[:], gate[:], gla[:, 8:12], ALU.mult).then_inc(S["silu_ready"].sem, 1)
            dve.wait_ge(S["rstd_ready"].sem, S["rstd_ready"].count(1))
            v.scalar_tensor_tensor(o_out[:].rearrange("p h c -> p (h c)"), bank[5][:, 0:4 * NS], g_norm[:, 0:1],
                                   sq[:].rearrange("p h c -> p (h c)"), ALU.mult, ALU.mult).then_inc(S["o_normed"].sem, 1)
            dve.wait_ge(S["o_normed"].sem, S["o_normed"].count(1))
            dve.wait_ge(S["silu_ready"].sem, S["silu_ready"].count(1))
            v.tensor_tensor(o_out[:], o_out[:], gate[:], ALU.mult).then_inc(S["o_out_ready"].sem, 1)

        @block.tensor
        def _(pe):
            mm = nc.tensor.matmul
            pe.wait_ge(S["smp_in"].sem, S["smp_in"].count(16 * len(loads)))
            pe.wait_ge(S["smp_set"].sem, S["smp_set"].count(len(zeroed) + 2))
            for t in range(2):
                last = mm(bank[5][:, t * NS:(t + 1) * NS], w_up[:, t], gla[:, 12], start=True, stop=True)
            last.then_inc(S["logits_full"].sem, 1)
            for hh in range(4):
                nc.tensor.transpose(bank[6][0:NS, hh * P:(hh + 1) * P], gla[:, 4 + hh], ident[:])
            for i in range(2):
                last = nc.tensor.transpose(bank[7][0:NS, i * P:(i + 1) * P], swa[:, 4 + i], ident[:])
            last.then_inc(S["v_turned"].sem, 1)
            pe.wait_ge(S["k_cache_in"].sem, S["k_cache_in"].count(16))
            pe.wait_ge(S["qw_ready"].sem, S["qw_ready"].count(1))
            for s in range(NSEQ):
                q = qw[:, s].rearrange("p k t c -> p (k t c)")
                rows = slice(32 * (s % 4), 32 * (s % 4) + 32)
                mm(bank[s // 4][rows, 0:WIN], q, k_cache[:, s], start=True, stop=True, tile_position=(0, 32 * (s % 4)))
                last = mm(bank[s // 4][rows, WIN:WIN + NS], q, swa[:, 4], start=True, stop=True, tile_position=(0, 32 * (s % 4)))
            last.then_inc(S["scores0_full"].sem, 1)
            pe.wait_ge(S["qez_ready"].sem, S["qez_ready"].count(1))
            for t in range(2):
                last = mm(bank[4][0:NS, t * 2 * NS:(t + 1) * 2 * NS], kt[:, t], qz[:, t].rearrange("p h c -> p (h c)"), start=True, stop=True)
            last.then_inc(S["att_full"].sem, 1)
            pe.wait_ge(S["v_ready"].sem, S["v_ready"].count(1))
            for t in range(2):
                last = nc.tensor.transpose(bank[6][0:NS, t * P:(t + 1) * P], kd[:, t], ident[:])
            last.then_inc(S["kd_turned"].sem, 1)
            pe.wait_ge(S["att_ready"].sem, S["att_ready"].count(1))
            pe.wait_ge(S["lm_ready"].sem, S["lm_ready"].count(1))
            for hh in range(4):
                mm(bank[5][:, hh * NS:(hh + 1) * NS], v_tok[:, hh], att[:, hh], start=(hh == 0), stop=False, skip_group_check=True)
            pe.wait_ge(S["smp_late_in"].sem, S["smp_late_in"].count(16 * len(late_loads)))
            out = bank[5][:, 0:4 * NS].rearrange("p (t h c) -> p t h c", t=2, h=2)
            for s in range(NSEQ):
                for t in range(2):
                    cols = slice(s * SLEN, (s + 1) * SLEN)
                    last = mm(out[:, t, :, cols], state_in[:, t, s], qez[:, t, :, cols], start=False,
                              stop=(s == NSEQ - 1 and t == 1), skip_group_check=True)
            last.then_inc(S["o_full"].sem, 1)
            pe.wait_ge(S["kd_ready_turned"].sem, S["kd_ready_turned"].count(1))
            pe.wait_ge(S["s0_ready"].sem, S["s0_ready"].count(1))
            for s in range(NSEQ):
                for t in range(2):
                    for hh in range(2):
                        rows = slice(hh * HALF, (hh + 1) * HALF)
                        at = (s % 2) * 2 * P + t * P
                        last = mm(bank[s // 2][rows, at:at + P], kdz[:, s, t, rows], v_tok[:, 2 * t + hh], start=True, stop=True)
            last.then_inc(S["u_full"].sem, 1)
            pe.wait_ge(S["o_squared"].sem, S["o_squared"].count(1))
            mm(bank[4][:, 0:4 * NS], ones[:], sq[:].rearrange("p h c -> p (h c)"), start=True, stop=True).then_inc(S["sums_full"].sem, 1)
            pe.wait_ge(S["p0_ready"].sem, S["p0_ready"].count(1))
            pe.wait_ge(S["kv_tok_ready"].sem, S["kv_tok_ready"].count(1))
            for g in range(2):
                nc.tensor.transpose(bank[7][:, g * P:(g + 1) * P], p[:, g, 0:WIN], ident[:])
                last = nc.tensor.transpose(bank[7][0:NS, (2 + g) * P:(3 + g) * P], p[:, g, WIN:], ident[:])
            last.then_inc(S["pt0_full"].sem, 1)
            pe.wait_ge(S["pt0_read_a"].sem, S["pt0_read_a"].count(1))
            pe.wait_ge(S["pt0_read_b"].sem, S["pt0_read_b"].count(1))
            for s in range(NSEQ):
                cols = slice(32 * (s % 4), 32 * (s % 4) + 32)
                o = bank[7][:, 256 + 32 * s:256 + 32 * (s + 1)]
                mm(o, v_cache[:, s], pt_cache[:, s // 4, cols], start=True, stop=False)
                last = mm(o, kv_tok[:, 1], pt_new[:, s // 4, cols], start=False, stop=True)
            last.then_inc(S["ow0_full"].sem, 1)

        S["sums_full"].passed(1)


def merge_phase(pg, ws, o_raw):
    nc, dram = pg.nc, pg.dram
    S = pg
    z, merged = dram["z"], dram["merged"]
    NT = D // P
    with ExitStack() as own, nc.Block() as block:
        def sb(name, shape, dt=F32):
            return own.enter_context(nc.sbuf_tensor(f"{name}_mrg", shape, dt))
        ws.tiles(dram["w_branch"], NT, dram["w_out"])
        o_hi, o_lo = sb("o_hi", [P, 8, T], F32R), sb("o_lo", [P, 8, T], F32R)
        gates = [sb(f"gates{i}", [P, 2, TB]) for i in range(2)]
        part = [sb(f"part{i}", [P, 2, TB]) for i in range(2)]
        out = [sb(f"merged{i}", [P, TB]) for i in range(2)]
        o_in = [S["o_in_even"], S["o_in_odd"]]
        gates_in, stored = [S["gates_in_even"], S["gates_in_odd"]], [S["merged_stored_even"], S["merged_stored_odd"]]

        def tokens(b):
            return slice(b * TB, (b + 1) * TB)

        def before(pair, slot, b):
            return pair * NB + (slot * NB + b) // 2

        @block.sync
        def _(sp):
            def store(n, slot, b):
                sp.wait_ge(S["merged_ready"].sem, S["merged_ready"].count(n * NB + (b - 1)))
                n, b = (n, b - 2) if b >= 2 else (n - 1, b + NB - 2)
                sp.dma_start(merged[one(n), :, tokens(b)].rearrange("o p t -> (o p) t"), out[slot][:]).then_inc(stored[slot].sem, 16)

            def body(n, pair, slot):
                for b in range(NB):
                    s = (slot + b) % 2
                    if isinstance(n, int) and n == 0 and b + 2 < NB:
                        sp.wait_ge(S["o_lo_ready"].sem, S["o_lo_ready"].count(2 * (b + 1)))
                        load_branches(pg, sp, o_raw, b + 2)
                    if (due := S["parts_ready"].count(n * NB + (b - 1))) is not None:
                        sp.wait_ge(S["parts_ready"].sem, due)
                    for i, tile in enumerate((Z_GATE_A, Z_GATE_B)):
                        sp.dma_start(gates[s][:, i], z[one(n + tile), :, tokens(b)].rearrange("o p t -> (o p) t")
                                     ).then_inc(gates_in[s].sem, 16)
                    if not isinstance(n, int) or n * NB + b >= 2:
                        store(n, s, b)
                    if b == 1:
                        ws.load(sp, n + 2, pair + 1, slot)
            each_pair_ahead(sp, NT, body)
            for b in (NB - 2, NB - 1):
                sp.wait_ge(S["merged_ready"].sem, S["merged_ready"].count((NT - 1) * NB + (b + 1)))
                slot = (1 + b) % 2
                sp.dma_start(merged[NT - 1, :, tokens(b)], out[slot][:]).then_inc(stored[slot].sem, 16)
            for slot in range(2):
                sp.wait_ge(stored[slot].sem, stored[slot].count(NT * NB // 2 * 16))

        @block.scalar
        def _(act):
            def high(b):
                act.wait_ge(o_in[b % 2].sem, o_in[b % 2].count(16 * (b // 2 + 1)))
                for half in range(2):
                    k = slice(4 * half, 4 * half + 4)
                    nc.scalar.activation(o_hi[:, k, tokens(b)], o_raw[b % 2][:, k], ACT.Copy).then_inc(S["o_hi_ready"].sem, 1)

            def body(n, pair, slot):
                for b in range(NB):
                    s = (slot + b) % 2
                    if isinstance(n, int) and n == 0 and b + 1 < NB:
                        high(b + 1)
                    act.wait_ge(gates_in[s].sem, gates_in[s].count((before(pair, slot, b) + 1) * 32))
                    nc.scalar.activation(gates[s][:], gates[s][:], ACT.Sigmoid).then_inc(S["gates_ready"].sem, 1)
                ws.split_hi(act, n + 2, pair + 1, slot)
            high(0)
            each_pair_ahead(act, NT, body)

        @block.vector
        def _(dve):
            v = nc.vector

            def low(b):
                for half in range(2):
                    dve.wait_ge(S["o_hi_ready"].sem, S["o_hi_ready"].count(2 * b + (half + 1)))
                    k = slice(4 * half, 4 * half + 4)
                    v.tensor_tensor(o_lo[:, k, tokens(b)], o_raw[b % 2][:, k], o_hi[:, k, tokens(b)].bitcast(F32), ALU.subtract
                                    ).then_inc(S["o_lo_ready"].sem, 1)

            def body(n, pair, slot):
                for b in range(NB):
                    s = (slot + b) % 2
                    if isinstance(n, int) and n == 0 and b + 1 < NB:
                        low(b + 1)
                    dve.wait_ge(S["psum_full"].sem, S["psum_full"].count(n * NB + (b + 1)))
                    dve.wait_ge(S["gates_ready"].sem, S["gates_ready"].count(n * NB + (b + 1)))
                    if (due := S["merged_ready"].count(n * NB + (b - 1))) is not None:
                        dve.wait_ge(S["merged_ready"].sem, due)
                    for i in range(2):
                        last = v.tensor_tensor(part[s][:, i], gates[s][:, i], pg.bank[2 * s + i][:, :TB], ALU.mult)
                    last.then_inc(S["parts_ready"].sem, 1)
                ws.split_lo(dve, n + 2, pair + 1, slot)
            low(0)
            each_pair_ahead(dve, NT, body)

        @block.gpsimd
        def _(pool):
            def body(n, pair, slot):
                for b in range(NB):
                    s = (slot + b) % 2
                    if (due := stored[s].count(before(pair, slot, b) * 16)) is not None:
                        pool.wait_ge(stored[s].sem, due)
                    pool.wait_ge(S["parts_ready"].sem, S["parts_ready"].count(n * NB + (b + 1)))
                    nc.gpsimd.tensor_tensor(out[s][:], part[s][:, 0], part[s][:, 1], ALU.add).then_inc(S["merged_ready"].sem, 1)
            for n in range(2):
                body(n, 0, n)
            later_pairs(pool, NT, body)

        @block.tensor
        def _(pe):
            def body(n, pair, slot):
                pe.wait_ge(ws.hi_ready.sem, ws.hi_ready.count(n + 1))
                pe.wait_ge(ws.lo_ready.sem, ws.lo_ready.count(n + 1))
                for b in range(NB):
                    if isinstance(n, int) and n == 0:
                        pe.wait_ge(S["o_lo_ready"].sem, S["o_lo_ready"].count(2 * (b + 1)))
                    if (due := S["parts_ready"].count(n * NB + (b - 1))) is not None:
                        pe.wait_ge(S["parts_ready"].sem, due)
                    for i in range(2):
                        for k in range(4):
                            kk = 4 * i + k
                            last = pg.split_matmul(pg.bank[2 * ((slot + b) % 2) + i][:, :TB], ws.hi[slot][:, kk], ws.lo[slot][:, kk],
                                                   o_hi[:, kk, tokens(b)], o_lo[:, kk, tokens(b)], k == 0, k == 3)
                    last.then_inc(S["psum_full"].sem, 1)
            for n in range(2):
                body(n, 0, n)
            later_pairs(pe, NT, body)

        ws.passed(NT)
        S["psum_full"].passed(NT * NB)


def each_last(engine, n, body):
    body(0, n == 1)
    if n > 2:
        with engine.Fori(1, n - 1) as i:
            body(i, False)
    if n > 1:
        body(n - 1, True)


def project_out_phase(pg, ws, tag, src, weights, nk, norm_w, residual, dst, following=None, ahead=None):
    nc, dram = pg.nc, pg.dram
    S = pg
    NT = D // P
    KK = nk // 2
    U = 2 * KK
    BANKS = ((1, 2, 3, 0), (4, 5, 6, 0))
    SUMS = pg.bank[7]
    NORM_AT = 1
    with ExitStack() as own, nc.Block() as block:
        def sb(name, shape, dt=F32):
            return own.enter_context(nc.sbuf_tensor(f"{name}_{tag}", shape, dt))
        kept_w = {un: sb(f"w_kept{un}", [P, 8, P]) for un in range(2, U, 2)}
        raw = [sb(f"src_raw{i}", [P, 2, TB]) for i in range(2)]
        s_hi, s_lo = sb("src_hi", [P, nk, TB], F32R), sb("src_lo", [P, nk, TB], F32R)
        y, x = sb("y", [P, NT, TB]), sb("x", [P, NT, TB])
        yn = sb("y_normed", [P, NT, TB])
        sq = [sb(f"sq{i}", [P, TB]) for i in range(2)]
        acc, rstd = sb("acc", [P, TB]), sb("rstd", [P, TB])
        w, ones, eps = sb("norm_w", [P, NT]), sb("ones", [P, P]), sb("eps", [P, 1])
        src_in = [S["src_in_even"], S["src_in_odd"]]
        src_loads = [(KK + 1) // 2, KK // 2]

        def tokens(b):
            return slice(b * TB, (b + 1) * TB) if isinstance(b, int) else bass.ds(b * TB, TB)

        def first(b):
            return isinstance(b, int) and b == 0

        def raw_w(un):
            return kept_w[un] if un in kept_w else ws.raw[un % 2]

        @block.sync
        def _(sp):
            sp.dma_start(w[:], norm_w).then_inc(S["const_in"].sem, 16)

            def load_src(b, kk):
                before = b * KK + (kk - 1) if kk >= 2 else b * KK - (KK - 1 - max(k for k in range(KK) if k % 2 == kk))
                if (due := S["src_lo_ready"].count(before)) is not None:
                    sp.wait_ge(S["src_lo_ready"].sem, due)
                sp.dma_start(raw[kk % 2][:], src[2 * kk:2 * kk + 2, :, tokens(b)].rearrange("t p c -> p t c")
                             ).then_inc(src_in[kk % 2].sem, 16)

            def load_w(b, un, src_w):
                if un not in kept_w or first(b):
                    if (due := ws.lo_ready.count(b * U + (un - 1))) is not None:
                        sp.wait_ge(ws.lo_ready.sem, due)
                    sp.dma_start(raw_w(un)[:], src_w).then_inc(ws.w_in[un % 2].sem, 16)

            def load_residual(b):
                if (due := S["y_stored"].count(b * 32)) is not None:
                    sp.wait_ge(S["y_stored"].sem, due)
                sp.dma_start(x[:], residual[:, :, tokens(b)].rearrange("k p t -> p k t")).then_inc(S["residual_in"].sem, 16)

            def store(b, half):
                sp.wait_ge(S["y_added"].sem, S["y_added"].count(b * 2 + (half + 1)))
                columns = slice(4 * half, 4 * half + 4)
                sp.dma_start(dst[columns, :, tokens(b)].rearrange("k p t -> p k t"), x[:, columns]).then_inc(S["y_stored"].sem, 16)

            def body(b, tail):
                for un in range(U):
                    if tail and un == KK and ahead is not None:
                        sp.wait_ge(S["y_stored"].sem, S["y_stored"].count(2 * 32))
                        ahead.sync(sp, 0)
                    if first(b) and un + 2 < KK:
                        load_src(0, un + 2)
                    if un + 2 < U:
                        load_w(b, un + 2, weights[un + 2])
                    elif not tail:
                        load_w(b + 1, un + 2 - U, weights[un + 2 - U])
                    elif following is not None:
                        load_w(b + 1, un + 2 - U, following[un + 2 - U])
                    if un >= KK and not tail:
                        load_src(b + 1, un - KK)
                    if un == NORM_AT + 5 and not first(b):
                        for half in range(2):
                            store(b - 1, half)
                    if un == U - 1:
                        load_residual(b)
            for kk in range(2):
                load_src(0, kk)
            each_last(sp, NB, body)
            if ahead is not None:
                ahead.sync(sp, 1)
            for half in range(2):
                store(NB - 1, half)
            sp.wait_ge(S["y_stored"].sem, S["y_stored"].count(NB * 32))

        @block.scalar
        def _(act):
            def copy(out, in_):
                return nc.scalar.activation(out, in_, ACT.Copy)

            def split_w(b, un):
                if un % 2:
                    act.wait_ge(ws.w_in[1].sem, ws.w_in[1].count((b * KK + (un // 2 + 1)) * 16))
                elif first(b):
                    act.wait_ge(ws.w_in[0].sem, ws.w_in[0].count((un // 2 + 1) * 16))
                elif un == 0:
                    act.wait_ge(ws.w_in[0].sem, ws.w_in[0].count((b + KK) * 16))
                copy(ws.hi[un % 2][:], raw_w(un)[:]).then_inc(ws.hi_ready.sem, 1)

            def split_src(b, kk):
                act.wait_ge(src_in[kk % 2].sem, src_in[kk % 2].count((b * src_loads[kk % 2] + (kk // 2 + 1)) * 16))
                copy(s_hi[:, 2 * kk:2 * kk + 2], raw[kk % 2][:]).then_inc(S["src_hi_ready"].sem, 1)

            def evacuate(b, half, columns):
                for j in columns:
                    n = 4 * half + j
                    if j < 3:
                        act.wait_ge(S["column_full"].sem, S["column_full"].count(b * 6 + (half * 3 + j + 1)))
                    if not first(b):
                        act.wait_ge(S["y_normed"].sem, S["y_normed"].count(b * NT + (n + 1 - NT)))
                    if (due := S["squares_added"].count(b * NT + (n - 1))) is not None:
                        act.wait_ge(S["squares_added"].sem, due)
                    bank = pg.bank[BANKS[half][j]]
                    copy(y[:, n], bank[:, :TB])
                    nc.scalar.activation(sq[n % 2][:], bank[:, :TB], ACT.Square).then_inc(S["column_read"].sem, 1)

            def root(b):
                act.wait_ge(S["sums_full"].sem, S["sums_full"].count(b + 1))
                nc.scalar.activation(rstd[:], SUMS[:, :TB], ACT.Sqrt, bias=eps[:], scale=1.0 / D).then_inc(S["y_rooted"].sem, 1)

            def body(b, tail):
                for un in range(U):
                    if un == NORM_AT and not first(b):
                        root(b - 1)
                    if first(b) and un + 2 < KK:
                        split_src(0, un + 2)
                    if un in (KK - 1, U - 1):
                        evacuate(b, un // KK, range(3))
                    act.wait_ge(S["unit_done"].sem, S["unit_done"].count(b * U + (un + 1)))
                    if un in (KK - 1, U - 1):
                        evacuate(b, un // KK, (3,))
                    if un + 2 < U:
                        split_w(b, un + 2)
                    elif not tail or following is not None:
                        split_w(b + 1, un + 2 - U)
                    if un >= KK and not tail:
                        split_src(b + 1, un - KK)
            act.wait_ge(S["const_set"].sem, S["const_set"].count(2))
            for kk in range(2):
                split_src(0, kk)
            each_last(act, NB, body)
            root(NB - 1)
            if ahead is not None:
                ahead.square(act, 0)
                ahead.root(act, 0)

        @block.vector
        def _(dve):
            v = nc.vector

            def split_w(b, un):
                dve.wait_ge(ws.hi_ready.sem, ws.hi_ready.count(b * U + (un + 1)))
                v.tensor_tensor(ws.lo[un % 2][:], raw_w(un)[:], ws.hi[un % 2][:].bitcast(F32), ALU.subtract).then_inc(ws.lo_ready.sem, 1)

            def split_src(b, kk):
                dve.wait_ge(S["src_hi_ready"].sem, S["src_hi_ready"].count(b * KK + (kk + 1)))
                pair = slice(2 * kk, 2 * kk + 2)
                v.tensor_tensor(s_lo[:, pair], raw[kk % 2][:], s_hi[:, pair].bitcast(F32), ALU.subtract).then_inc(S["src_lo_ready"].sem, 1)

            def invert(b):
                dve.wait_ge(S["y_rooted"].sem, S["y_rooted"].count(b + 1))
                v.reciprocal(rstd[:], rstd[:]).then_inc(S["y_inverted"].sem, 1)

            def norm(b, half):
                dve.wait_ge(S["y_inverted"].sem, S["y_inverted"].count(b + 1))
                for n in range(4 * half, 4 * half + 4):
                    v.scalar_tensor_tensor(yn[:, n], y[:, n], w[:, n:n + 1], rstd[:], ALU.mult, ALU.mult).then_inc(S["y_normed"].sem, 1)

            def add(b, half):
                dve.wait_ge(S["residual_in"].sem, S["residual_in"].count((b + 1) * 16))
                dve.wait_ge(S["y_normed"].sem, S["y_normed"].count(b * NT + 4 * (half + 1)))
                columns = slice(4 * half, 4 * half + 4)
                v.tensor_tensor(x[:, columns], x[:, columns], yn[:, columns], ALU.add).then_inc(S["y_added"].sem, 1)

            norm_steps = (invert, lambda b: norm(b, 0), lambda b: norm(b, 1), lambda b: add(b, 0), lambda b: add(b, 1))

            def body(b, tail):
                for un in range(U):
                    if 0 <= un - NORM_AT < 5 and not first(b):
                        norm_steps[un - NORM_AT](b - 1)
                    if first(b) and un + 2 < KK:
                        split_src(0, un + 2)
                    if un + 2 < U:
                        split_w(b, un + 2)
                    elif not tail or following is not None:
                        split_w(b + 1, un + 2 - U)
                    if un >= KK and not tail:
                        split_src(b + 1, un - KK)
            if ahead is not None:
                ahead.constants(dve)
            v.memset(ones[:], 1.0).then_inc(S["const_set"].sem, 1)
            v.memset(eps[:], EPS).then_inc(S["const_set"].sem, 1)
            dve.wait_ge(S["const_in"].sem, S["const_in"].count(16))
            for kk in range(2):
                split_src(0, kk)
            each_last(dve, NB, body)
            invert(NB - 1)
            for half in range(2):
                norm(NB - 1, half)
                add(NB - 1, half)

        @block.gpsimd
        def _(pool):
            g = nc.gpsimd

            def body(b):
                for n in range(NT):
                    pool.wait_ge(S["column_read"].sem, S["column_read"].count(b * NT + (n + 1)))
                    if n == 1:
                        if (due := S["sums_full"].count(b)) is not None:
                            pool.wait_ge(S["sums_full"].sem, due)
                        g.tensor_tensor(acc[:], sq[0][:], sq[1][:], ALU.add).then_inc(S["squares_added"].sem, 2)
                    elif n > 1:
                        if (due := S["squares_added"].count(b * NT + n)) is not None:
                            pool.wait_ge(S["squares_added"].sem, due)
                        g.tensor_tensor(acc[:], acc[:], sq[n % 2][:], ALU.add).then_inc(S["squares_added"].sem, 1)

            each(pool, NB, body)
            if ahead is not None:
                ahead.add(pool, 0)

        @block.tensor
        def _(pe):
            def sums(b):
                pe.wait_ge(S["squares_added"].sem, S["squares_added"].count((b + 1) * NT))
                if (due := S["y_rooted"].count(b)) is not None:
                    pe.wait_ge(S["y_rooted"].sem, due)
                nc.tensor.matmul(SUMS[:, :TB], ones[:], acc[:], start=True, stop=True).then_inc(S["sums_full"].sem, 1)

            def body(b):
                for half in range(2):
                    for kk in range(KK):
                        un = half * KK + kk
                        if un == NORM_AT and not first(b):
                            sums(b - 1)
                        pe.wait_ge(ws.hi_ready.sem, ws.hi_ready.count(b * U + (un + 1)))
                        pe.wait_ge(ws.lo_ready.sem, ws.lo_ready.count(b * U + (un + 1)))
                        if half == 0:
                            pe.wait_ge(S["src_lo_ready"].sem, S["src_lo_ready"].count(b * KK + (kk + 1)))
                        for j in range(4):
                            if kk == 0:
                                n = 4 * half + j
                                if (due := S["column_read"].count(b * NT + (n - 7 if j < 3 else (0, 4)[half]))) is not None:
                                    pe.wait_ge(S["column_read"].sem, due)
                            bank = pg.bank[BANKS[half][j]][:, :TB]
                            for k in range(2):
                                at = k * 4 + j
                                last = pg.split_matmul(bank, ws.hi[un % 2][:, at], ws.lo[un % 2][:, at], s_hi[:, 2 * kk + k], s_lo[:, 2 * kk + k],
                                                       kk == 0 and k == 0, kk == KK - 1 and k == 1)
                            if kk == KK - 1 and j < 3:
                                last.then_inc(S["column_full"].sem, 1)
                        last.then_inc(S["unit_done"].sem, 1)
            pe.wait_ge(S["const_set"].sem, S["const_set"].count(2))
            each(pe, NB, body)
            sums(NB - 1)
            if ahead is not None:
                pe.wait_ge(S["y_rooted"].sem, S["y_rooted"].count(NB))
                ahead.sum_rows(pe, 0)

        ws.w_in[0].passed((KK + NB - 1) * 16)
        ws.w_in[1].passed(NB * KK * 16)
        ws.hi_ready.passed(NB * U)
        ws.lo_ready.passed(NB * U)
        S["unit_done"].passed(NB * U)
        for i in range(2):
            src_in[i].passed(NB * src_loads[i] * 16)
        for name, n in (("src_hi_ready", NB * KK), ("src_lo_ready", NB * KK), ("column_full", NB * 6), ("column_read", NB * NT),
                        ("squares_added", NB * NT), ("y_normed", NB * NT), ("y_added", NB * 2), ("y_rooted", NB), ("y_inverted", NB),
                        ("sums_full", NB), ("y_stored", NB * 32), ("residual_in", NB * 16), ("const_in", 16), ("const_set", 2)):
            S[name].passed(n)


def ffn_in_phase(pg, ws, norm):
    nc, dram = pg.nc, pg.dram
    S = pg
    LU = 2 + SEQ + NSEQ * (2 + SLEN)
    LC = LU - 2
    LAST = (NB - 1) * TB
    TAIL = SEQ - LAST
    U_BANKS, G_BANK0 = 2, 2
    with ExitStack() as own, nc.Block() as block:
        def sb(name, shape, dt=F32):
            return own.enter_context(nc.sbuf_tensor(f"{name}_ffn", shape, dt))
        h_hi, h_lo = sb("h_hi", [P, KD, T], F32R), sb("h_lo", [P, KD, T], F32R)
        ws.tiles(dram["w_ffn_in"], 2 * KF, dram["w_ffn_out"])
        norm.h_hi, norm.h_lo = h_hi, h_lo
        up = norm.x[1][:].rearrange("p k t -> p (k t)")[:, 0:LU]
        conv = norm.x[0][:].rearrange("p k t -> p (k t)")[:, 0:LC]
        FIRST = (((0, 0), (1, 0)), ((0, 1), (1, 1)), ((1, 2),), ((1, 3), (0, 2)), ((0, 3), (0, 4), (1, 4)))
        first_order = [product for products in FIRST for product in products]
        U_READY = [first_order.index((0, b)) + 1 for b in range(NB)]
        weights_used = [max(first_order.index((tile, b)) for b in range(NB)) + 1 for tile in range(2)]
        smp = sb("act_sample", [P, NS])
        taps, states, kept = sb("taps", [P, KF, 4]), sb("states", [P, KF, NSEQ, 2]), sb("kept", [P, KF, 2 + 2 * NSEQ])
        stored = S["act_stored"]

        def sample_cols(ap, start, n, at):
            return ap[:, start:start + NSEQ * (2 + SLEN)].rearrange("p (s c) -> p s c", s=NSEQ)[:, :, at:at + n]

        def read_u(act, j, b, products):
            act.wait_ge(S["psum_full"].sem, S["psum_full"].count(products))
            src = pg.bank[b % U_BANKS]
            if b < NB - 1:
                nc.scalar.activation(up[:, 2 + b * TB:2 + (b + 1) * TB], src[:, :TB], ACT.Copy).then_inc(S["u_read"].sem, 1)
            else:
                smp_u = src[:, TAIL:TB].rearrange("p (s c) -> p s c", s=NSEQ)
                nc.scalar.activation(up[:, 2 + LAST:2 + SEQ], src[:, :TAIL], ACT.Copy)
                nc.scalar.activation(sample_cols(up, 2 + SEQ, SLEN, 2), smp_u, ACT.Copy)
                k = kept[:, one(j)].rearrange("p o c -> p (o c)")
                nc.scalar.activation(k[:, 0:2], src[:, TAIL - 2:TAIL], ACT.Copy)
                nc.scalar.activation(k[:, 2:].rearrange("p (s c) -> p s c", s=NSEQ), smp_u[:, :, SLEN - 2:], ACT.Copy
                                     ).then_inc(S["u_read"].sem, 1)

        @block.sync
        def _(sp):
            sp.dma_start(taps[:], dram["conv_taps"]).then_inc(S["ffn_const_in"].sem, 16)
            sp.dma_start(states[:], dram["conv_states"]).then_inc(S["ffn_const_in"].sem, 16)
            for b in range(2, NB):
                norm.sync(sp, b)

            def body(n, j, slot):
                ws.load(sp, n + 2, j + 1, slot)
                if slot == 1:
                    sp.wait_ge(S["g_read"].sem, S["g_read"].count((j + 1) * NB))
                    a = dram["act"][one(j)].rearrange("o p t -> (o p) t")
                    sp.dma_start(a[:, 0:SEQ], conv[:, 0:SEQ]).then_inc(stored.sem, 16)
                    sp.dma_start(a[:, SEQ:T], smp[:]).then_inc(stored.sem, 16)
            each_pair_ahead(sp, 2 * KF, body)
            sp.wait_ge(S["u_read"].sem, S["u_read"].count(KF * NB))
            sp.dma_start(dram["conv_kept"], kept[:]).then_inc(S["kept_stored"].sem, 16)
            sp.wait_ge(S["kept_stored"].sem, S["kept_stored"].count(16))
            sp.wait_ge(stored.sem, stored.count(KF * 32))

        @block.scalar
        def _(act):
            for b in range(NB):
                if b + 1 < NB:
                    norm.square(act, b + 1)
                norm.high(act, b)
                if b + 1 < NB:
                    norm.root(act, b + 1)
                if b == 3:
                    norm.used(act, 4)
                    for block_u in range(2):
                        read_u(act, 0, block_u, U_READY[block_u])
            for block_u in range(2, NB):
                read_u(act, 0, block_u, U_READY[block_u])
            ws.split_hi(act, 2, 1, 0, used=weights_used[0])

            def body(n, j, slot):
                if slot == 0:
                    act.wait_ge(S["conv_done"].sem, S["conv_done"].count(j))
                    for b in range(NB):
                        read_u(act, j, b, n * NB + (b + 1))
                else:
                    act.wait_ge(S["conv_done"].sem, S["conv_done"].count(j + 1))
                    nc.scalar.activation(conv[:, 0:SEQ], conv[:, 0:SEQ], ACT.Gelu_apprx_tanh)
                    if (due := stored.count(j * 32)) is not None:
                        act.wait_ge(stored.sem, due)
                    nc.scalar.activation(smp[:].rearrange("p (s c) -> p s c", s=NSEQ), sample_cols(conv, SEQ, SLEN, 2),
                                         ACT.Gelu_apprx_tanh).then_inc(S["gelu_done"].sem, 1)
                ws.split_hi(act, n + 2, j + 1, slot)
            body(1, 0, 1)
            later_pairs_ahead(act, 2 * KF, body)

        @block.vector
        def _(dve):
            v = nc.vector
            norm.vector(dve)
            dve.wait_ge(S["ffn_const_in"].sem, S["ffn_const_in"].count(32))

            def body(n, j, slot):
                if slot == 0:
                    tap = lambda i: taps[:, one(j), i:i + 1].rearrange("p o c -> p (o c)")
                    dve.wait_ge(S["u_read"].sem, S["u_read"].count((j + 1) * NB))
                    dve.wait_ge(S["heads_set"].sem, S["heads_set"].count(j + 1))
                    if (due := stored.count(j * 32)) is not None:
                        dve.wait_ge(stored.sem, due)
                    v.tensor_scalar(conv, up[:, 2:], tap(2), tap(3), ALU.mult, ALU.add).then_inc(S["tap2_done"].sem, 1)
                    dve.wait_ge(S["tap2_done"].sem, S["tap2_done"].count(j + 1))
                    v.scalar_tensor_tensor(conv, up[:, 1:LU - 1], tap(1), conv, ALU.mult, ALU.add).then_inc(S["tap1_done"].sem, 1)
                    dve.wait_ge(S["tap1_done"].sem, S["tap1_done"].count(j + 1))
                    v.scalar_tensor_tensor(conv, up[:, 0:LU - 2], tap(0), conv, ALU.mult, ALU.add).then_inc(S["conv_done"].sem, 1)
                else:
                    dve.wait_ge(S["gelu_done"].sem, S["gelu_done"].count(j + 1))
                    for b in range(NB):
                        dve.wait_ge(S["psum_full"].sem, S["psum_full"].count(n * NB + (b + 1)))
                        g = pg.bank[G_BANK0 + b]
                        cols = slice(b * TB, min((b + 1) * TB, SEQ))
                        last = v.tensor_tensor(conv[:, cols], conv[:, cols], g[:, :cols.stop - cols.start], ALU.mult)
                        if b == NB - 1:
                            last = v.tensor_tensor(smp[:], smp[:], g[:, TAIL:TB], ALU.mult)
                        last.then_inc(S["g_read"].sem, 1)
                ws.split_lo(dve, n + 2, j + 1, slot)
            each_pair_ahead(dve, 2 * KF, body)

        @block.gpsimd
        def _(pool):
            for b in range(NB):
                if b + 1 < NB:
                    norm.add(pool, b + 1)
                norm.low_last(pool, b)
            pool.wait_ge(S["ffn_const_in"].sem, S["ffn_const_in"].count(32))
            norm.used(pool, 4)
            nc.gpsimd.memset(up[:, 0:2], 0.0).then_inc(S["u_front_zeroed"].sem, 1)
            pool.wait_ge(S["u_front_zeroed"].sem, S["u_front_zeroed"].count(1))

            def body(j):
                if (due := S["conv_done"].count(j)) is not None:
                    pool.wait_ge(S["conv_done"].sem, due)
                pool.wait_ge(S["u_front_zeroed"].sem, S["u_front_zeroed"].count(1))
                nc.gpsimd.tensor_copy(sample_cols(up, 2 + SEQ, 2, 0), states[:, one(j)].rearrange("p o s c -> p (o s) c")
                                      ).then_inc(S["heads_set"].sem, 1)
            each(pool, KF, body)

        @block.tensor
        def _(pe):
            for n in range(2):
                pe.wait_ge(ws.hi_ready.sem, ws.hi_ready.count(n + 1))
                pe.wait_ge(ws.lo_ready.sem, ws.lo_ready.count(n + 1))
            for b in range(NB):
                if b + 1 < NB:
                    norm.sum_rows(pe, b + 1)
                norm.ready(pe, b)
                for tile, block_h in FIRST[b]:
                    if tile == 0 and (due := S["u_read"].count(block_h - 1)) is not None:
                        pe.wait_ge(S["u_read"].sem, due)
                    bank = pg.bank[G_BANK0 + block_h if tile else block_h % U_BANKS]
                    project_block(pg, ws, h_hi, h_lo, bank, tile, tile, block_h)

            def body(n, j, slot):
                pe.wait_ge(ws.hi_ready.sem, ws.hi_ready.count(n + 1))
                pe.wait_ge(ws.lo_ready.sem, ws.lo_ready.count(n + 1))
                for b in range(NB):
                    if slot == 0:
                        pe.wait_ge(S["u_read"].sem, S["u_read"].count(j * NB + (b - 1)))
                        bank = pg.bank[b % U_BANKS]
                    else:
                        pe.wait_ge(S["g_read"].sem, S["g_read"].count((j - 1) * NB + (b + 1)))
                        bank = pg.bank[G_BANK0 + b]
                    project_block(pg, ws, h_hi, h_lo, bank, n, slot, b)
            later_pairs(pe, 2 * KF, body)

        norm.done()
        ws.passed(2 * KF)


def build(nc, dram):
    with ExitStack() as ctx:
        pg = Program(nc, ctx, dram)
        ws = WeightStream(pg, lambda name, shape, dt: ctx.enter_context(nc.sbuf_tensor(f"{name}_sb", shape, dt)))
        mixer_phases(pg, ws)
        with ExitStack() as branches:
            o_raw = [branches.enter_context(nc.sbuf_tensor(f"o_raw{i}", [P, 8, TB], F32)) for i in range(2)]
            sample_phase(pg, o_raw)
            merge_phase(pg, ws, o_raw)
        with ExitStack() as ffn:
            norm = norm_blocks(pg, lambda name, shape, dt: ffn.enter_context(nc.sbuf_tensor(name, shape, dt)),
                               dram["x1"].rearrange("k p t -> (k p) t"), dram["norm_ffn_pre"], "ffn")
            project_out_phase(pg, ws, "mix", dram["merged"], dram["w_out"], KD, dram["norm_mix_post"],
                              dram["xT"].rearrange("(k p) t -> k p t", p=P), dram["x1"], dram["w_ffn_in"], norm)
            ffn_in_phase(pg, ws, norm)
        project_out_phase(pg, ws, "out", dram["act"], dram["w_ffn_out"], KF, dram["norm_ffn_post"], dram["x1"], dram["yT"])


def tiles(w, columns):
    w = w[:, columns].reshape(w.shape[0] // P, P, len(columns) // P, P)
    return np.ascontiguousarray(w.transpose(2, 1, 0, 3))


def by_partition(v):
    return np.ascontiguousarray(v.reshape(-1, P).T)


def units(w):
    w = w.reshape(w.shape[0] // (2 * P), 2, P, 2, 4, P)
    return np.ascontiguousarray(w.transpose(3, 0, 2, 1, 4, 5)).reshape(-1, P, 8, P)


def sample_bias(slopes):
    s4, kv, t, tok, g, key = np.meshgrid(*[np.arange(n) for n in (4, KVH, 4, SLEN, 2, WIN + NS)], indexing="ij")
    new = key - WIN
    rel = np.where(key < WIN, tok + WIN - key, tok - new % SLEN)
    seen = (rel >= 0) & (rel < WIN) & ((key < WIN) | (new // SLEN == 4 * g + s4))
    return np.where(seen, -slopes[kv * 4 + t] * rel, NEG).astype(np.float32).reshape(P, 2, WIN + NS)


def host_arrays(a):
    w_in = a["w_in"][0]
    edges = np.cumsum([0, 256, 256, 512, RANK, 512, 512, 128, 128, D, D])
    qa, ka, va, r, ga, qb, kb, vb, gate_a, gate_b = (np.arange(x, y) for x, y in zip(edges[:-1], edges[1:]))
    head_rows = np.concatenate([np.r_[t * HD:(t + 1) * HD, (t + 4) * HD:(t + 5) * HD] for t in range(4)])
    columns = np.concatenate([qa, ka, va, ga, np.full(P, edges[-1]), qb[head_rows], kb, vb, gate_a, gate_b])
    columns[12 * P:12 * P + RANK] = r
    w_in = np.concatenate([w_in, np.zeros((D, 1), w_in.dtype)], axis=1)
    x = np.concatenate([a["x_prompt"][0], a["x_sample"].reshape(NS, D)], axis=0)
    w_up = np.zeros((P, H * DK), np.float32)
    w_up[:RANK] = a["w_gate_up"][0]
    head = np.arange(4)[:, None] + 4 * np.arange(2)[None, :]
    q, key = np.arange(WIN)[:, None] + WIN, np.arange(2 * WIN)[None, :]
    rel = np.where((q >= key) & (q - key < WIN), key - q, NEG).astype(np.float32)
    t = np.arange(P)
    out = {
        "xT": np.ascontiguousarray(x.T),
        "w_in": tiles(w_in, columns),
        "norm_mix_pre": by_partition(a["norm_mix_pre"]),
        "w_gate_up": w_up, "b_gate": by_partition(a["b_gate"]), "gla_norm": by_partition(a["gla_norm"]),
        "sinks": np.ascontiguousarray(np.broadcast_to(a["sinks"][0][head], (P, 4, 2))),
        "ident": np.eye(P, dtype=np.float32),
        "rel": rel, "rel_first": np.where(key < WIN, NEG, rel).astype(np.float32),
        "scan_keep": np.ascontiguousarray(np.broadcast_to((np.arange(2 * P) % CH != 0).astype(np.float32), (P, 2 * P))),
        "causal": ((t[:, None] // CH == t[None] // CH) & (t[:, None] <= t[None])).astype(np.float32),
    }
    s = np.arange(NS)
    w_ffn_in = a["w_ffn_in"][0]
    ffn_columns = np.concatenate([np.arange(j * P, (j + 1) * P) + half * FF for j in range(KF) for half in range(2)])
    taps = np.concatenate([a["conv_w"][0], a["conv_b"]], axis=0)
    caches = {n: a[f"cache_swa_{n}"][0].reshape(NSEQ, WIN, P) for n in ("k", "v")}
    out.update({
        "k_cache": np.ascontiguousarray(caches["k"]), "v_cache": np.ascontiguousarray(caches["v"]),
        "k_cacheT": np.ascontiguousarray(caches["k"].transpose(2, 0, 1)),
        "state_gla": np.ascontiguousarray(a["state_gla"][0]),
        "sample_keep": np.ascontiguousarray(np.broadcast_to((np.arange(2 * NS) % SLEN != 0).astype(np.float32), (P, 2 * NS))),
        "sample_causal": ((s[:, None] // SLEN == s[None] // SLEN) & (s[:, None] <= s[None])).astype(np.float32),
        "sample_rows": (s[:, None] // SLEN == np.arange(NSEQ)[None]).astype(np.float32),
        "sample_bias": sample_bias(np.array([slope(n) for n in range(QH)])),
        "sample_sinks": np.ascontiguousarray(np.tile(np.repeat(a["sinks"][0], SLEN), 4)[:, None]),
        "w_branch": np.concatenate([tiles(a["w_branch_a"][0], np.arange(D)),
                                    tiles(a["w_branch_b"][0][head_rows], np.arange(D))], axis=2),
        "w_out": units(a["w_out"][0]), "w_ffn_out": units(a["w_ffn_out"][0]),
        "w_ffn_in": tiles(w_ffn_in, ffn_columns),
        "norm_mix_post": by_partition(a["norm_mix_post"]), "norm_ffn_pre": by_partition(a["norm_ffn_pre"]),
        "norm_ffn_post": by_partition(a["norm_ffn_post"]),
        "conv_taps": np.ascontiguousarray(taps.reshape(4, KF, P).transpose(2, 1, 0)),
        "conv_states": np.ascontiguousarray(a["state_ffn_conv"][0].reshape(NSEQ, 2, KF, P).transpose(3, 2, 0, 1)),
    })
    return out


SCRATCH = {"z": (N_Z, P, T), "o": (8, P, T), "merged": (KD, P, T), "x1": (KD, P, T), "act": (KF, P, T)}
OUTPUTS = {"gla_state_prompt": (H, DK, DV), "yT": (KD, P, T), "gla_state_sample": (NSEQ, H, DK, DV),
           "swa_k_promptT": (P, WIN), "swa_v_promptT": (P, WIN),
           "swa_k_sample": (NSEQ, WIN, P), "swa_v_sample": (NSEQ, WIN, P), "conv_kept": (P, KF, 2 + 2 * NSEQ)}


def kernel(**inputs):
    import concourse.bacc as bacc
    from concourse.bass_utils import run_bass_kernel_spmd

    arrays = host_arrays({name: np.asarray(value) for name, value in inputs.items()})
    nc = bacc.Bacc("TRN2", target_bir_lowering=False, num_devices=1)
    dram = {name: nc.dram_tensor(name, a.shape, F32, kind="ExternalInput").ap() for name, a in arrays.items()}
    for name, shape in SCRATCH.items():
        dram[name] = nc.dram_tensor(name, shape, F32, kind="Internal").ap()
    for name, shape in OUTPUTS.items():
        dram[name] = nc.dram_tensor(name, shape, F32, kind="ExternalOutput").ap()
    build(nc, dram)
    out = run_bass_kernel_spmd(nc, [arrays], core_ids=[0]).results[0]

    y = np.asarray(out["yT"]).reshape(D, T).T
    kept = np.asarray(out["conv_kept"]).transpose(2, 1, 0).reshape(1 + NSEQ, 2, FF)
    windows = [np.ascontiguousarray(np.asarray(out[f"swa_{n}_promptT"]).T).reshape(1, 1, WIN, KVH, HD) for n in "kv"]
    caches = [np.asarray(out[f"swa_{n}_sample"]).reshape(1, NSEQ, WIN, KVH, HD) for n in "kv"]
    return (np.ascontiguousarray(y[:SEQ])[None], np.ascontiguousarray(y[SEQ:]).reshape(NSEQ, SLEN, D),
            np.asarray(out["gla_state_prompt"]).reshape(1, 1, H, DK, DV),
            np.asarray(out["gla_state_sample"]).reshape(1, NSEQ, H, DK, DV),
            *windows, *caches, kept[None, :1], kept[None, 1:])
```
